# Optimizing a Trainium2 kernel written in Bass

```python
import math
import jax, jax.numpy as jnp
from jax import lax
import numpy as np

D_MODEL = 1024
BATCH = 1
SEQ = 256
DEPTH = 2

GRID_W = 64
CTX_LEN = 256
N_EVEN = (DEPTH + 1) // 2
N_ODD = DEPTH // 2

NA_HEADS = 8
NA_HEAD_DIM = 64
NA_W = NA_HEADS * NA_HEAD_DIM
NA_WIN_R = 8
NA_WIN_C = 16
NA_ROW_BLOCK = 2
RW_HEADS = 8
RW_HEAD_DIM = 64
RW_W = RW_HEADS * RW_HEAD_DIM
RW_DECAY_LORA = 64
RW_AAA_LORA = 64
RW_GATE_LORA = 128
RW_IN = 3 * RW_W + RW_DECAY_LORA + RW_AAA_LORA + RW_GATE_LORA
RW_SPLITS = (RW_W, 2 * RW_W, 3 * RW_W, 3 * RW_W + RW_DECAY_LORA, 3 * RW_W + RW_DECAY_LORA + RW_AAA_LORA)
RW_GN_EPS = 64e-5
SHIFT_WIDTH = 3
EVEN_IN = 3 * NA_W + RW_IN
EVEN_OUT = NA_W + RW_W
DA_HEADS = 8
DA_HEAD_DIM = 64
DA_QK = DA_HEADS * 2 * DA_HEAD_DIM
DA_V = DA_HEADS * 2 * DA_HEAD_DIM
ODD_IN = 2 * DA_QK + DA_V
Q_BLOCK = 128
ROPE_THETA = 10000.0
N_EXPERTS = 16
N_GROUPS = 4
EXP_PER_GROUP = N_EXPERTS // N_GROUPS
TOP_K = 2
D_EXPERT = 512
ALPHA = (2 * DEPTH) ** 0.25
BETA = (8 * DEPTH) ** -0.25
LN_EPS = 1e-5
F32 = jnp.float32

kernel_name = "hybrid_na_rwkv7_diffattn_grouped_moe_dit"

def _layer_norm(x, g, b):
    xf = x.astype(F32)
    mu = xf.mean(-1, keepdims=True)
    var = jnp.square(xf - mu).mean(-1, keepdims=True)
    return ((xf - mu) * lax.rsqrt(var + LN_EPS) * g + b).astype(x.dtype)

def _ada(cvec, w, b):
    return jnp.split(jax.nn.silu(cvec) @ w + b, 6, axis=-1)

def _modulate(h, shift, scale):
    return h * (1.0 + scale[:, None, :]) + shift[:, None, :]

def _axial_rope(z, pos_r, pos_c):
    half = z.shape[-1] // 2
    nf = half // 2
    inv = ROPE_THETA ** (-jnp.arange(nf, dtype=F32) / nf)

    def rot(za, pos):
        ang = pos.astype(F32)[:, None] * inv
        cos = jnp.cos(ang)[None, :, None, :]
        sin = jnp.sin(ang)[None, :, None, :]
        z1, z2 = za[..., :nf].astype(F32), za[..., nf:].astype(F32)
        return jnp.concatenate([z1 * cos - z2 * sin, z1 * sin + z2 * cos], -1)

    return jnp.concatenate([rot(z[..., :half], pos_r), rot(z[..., half:], pos_c)], -1).astype(z.dtype)

def _short_conv(z, w):
    pad = SHIFT_WIDTH // 2
    n = z.shape[1]
    zp = jnp.pad(z, ((0, 0), (pad, pad), (0, 0)))
    return sum(zp[:, j:j + n] * w[j] for j in range(SHIFT_WIDTH))

def _context_attention(q, k, v):
    B, L, H, Dh = q.shape
    s = jnp.einsum('bqhd,bkhd->bhqk', q, k).astype(F32) * Dh ** -0.5
    p = jax.nn.softmax(s, -1).astype(v.dtype)
    return jnp.einsum('bhqk,bkhd->bqhd', p, v).reshape(B, L, H * Dh)

def _na_attention(q, k, v, kc, vc, rpb):
    B, T, H, Dh = q.shape
    rows = T // GRID_W
    wr = min(NA_WIN_R, rows)
    r = np.arange(rows)
    row_idx = np.clip(r - wr // 2, 0, rows - wr)[:, None] + np.arange(wr)[None]
    c = np.arange(GRID_W)
    col_idx = np.clip(c - NA_WIN_C // 2, 0, GRID_W - NA_WIN_C)[:, None] + np.arange(NA_WIN_C)[None]
    d_row = row_idx - r[:, None] + (NA_WIN_R - 1)
    d_col = jnp.asarray(col_idx - c[:, None] + (NA_WIN_C - 1), jnp.int32)
    col_idx = jnp.asarray(col_idx, jnp.int32)
    n_blk = rows // NA_ROW_BLOCK
    row_idx_b = jnp.asarray(row_idx.reshape(n_blk, NA_ROW_BLOCK, wr), jnp.int32)
    d_row_b = jnp.asarray(d_row.reshape(n_blk, NA_ROW_BLOCK, wr), jnp.int32)
    qg = (q * Dh ** -0.5).reshape(B, rows, GRID_W, H, Dh)
    kg = k.reshape(B, rows, GRID_W, H, Dh)
    vg = v.reshape(B, rows, GRID_W, H, Dh)
    q_b = jnp.moveaxis(qg.reshape(B, n_blk, NA_ROW_BLOCK, GRID_W, H, Dh), 1, 0)
    n_loc = wr * NA_WIN_C

    def block(args):
        qb, ridx, dri = args
        kw = kg[:, ridx][:, :, :, col_idx]
        vw = vg[:, ridx][:, :, :, col_idx]
        bias = rpb[:, dri[:, :, None, None], d_col[None, None]]
        s_loc = jnp.einsum('bqchd,bqrcjhd->bhqcrj', qb, kw).astype(F32) + jnp.swapaxes(bias, 2, 3).astype(F32)
        s_ctx = jnp.einsum('bqchd,blhd->bhqcl', qb, kc).astype(F32)
        s = jnp.concatenate([s_loc.reshape(B, H, NA_ROW_BLOCK, GRID_W, n_loc), s_ctx], -1)
        p = jax.nn.softmax(s, -1).astype(v.dtype)
        p_loc = p[..., :n_loc].reshape(B, H, NA_ROW_BLOCK, GRID_W, wr, NA_WIN_C)
        return (jnp.einsum('bhqcrj,bqrcjhd->bqchd', p_loc, vw)
                + jnp.einsum('bhqcl,blhd->bqchd', p[..., n_loc:], vc))

    o = lax.map(block, (q_b, row_idx_b, d_row_b))
    return jnp.moveaxis(o, 0, 1).reshape(B, T, H * Dh)

def _rw_heads(z):
    return z.reshape(*z.shape[:-1], RW_HEADS, RW_HEAD_DIM)

def _rw_direction(p, w0, w_up, a0, a_up, k_k, k_a, r_k):
    r, k, v, xw, xa, _ = jnp.split(p.astype(F32), RW_SPLITS, axis=-1)
    decay = jnp.exp(-jnp.exp(-jax.nn.softplus(-(w0 + jnp.tanh(xw) @ w_up)) - 0.5))
    a = jax.nn.sigmoid(a0 + xa @ a_up)
    kk = _rw_heads(k * k_k)
    kk = kk / jnp.maximum(jnp.sqrt(jnp.sum(kk * kk, -1, keepdims=True)), 1e-12)
    k_eff = _rw_heads(k * (1.0 + (a - 1.0) * k_a))
    r, v, a = _rw_heads(r), _rw_heads(v), _rw_heads(a)
    bonus = jnp.sum(r * k_eff * r_k, -1, keepdims=True) * v
    return (r, _rw_heads(decay), k_eff, v, -kk, kk * a), bonus

def _rw_step(S, inp):
    r_t, w_t, k_t, v_t, a_t, b_t = inp
    sa = jnp.einsum('bhij,bhj->bhi', S, a_t)
    S = S * w_t[:, :, None, :] + sa[..., None] * b_t[:, :, None, :] + v_t[..., None] * k_t[:, :, None, :]
    return S, jnp.einsum('bhij,bhj->bhi', S, r_t)

def _rw_scan(S0, seq_inputs, reverse):
    xs = tuple(jnp.moveaxis(z, 1, 0) for z in seq_inputs)
    S, ys = lax.scan(_rw_step, S0, xs, reverse=reverse)
    return S, jnp.moveaxis(ys, 0, 1)

def _rwkv7_bidir(p_lat, p_ctx, w0, w_up, a0, a_up, g_up, k_k, k_a, r_k, gn_g, gn_b):
    B = p_lat.shape[0]
    S0 = jnp.zeros((B, RW_HEADS, RW_HEAD_DIM, RW_HEAD_DIM), F32)
    ys_lat, ys_ctx, bon_lat, bon_ctx = [], [], [], []
    for d, reverse in enumerate((False, True)):
        in_ctx, b_ctx = _rw_direction(p_ctx, w0[d], w_up[d], a0[d], a_up[d], k_k, k_a, r_k)
        in_lat, b_lat = _rw_direction(p_lat, w0[d], w_up[d], a0[d], a_up[d], k_k, k_a, r_k)
        S_ctx, y_c = _rw_scan(S0, in_ctx, reverse)
        _, y_l = _rw_scan(S_ctx, in_lat, reverse)
        ys_ctx.append(y_c); ys_lat.append(y_l); bon_ctx.append(b_ctx); bon_lat.append(b_lat)

    def finish(y, bonus, p):
        g = jax.nn.sigmoid(p[..., RW_SPLITS[-1]:].astype(F32)) @ g_up
        mu = y.mean(-1, keepdims=True)
        var = jnp.square(y - mu).mean(-1, keepdims=True)
        yn = ((y - mu) * lax.rsqrt(var + RW_GN_EPS)).reshape(*y.shape[:-2], RW_W) * gn_g + gn_b
        return ((yn + bonus.reshape(*bonus.shape[:-2], RW_W)) * g).astype(p.dtype)

    return (finish(ys_lat[0] + ys_lat[1], bon_lat[0] + bon_lat[1], p_lat),
            finish(ys_ctx[0] + ys_ctx[1], bon_ctx[0] + bon_ctx[1], p_ctx))

def _even_mixer(u_lat, u_ctx, w_in, w_out, conv_w, rpb, w0, w_up, a0, a_up, g_up, k_k, k_a, r_k, gn_g, gn_b):
    B, T, _ = u_lat.shape
    L = u_ctx.shape[1]
    p_lat = u_lat @ w_in
    p_ctx = u_ctx @ w_in

    def na_qkv(p, n):
        q, k, v = jnp.split(p[..., :3 * NA_W], 3, axis=-1)
        sh = (B, n, NA_HEADS, NA_HEAD_DIM)
        return q.reshape(sh), k.reshape(sh), v.reshape(sh)

    q, k, v = na_qkv(p_lat, T)
    qc, kc, vc = na_qkv(p_ctx, L)
    o_na_lat = _na_attention(q, k, v, kc, vc, rpb)
    o_na_ctx = _context_attention(qc, kc, vc)
    o_rw_lat, o_rw_ctx = _rwkv7_bidir(_short_conv(p_lat[..., 3 * NA_W:], conv_w),
                                      _short_conv(p_ctx[..., 3 * NA_W:], conv_w),
                                      w0, w_up, a0, a_up, g_up, k_k, k_a, r_k, gn_g, gn_b)
    y_lat = jnp.concatenate([o_na_lat, o_rw_lat], -1) @ w_out
    y_ctx = jnp.concatenate([o_na_ctx, o_rw_ctx], -1) @ w_out
    return y_lat, y_ctx

def _diff_mix(q, k, v, lam):
    s = jnp.einsum('bqhmd,bkhmd->bhmqk', q, k).astype(F32) * DA_HEAD_DIM ** -0.5
    p = jax.nn.softmax(s, -1)
    a = p[:, :, 0] - lam * p[:, :, 1]
    return jnp.einsum('bhqk,bkhe->bqhe', a.astype(v.dtype), v)

def _diff_attention_blocks(q, k, v, lam):
    B, T = q.shape[:2]
    nb = T // Q_BLOCK
    qb = jnp.moveaxis(q.reshape(B, nb, Q_BLOCK, *q.shape[2:]), 1, 0)
    o = lax.map(lambda blk: _diff_mix(blk, k, v, lam), qb)
    return jnp.moveaxis(o, 0, 1).reshape(B, T, *o.shape[3:])

def _odd_mixer(u_lat, u_ctx, w_in, w_out, lq1, lk1, lq2, lk2, subln_g, lambda_init, pos_r, pos_c, with_ctx_out):
    B, T, _ = u_lat.shape
    L = u_ctx.shape[1]
    lam = (jnp.exp(jnp.sum(lq1.astype(F32) * lk1.astype(F32)))
           - jnp.exp(jnp.sum(lq2.astype(F32) * lk2.astype(F32))) + lambda_init)

    def qkv(u, n):
        p = u @ w_in
        q = p[..., :DA_QK].reshape(B, n, DA_HEADS, 2, DA_HEAD_DIM)
        k = p[..., DA_QK:2 * DA_QK].reshape(B, n, DA_HEADS, 2, DA_HEAD_DIM)
        v = p[..., 2 * DA_QK:].reshape(B, n, DA_HEADS, 2 * DA_HEAD_DIM)
        return q, k, v

    def rot(z):
        return _axial_rope(z.reshape(B, T, 2 * DA_HEADS, DA_HEAD_DIM), pos_r, pos_c).reshape(z.shape)

    def head_norm(o):
        of = o.astype(F32)
        of = of * lax.rsqrt(jnp.mean(of * of, -1, keepdims=True) + 1e-5) * subln_g * (1.0 - lambda_init)
        return of.astype(o.dtype)

    q, k, v = qkv(u_lat, T)
    qc, kc, vc = qkv(u_ctx, L)
    q, k = rot(q), rot(k)
    k_all = jnp.concatenate([k, kc], axis=1)
    v_all = jnp.concatenate([v, vc], axis=1)
    y_lat = head_norm(_diff_attention_blocks(q, k_all, v_all, lam)).reshape(B, T, DA_V) @ w_out
    y_ctx = head_norm(_diff_mix(qc, kc, vc, lam)).reshape(B, L, DA_V) @ w_out if with_ctx_out else None
    return y_lat, y_ctx

def _moe(h, router_w, router_b, w_gate, w_up, w_down):
    s = jax.nn.sigmoid((h @ router_w).astype(F32))
    sel = (s + router_b.astype(F32)).reshape(-1, N_GROUPS, EXP_PER_GROUP)
    grp = jnp.argmax(lax.top_k(sel, TOP_K)[0].sum(-1), axis=-1)
    in_grp = jnp.take_along_axis(sel, grp[:, None, None], axis=1)[:, 0]
    _, idx = lax.top_k(in_grp, TOP_K)
    eid = grp[:, None] * EXP_PER_GROUP + idx
    gate = jnp.take_along_axis(s, eid, axis=-1)
    gate = gate / gate.sum(-1, keepdims=True)
    combine = jnp.einsum('nk,nke->ne', gate, jax.nn.one_hot(eid, N_EXPERTS, dtype=F32)).astype(h.dtype)
    out = jnp.zeros_like(h)
    for e in range(N_EXPERTS):
        he = jax.nn.silu(h @ w_gate[e]) * (h @ w_up[e])
        out = out + combine[:, e:e + 1] * (he @ w_down[e])
    return out

def setup_inputs(seed: int = 0) -> dict:
    key = jax.random.key(seed)
    keys = jax.random.split(key, 40)
    counter = iter(range(40))

    def nk():
        return keys[next(counter)]

    def nrm(shape, std):
        return jax.random.normal(nk(), shape, F32) * std

    D = D_MODEL
    even_scale = np.ones((EVEN_IN,), np.float32)
    even_scale[2 * NA_W:3 * NA_W] = BETA
    even_scale[3 * NA_W + 2 * RW_W:3 * NA_W + 3 * RW_W] = BETA
    odd_scale = np.ones((ODD_IN,), np.float32)
    odd_scale[2 * DA_QK:] = BETA
    return {
        "x": nrm((BATCH, SEQ, D), 1.0),
        "c": nrm((BATCH, D), 1.0),
        "ctx": nrm((BATCH, CTX_LEN, D), 1.0),
        "c_ctx": nrm((D,), 1.0),
        "ada_w": nrm((DEPTH, D, 6 * D), 0.5 * D ** -0.5),
        "ada_b": nrm((DEPTH, 6 * D), 0.02),
        "ln_g": 1.0 + nrm((DEPTH, 2, D), 0.02),
        "ln_b": nrm((DEPTH, 2, D), 0.02),
        "even_w_in": nrm((N_EVEN, D, EVEN_IN), D ** -0.5) * jnp.asarray(even_scale),
        "even_w_out": nrm((N_EVEN, EVEN_OUT, D), BETA * EVEN_OUT ** -0.5),
        "shift_w": jnp.array([0.3, 1.0, 0.3], F32)[None, :, None] + nrm((N_EVEN, SHIFT_WIDTH, RW_IN), 0.1),
        "na_rpb": nrm((N_EVEN, NA_HEADS, 2 * NA_WIN_R - 1, 2 * NA_WIN_C - 1), 0.1),
        "rw_w0": jax.random.uniform(nk(), (N_EVEN, 2, RW_W), F32, minval=-4.0, maxval=1.0),
        "rw_w_up": nrm((N_EVEN, 2, RW_DECAY_LORA, RW_W), 0.1 * RW_DECAY_LORA ** -0.5),
        "rw_a0": nrm((N_EVEN, 2, RW_W), 0.1),
        "rw_a_up": nrm((N_EVEN, 2, RW_AAA_LORA, RW_W), 0.5 * RW_AAA_LORA ** -0.5),
        "rw_g_up": nrm((N_EVEN, RW_GATE_LORA, RW_W), RW_GATE_LORA ** -0.5),
        "rw_k_k": 0.85 + nrm((N_EVEN, RW_W), 0.05),
        "rw_k_a": 1.0 + nrm((N_EVEN, RW_W), 0.05),
        "rw_r_k": nrm((N_EVEN, RW_HEADS, RW_HEAD_DIM), 0.1),
        "rw_gn_g": 1.0 + nrm((N_EVEN, RW_W), 0.02),
        "rw_gn_b": nrm((N_EVEN, RW_W), 0.02),
        "odd_w_in": nrm((N_ODD, D, ODD_IN), D ** -0.5) * jnp.asarray(odd_scale),
        "odd_w_out": nrm((N_ODD, DA_V, D), BETA * DA_V ** -0.5),
        "da_lq1": nrm((N_ODD, DA_HEAD_DIM), 0.1),
        "da_lk1": nrm((N_ODD, DA_HEAD_DIM), 0.1),
        "da_lq2": nrm((N_ODD, DA_HEAD_DIM), 0.1),
        "da_lk2": nrm((N_ODD, DA_HEAD_DIM), 0.1),
        "da_subln_g": 1.0 + nrm((N_ODD, 2 * DA_HEAD_DIM), 0.02),
        "router_w": nrm((D, N_EXPERTS), D ** -0.5),
        "router_b": nrm((N_EXPERTS,), 0.01),
        "exp_w_gate": nrm((DEPTH, N_EXPERTS, D, D_EXPERT), D ** -0.5),
        "exp_w_up": nrm((DEPTH, N_EXPERTS, D, D_EXPERT), D ** -0.5),
        "exp_w_down": nrm((DEPTH, N_EXPERTS, D_EXPERT, D), BETA * D_EXPERT ** -0.5),
    }

def reference(x, c, ctx, c_ctx, ada_w, ada_b, ln_g, ln_b, even_w_in, even_w_out, shift_w, na_rpb,
              rw_w0, rw_w_up, rw_a0, rw_a_up, rw_g_up, rw_k_k, rw_k_a, rw_r_k, rw_gn_g, rw_gn_b,
              odd_w_in, odd_w_out, da_lq1, da_lk1, da_lq2, da_lk2, da_subln_g,
              router_w, router_b, exp_w_gate, exp_w_up, exp_w_down):
    B, T, D = x.shape
    t = jnp.arange(T)
    pos_r, pos_c = t // GRID_W, t % GRID_W
    h_lat, h_ctx = x, ctx
    for l in range(DEPTH):
        last = l == DEPTH - 1
        m_lat = _ada(c, ada_w[l], ada_b[l])
        m_ctx = _ada(c_ctx[None], ada_w[l], ada_b[l])
        u_lat = _modulate(h_lat, m_lat[0], m_lat[1])
        u_ctx = _modulate(h_ctx, m_ctx[0], m_ctx[1])
        if l % 2 == 0:
            i = l // 2
            y_lat, y_ctx = _even_mixer(u_lat, u_ctx, even_w_in[i], even_w_out[i], shift_w[i], na_rpb[i],
                                       rw_w0[i], rw_w_up[i], rw_a0[i], rw_a_up[i], rw_g_up[i],
                                       rw_k_k[i], rw_k_a[i], rw_r_k[i], rw_gn_g[i], rw_gn_b[i])
        else:
            i = l // 2
            lambda_init = 0.8 - 0.6 * math.exp(-0.3 * l)
            y_lat, y_ctx = _odd_mixer(u_lat, u_ctx, odd_w_in[i], odd_w_out[i], da_lq1[i], da_lk1[i],
                                      da_lq2[i], da_lk2[i], da_subln_g[i], lambda_init, pos_r, pos_c,
                                      not last)
        h_lat = _layer_norm(ALPHA * h_lat + m_lat[2][:, None, :] * y_lat, ln_g[l, 0], ln_b[l, 0])
        u_lat = _modulate(h_lat, m_lat[3], m_lat[4])
        if last:
            f_lat = _moe(u_lat.reshape(-1, D), router_w, router_b,
                         exp_w_gate[l], exp_w_up[l], exp_w_down[l]).reshape(B, T, D)
        else:
            h_ctx = _layer_norm(ALPHA * h_ctx + m_ctx[2][:, None, :] * y_ctx, ln_g[l, 0], ln_b[l, 0])
            u_ctx = _modulate(h_ctx, m_ctx[3], m_ctx[4])
            L = u_ctx.shape[1]
            f = _moe(jnp.concatenate([u_lat.reshape(-1, D), u_ctx.reshape(-1, D)], 0), router_w, router_b,
                     exp_w_gate[l], exp_w_up[l], exp_w_down[l])
            f_lat = f[:B * T].reshape(B, T, D)
            h_ctx = _layer_norm(ALPHA * h_ctx + m_ctx[5][:, None, :] * f[B * T:].reshape(B, L, D),
                                ln_g[l, 1], ln_b[l, 1])
        h_lat = _layer_norm(ALPHA * h_lat + m_lat[5][:, None, :] * f_lat, ln_g[l, 1], ln_b[l, 1])
    return h_lat


_drawn_inputs = setup_inputs


def setup_inputs(seed=0):
    import zlib

    import numpy as np

    out = dict(_drawn_inputs(seed))
    spreads = {}
    factors = {'ada_b': 2.997,
     'na_rpb': 64.0,
     'rw_w_up': 8.0,
     'rw_a0': 8.0,
     'rw_a_up': 3.48,
     'rw_k_k': 27.929,
     'rw_k_a': 6.189,
     'rw_gn_g': 43.451,
     'rw_gn_b': 35.714,
     'da_lq1': 64.0,
     'da_lk1': 64.0,
     'da_lq2': 3.768,
     'da_lk2': 6.038,
     'da_subln_g': 34.387,
     'router_b': 2.814}
    for name, (base, spread) in spreads.items():
        noise = np.random.default_rng([zlib.crc32(name.encode()), seed]).standard_normal(out[name].shape)
        drawn = base * np.exp(spread * noise) if base else spread * noise
        out[name] = __import__('jax').numpy.asarray(drawn.astype(out[name].dtype))
    for name, factor in factors.items():
        out[name] = (out[name] * factor).astype(out[name].dtype)
    return out
```

```python
from contextlib import ExitStack, contextmanager

import concourse.bass as bass
from concourse import mybir

F32 = mybir.dt.float32
ACT = mybir.ActivationFunctionType
ALU = mybir.AluOpType
AX = mybir.AxisListType

P = 128
D = 1024
KD = D // P
T_CTX, T_LAT = 256, 256
T = T_CTX + T_LAT
NB = T // P
DEPTH = 2
GRID_W = 64
HP = 4
CH = 64
RW_IN = 1792
N_EXP, D_EXP = 16, 512
ALPHA = (2 * DEPTH) ** 0.25
DECAY = 0.6065306597126334
HD = 64
WIN_C = 16
DA_H = 8
LAMBDA_INIT = 0.3555090675909693
NEG = -1.0e30

C_ID, C_ONES, C_MASK, C_LVL, C_WIN, C_ROT, C_IOTA, C_TRI, C_ALL, C_END = 0, 128, 256, 768, 1536, 1600, 1728, 1856, 1984, 2112
C_EIDX = C_END
C_JIDX = C_END + 16
C_END += 16 + 32
N_ITEM = 26
R_C, R_CC, R_SW, R_W0, R_A0, R_KK, R_KA, R_RK, R_GG, R_GB, R_END = 0, 8, 16, 58, 66, 74, 78, 82, 86, 90, 94


class Tiles:

    ndump = 0


class Link:

    def __init__(self, eng, sem):
        self.eng, self.sem, self.n = eng, sem, 0

    def __call__(self, ins):
        self.n += 1
        ins.then_inc(self.sem, 1)
        self.eng.wait_ge(self.sem, self.n)


def clear_block(nc, sems):
    with nc.Block() as block:
        @block.sync
        def _(sp):
            for s in sems:
                sp.sem_clear(s)


@contextmanager
def phase(nc, sems):
    with nc.Block() as block:
        yield block
    clear_block(nc, sems)


def shape_constants(np):
    c = np.zeros((P, C_END), np.float32)
    i = np.arange(P)
    c[:, C_ID:C_ID + P] = np.eye(P)
    same_head = (i[:, None] // CH) == (i[None] // CH)
    c[:, C_ONES:C_ONES + P] = same_head
    s, t = i[:, None] % CH, i[None] % CH
    for n, m in enumerate((s < t, s <= t, s > t, s >= t)):
        c[:, C_MASK + n * P:C_MASK + (n + 1) * P] = m & same_head
    for n in range(6):
        b = 1 << n
        c[:, C_LVL + n * P:C_LVL + (n + 1) * P] = same_head & (s // (2 * b) == t // (2 * b)) & (s // b != t // b)
    c[:, C_IOTA:C_IOTA + P] = i[None]
    c[:, C_EIDX:C_EIDX + 16] = np.arange(16)[None]
    c[:, C_JIDX:C_JIDX + 32] = np.arange(32)[None]
    c[:, C_TRI:C_TRI + P] = i[:, None] < i[None]
    c[:, C_ALL:C_ALL + P] = 1.0
    q, k = i[:, None] % GRID_W, np.arange(GRID_W)[None]
    lo = np.clip(q - WIN_C // 2, 0, GRID_W - WIN_C)
    c[:, C_WIN:C_WIN + GRID_W] = np.where((k >= lo) & (k < lo + WIN_C), 0.0, NEG)
    for r in range(P):
        m = r % 32
        if m < 16:
            c[r + 16, C_ROT + r] = -1.0
        else:
            c[r - 16, C_ROT + r] = 1.0
    rope = np.zeros((P, 2, T_LAT), np.float32)
    tok = np.arange(T_LAT)
    inv = (np.float32(10000.0) ** (-np.arange(16, dtype=np.float32) / np.float32(16))).astype(np.float32)
    for r in range(P):
        pos = tok // GRID_W if (r % 64) < 32 else tok % GRID_W
        ang = pos.astype(np.float32) * inv[r % 16]
        rope[r, 0], rope[r, 1] = np.cos(ang), np.sin(ang)
    return c, rope.reshape(P, 2 * T_LAT)


def setup_block(nc, g, S):
    with ExitStack() as ctx:
        rows = ctx.enter_context(nc.sbuf_tensor("rows", [R_END, P], F32))
        abrows = ctx.enter_context(nc.sbuf_tensor("abrows", [96, P], F32))
        loaded = ctx.enter_context(nc.semaphore("consts_loaded"))
        turned = ctx.enter_context(nc.semaphore("columns_turned"))
        copied = ctx.enter_context(nc.semaphore("columns_copied"))
        block = ctx.enter_context(phase(nc, [loaded, turned, copied]))
        loads = [
            (S.cst[:, :], g.const),
            (abrows[:, :], g.ada_b.rearrange("l (j p) -> (l j) p", p=P)),
            (rows[R_C:R_CC, :], g.c.rearrange("b (k p) -> (b k) p", p=P)),
            (rows[R_CC:R_SW, :], g.c_ctx.rearrange("(k p) -> k p", p=P)),
            (rows[R_SW:R_W0, :], g.shift_w.rearrange("n j (k p) -> (n j k) p", p=P)),
            (rows[R_W0:R_A0, :], g.rw_w0.rearrange("n d (k p) -> (n d k) p", p=P)),
            (rows[R_A0:R_KK, :], g.rw_a0.rearrange("n d (k p) -> (n d k) p", p=P)),
            (rows[R_KK:R_KA, :], g.rw_k_k.rearrange("n (k p) -> (n k) p", p=P)),
            (rows[R_KA:R_RK, :], g.rw_k_a.rearrange("n (k p) -> (n k) p", p=P)),
            (rows[R_RK:R_GG, :], g.rw_r_k.rearrange("n (k a) p -> (n k) (a p)", a=2)),
            (rows[R_GG:R_GB, :], g.rw_gn_g.rearrange("n (k p) -> (n k) p", p=P)),
            (rows[R_GB:R_END, :], g.rw_gn_b.rearrange("n (k p) -> (n k) p", p=P)),
            (S.router[:, :, :], g.router_w.rearrange("(k p) e -> p k e", p=P)),
            (S.rbias[:, :], g.router_b.rearrange("(a e) -> a e", a=1).to_broadcast([P, N_EXP])),
        ]

        @block.sync
        def _(sp):
            for dst, src in loads:
                sp.dma_start(dst, src).then_inc(loaded, 16)

        @block.tensor
        def _(pe):
            pe.wait_ge(loaded, 16 * len(loads))
            nc.tensor.transpose(S.ps[:, 0, 0:R_END], rows[:, :], S.cst[0:R_END, C_ID:C_ID + R_END]).then_inc(turned, 1)
            nc.tensor.transpose(S.ps[:, 1, 0:96], abrows[:, :], S.cst[0:96, C_ID:C_ID + 96]).then_inc(turned, 1)

        @block.vector
        def _(dve):
            dve.wait_ge(turned, 1)
            nc.vector.tensor_copy(S.col[:, :], S.ps[:, 0, 0:R_END]).then_inc(copied, 1)
            dve.wait_ge(turned, 2)
            nc.vector.tensor_copy(S.adab[:, :], S.ps[:, 1, 0:96])

        @block.scalar
        def _(act):
            act.wait_ge(copied, 1)
            nc.scalar.activation(S.csil[:, :], S.col[:, R_C:R_SW], ACT.Silu)


ADA_U = 4
ADA_W = 512


def ada_blocks(nc, g, S):
    with ExitStack() as ctx:
        slab = ctx.enter_context(nc.sbuf_tensor("ada_slab", [P, ADA_U, KD, ADA_W], F32))
        full = [ctx.enter_context(nc.semaphore(f"ada_slab_full{u}")) for u in range(ADA_U)]
        summed = ctx.enter_context(nc.semaphore("ada_summed"))
        cc = csil = S.csil[:, :].rearrange("p (w k) -> p k w", w=2)
        per = ADA_U * ADA_W // P
        for l in range(DEPTH):
            src = g.ada_w[l].rearrange("(k p) n -> p k n", p=P)
            with nc.Fori(0, 6 * D // (ADA_U * ADA_W)) as it:
                with nc.Block() as block:
                    @block.sync
                    def _(sp):
                        for u in range(0, ADA_U, 2):
                            sp.dma_start(slab[:, u], src[:, :, bass.ds(it * (ADA_U * ADA_W) + u * ADA_W, ADA_W)]).then_inc(full[u], 16)

                    @block.scalar
                    def _(act):
                        for u in range(1, ADA_U, 2):
                            act.dma_start(slab[:, u], src[:, :, bass.ds(it * (ADA_U * ADA_W) + u * ADA_W, ADA_W)]).then_inc(full[u], 16)

                    @block.tensor
                    def _(pe):
                        for u in range(ADA_U):
                            pe.wait_ge(full[u], 16)
                            for j in range(ADA_W // P):
                                n = u * (ADA_W // P) + j
                                for k in range(KD):
                                    last = nc.tensor.matmul(S.ps[:, 0, 2 * n:2 * n + 2], slab[:, u, k, j * P:(j + 1) * P],
                                                            csil[:, k, :], start=(k == 0), stop=(k == KD - 1))
                        last.then_inc(summed, 1)

                    @block.vector
                    def _(dve):
                        dve.wait_ge(summed, 1)
                        for w in range(2):
                            nc.vector.tensor_tensor(
                                S.mcol[:, l, w, bass.ds(it * per, per)],
                                S.ps[:, 0, 0:2 * per].rearrange("p (n w) -> p w n", w=2)[:, w, :],
                                S.adab[:, bass.ds(it * per + l * 48, per)], ALU.add)
                clear_block(nc, full + [summed])
        with nc.Block() as block:
            @block.vector
            def _(dve):
                for l in range(DEPTH):
                    for m in (1, 4):
                        nc.vector.tensor_scalar(S.mcol[:, l, :, m * KD:(m + 1) * KD], S.mcol[:, l, :, m * KD:(m + 1) * KD],
                                                1.0, None, ALU.add)


def modulate_block(nc, g, S, l, m, load_h=False, blocks=range(NB)):
    tag = f"{l}_{m}"
    blocks = list(blocks)
    with ExitStack() as ctx:
        loaded = ctx.enter_context(nc.semaphore("h_loaded" + tag))
        turned = ctx.enter_context(nc.semaphore("h_turned" + tag))
        lat_done = ctx.enter_context(nc.semaphore("u_lat_done" + tag))
        ctx_done = ctx.enter_context(nc.semaphore("u_ctx_done" + tag))
        block = ctx.enter_context(phase(nc, [loaded, turned, lat_done, ctx_done]))

        @block.sync
        def _(sp):
            if load_h:
                load_tokens(sp, g, S.h, loaded)

        @block.tensor
        def _(pe):
            if load_h:
                pe.wait_ge(loaded, 32)
            for k in range(KD):
                for half, done in ((0, ctx_done), (1, lat_done)):
                    mine = [b for b in blocks if b // 2 == half]
                    if mine and k >= 4:
                        pe.wait_ge(done, k - 3)
                    for b in mine:
                        last = nc.tensor.transpose(S.ps[:, 4 * half + k % 4, (b % 2) * P:(b % 2 + 1) * P],
                                                   S.h[:, b, k * P:(k + 1) * P], S.cst[:, C_ID:C_ID + P])
                last.then_inc(turned, 1)

        def col(w, r, k):
            return S.mcol[:, l, w, (m + r) * KD + k:(m + r) * KD + k + 1]

        @block.scalar
        def _(act):
            for k in range(KD):
                act.wait_ge(turned, k + 1)
                nc.scalar.activation(S.uT[:, k, T_CTX:T], S.ps[:, 4 + k % 4, 0:T_LAT], ACT.Identity,
                                     bias=col(0, 0, k), scale=col(0, 1, k)).then_inc(lat_done, 1)

        @block.vector
        def _(dve):
            if blocks[0] == 0:
                for k in range(KD):
                    dve.wait_ge(turned, k + 1)
                    nc.vector.tensor_scalar(S.uT[:, k, 0:T_CTX], S.ps[:, k % 4, 0:T_CTX],
                                            col(1, 1, k), col(1, 0, k), ALU.mult, ALU.add).then_inc(ctx_done, 1)


def load_tokens(sp, g, h, sem):
    sp.dma_start(h[:, 0:2, :], g.ctx[0].rearrange("(b p) d -> p b d", p=P)).then_inc(sem, 16)
    sp.dma_start(h[:, 2:4, :], g.x[0].rearrange("(b p) d -> p b d", p=P)).then_inc(sem, 16)


def dump_block(nc, S, dst, src):
    with ExitStack() as ctx:
        S.ndump += 1
        sem = ctx.enter_context(nc.semaphore(f"dumped{S.ndump}"))
        block = ctx.enter_context(nc.Block())

        @block.sync
        def _(sp):
            sp.dma_start(dst, src).then_inc(sem, 16)
            sp.wait_ge(sem, 16)


NA_SCALE = float(HD) ** -0.5
PAIR = 2 * HD
W_NA = 512


def load_pair_slabs(sp, g, S, hp):
    src = g.even_w_in[0].rearrange("(k p) n -> p k n", p=P)
    for n in range(6):
        sp.dma_start(S.wslab[:, n], src[:, :, bass.ds(hp * PAIR + n * W_NA, PAIR)]).then_inc(S.slab_full, 16)


def lora_block(nc, g, S):
    with ExitStack() as ctx:
        slab = ctx.enter_context(nc.sbuf_tensor("lora_slab", [P, KD, 256], F32))
        loaded = ctx.enter_context(nc.semaphore("lora_loaded"))
        cleared = ctx.enter_context(nc.semaphore("lora_cleared"))
        projected = ctx.enter_context(nc.semaphore("lora_projected"))
        scaled = ctx.enter_context(nc.semaphore("lora_scaled"))
        chain = ctx.enter_context(nc.semaphore("lora_conv_chain"))
        conved = ctx.enter_context(nc.semaphore("lora_conved"))
        block = ctx.enter_context(phase(nc, [loaded, cleared, projected, scaled, chain, conved]))

        @block.sync
        def _(sp):
            src = g.even_w_in[0].rearrange("(k p) n -> p k n", p=P)
            sp.dma_start(slab[:, :, :], src[:, :, 3072:3328]).then_inc(loaded, 16)
            load_pair_slabs(sp, g, S, 0)
            sp.wait_ge(cleared, 1)
            for d in range(2):
                sp.dma_start(S.wall[0:64, d, :], g.rw_w_up[0, d]).then_inc(S.wall_full, 16)
                sp.dma_start(S.wall[64:128, 2 + d, :], g.rw_a_up[0, d]).then_inc(S.wall_full, 16)
            sp.dma_start(S.wall[:, 4, :], g.rw_g_up[0]).then_inc(S.wall_full, 16)

        @block.gpsimd
        def _(pool):
            nc.gpsimd.memset(S.wall[:, :, :], 0.0).then_inc(cleared, 1)

        @block.tensor
        def _(pe):
            pe.wait_ge(loaded, 16)
            for j in range(2):
                for k in range(KD):
                    last = nc.tensor.matmul(S.ps[:, j, :], slab[:, k, j * P:(j + 1) * P], S.uT[:, k, :],
                                            start=(k == 0), stop=(k == KD - 1))
                last.then_inc(projected, 1)

        @block.scalar
        def _(act):
            for j in range(2):
                act.wait_ge(projected, j + 1)
                w1 = R_SW + 14 + 12 + j
                nc.scalar.activation(S.xlora[:, j, :], S.ps[:, j, :], ACT.Copy, scale=S.col[:, w1:w1 + 1]).then_inc(scaled, 1)
            act.wait_ge(conved, 1)
            nc.scalar.activation(S.xlora[0:64, 0, :], S.xlora[0:64, 0, :], ACT.Tanh)
            act.wait_ge(conved, 2)
            nc.scalar.activation(S.xlora[:, 1, :], S.xlora[:, 1, :], ACT.Sigmoid)

        @block.vector
        def _(dve):
            link = Link(dve, chain)
            nc.vector.memset(S.reset[:, :], 1.0)
            for j in range(2):
                dve.wait_ge(scaled, j + 1)
                conv_taps(nc, link, S.xlora[:, j, :], S.ps[:, j, :],
                          S.col[:, R_SW + 12 + j:R_SW + 13 + j], S.col[:, R_SW + 28 + 12 + j:R_SW + 28 + 13 + j], conved)
            nc.vector.memset(S.reset[:, :].rearrange("p (c t) -> p c t", t=CH)[:, :, 0:1], 0.0)


def conv_taps(nc, link, out, raw, w0, w2, done):
    o = out.rearrange("p (g t) -> p g t", g=2)
    r = raw.rearrange("p (g t) -> p g t", g=2)
    n = T_CTX
    link(nc.vector.scalar_tensor_tensor(out=o[:, :, 1:n], in0=r[:, :, 0:n - 1], scalar=w0, in1=o[:, :, 1:n],
                                        op0=ALU.mult, op1=ALU.add))
    nc.vector.scalar_tensor_tensor(out=o[:, :, 0:n - 1], in0=r[:, :, 1:n], scalar=w2, in1=o[:, :, 0:n - 1],
                                   op0=ALU.mult, op1=ALU.add).then_inc(done, 1)


def project_block(nc, g, S, hp, A):
    with ExitStack() as ctx:
        sem = lambda n: ctx.enter_context(nc.semaphore("pj_" + n))
        ready, scaled, chain, picked, conved = sem("ready"), sem("scaled"), sem("chain"), sem("picked"), sem("conved")
        with nc.Block() as block:
            @block.tensor
            def _(pe):
                pe.wait_ge(S.slab_full, 16 * 6)
                for n in (0, 1, 3, 4, 5):
                    for k in range(KD):
                        last = nc.tensor.matmul(S.ps[:, n, :], S.wslab[:, n, k, :], S.uT[:, k, :],
                                                start=(k == 0), stop=(k == KD - 1))
                    last.then_inc(ready, 1)
                for b in range(NB):
                    for k in range(KD):
                        last = nc.tensor.matmul(S.ps[:, 2, b * P:(b + 1) * P], S.uT[:, k, b * P:(b + 1) * P],
                                                S.wslab[:, 2, k, :], start=(k == 0), stop=(k == KD - 1))
                last.then_inc(ready, 1)

            @block.scalar
            def _(act):
                act.wait_ge(ready, 1)
                nc.scalar.activation(A.qT[:, :], S.ps[:, 0, :], ACT.Copy)
                act.wait_ge(picked, 1)
                for j in range(3):
                    act.wait_ge(ready, 3 + j)
                    nc.scalar.activation(S.prc[:, j, :], S.ps[:, 3 + j, :], ACT.Copy, scale=S.hcol[:, 3 + j:4 + j]).then_inc(scaled, 1)
                act.wait_ge(ready, 6)
                nc.scalar.activation(A.v[:, :, :], S.ps[:, 2, :].rearrange("p (b n) -> p b n", b=NB), ACT.Copy)

            @block.vector
            def _(dve):
                link = Link(dve, chain)
                for j in range(3):
                    a = R_SW + 14 * j
                    nc.vector.tensor_copy(S.hcol[:, 3 * j:3 * j + 3].rearrange("p (n o) -> p n o", o=1),
                                          S.col[:, a:a + 12].rearrange("p (n h) -> p n h", h=HP)[:, :, bass.ds(hp, 1)])
                link(nc.vector.tensor_copy(S.hcol[:, 9:18].rearrange("p (n o) -> p n o", o=1),
                                           S.col[:, R_W0:R_END].rearrange("p (n h) -> p n h", h=HP)[:, :, bass.ds(hp, 1)]))
                link(nc.vector.tensor_scalar(S.hcol[:, 18:19], S.hcol[:, 14:15], -1.0, 1.0, ALU.mult, ALU.add))
                nc.vector.tensor_copy(S.wst[:, :, :], S.wall[:, :, bass.ds(hp * PAIR, PAIR)]).then_inc(picked, 1)
                dve.wait_ge(ready, 2)
                nc.vector.tensor_copy(A.kT[:, :], S.ps[:, 1, :])
                for j in range(3):
                    dve.wait_ge(scaled, j + 1)
                    conv_taps(nc, link, S.prc[:, j, :], S.ps[:, 3 + j, :], S.hcol[:, j:j + 1], S.hcol[:, 6 + j:7 + j], conved)
        clear_block(nc, [ready, scaled, chain, picked, conved])


def na_block(nc, g, S, hp, A):
    units = [(qb, hh) for qb in (2, 3, 0, 1) for hh in (0, 1)]
    with ExitStack() as ctx:
        sem = lambda n: ctx.enter_context(nc.semaphore("na_" + n))
        bias_full, masked = sem("bias_full"), sem("bias_masked")
        scored, read, maxed, exped = sem("scored"), sem("scores_read"), sem("maxed"), sem("exped")
        normed, turned, copied, summed, written, chain = (sem("normed"), sem("turned"), sem("pt_copied"), sem("av_summed"),
                                                          sem("o_written"), sem("chain"))
        sb = lambda n, s: ctx.enter_context(nc.sbuf_tensor("na_" + n, s, F32))
        bias = sb("bias", [P, 2, 2, T_LAT])
        s_, p_, pt = sb("s", [P, 2, T]), sb("p", [P, 2, T]), sb("pt", [P, 2, NB, P])
        nmax, ssum, rinv = sb("nmax", [P, 8]), sb("ssum", [P, 8]), sb("rinv", [P, 8])

        def keys(u):
            return T if units[u][0] >= 2 else T_CTX

        with nc.Block() as block:
            @block.sync
            def _(sp):
                for qt in range(2):
                    for r2 in range(2):
                        for hh in range(2):
                            sp.dma_start(bias[r2 * 64:(r2 + 1) * 64, qt, hh, :].rearrange("p (a b) -> p a b", a=4),
                                         g.toep[bass.ds(hp * 2 + hh, 1), :, 3 - 2 * qt - r2:7 - 2 * qt - r2, :].rearrange("o c a b -> (o c) a b")).then_inc(bias_full, 16)
                sp.sem_clear(S.slab_full)
                load_pair_slabs(sp, g, S, hp + 1)

            @block.gpsimd
            def _(pool):
                pool.wait_ge(bias_full, 16 * 8)
                b = bias[:, :, :, :].rearrange("p q h (r c) -> p (q h r) c", c=GRID_W)
                nc.gpsimd.tensor_tensor(b, b, S.cst[:, C_WIN:C_WIN + GRID_W].unsqueeze(1).to_broadcast([P, 16, GRID_W]),
                                        ALU.add).then_inc(masked, 1)

            @block.tensor
            def _(pe):
                n = len(units)
                for i in range(n + 2):
                    if i < n:
                        qb, hh = units[i]
                        if i >= 2:
                            pe.wait_ge(read, i - 1)
                        h0 = hh * HD
                        nc.tensor.matmul(S.ps[:, i % 2, 0:keys(i)], A.qT[h0:h0 + HD, qb * P:(qb + 1) * P],
                                         A.kT[h0:h0 + HD, 0:keys(i)], start=True, stop=True).then_inc(scored, 1)
                    if 0 <= i - 1 < n:
                        u = i - 1
                        pe.wait_ge(normed, u + 1)
                        if u >= 2:
                            pe.wait_ge(copied, u - 1)
                        for b in range(keys(u) // P):
                            last = nc.tensor.transpose(S.ps[:, 2 + u % 2, b * P:(b + 1) * P], p_[:, u % 2, b * P:(b + 1) * P],
                                                       S.cst[:, C_ID:C_ID + P])
                        last.then_inc(turned, 1)
                    if 0 <= i - 2 < n:
                        u = i - 2
                        qb, hh = units[u]
                        pe.wait_ge(copied, u + 1)
                        if u >= 2:
                            pe.wait_ge(written, u - 1)
                        h0 = hh * HD
                        nk = keys(u) // P
                        for b in range(nk):
                            last = nc.tensor.matmul(S.ps[h0:h0 + HD, 4 + u % 2, 0:P], A.v[:, b, h0:h0 + HD], pt[:, u % 2, b, :],
                                                    start=(b == 0), stop=(b == nk - 1))
                        last.then_inc(summed, 1)

            @block.vector
            def _(dve):
                link = Link(dve, chain)
                n = len(units)
                dve.wait_ge(masked, 1)
                for i in range(n + 1):
                    if i < n:
                        qb, hh = units[i]
                        dve.wait_ge(scored, i + 1)
                        if i >= 2:
                            dve.wait_ge(exped, i - 1)
                        if keys(i) == T:
                            nc.vector.tensor_scalar(s_[:, i % 2, 0:T_CTX], S.ps[:, i % 2, 0:T_CTX], NA_SCALE, None, ALU.mult)
                            nc.vector.scalar_tensor_tensor(out=s_[:, i % 2, T_CTX:T], in0=S.ps[:, i % 2, T_CTX:T],
                                                           scalar=NA_SCALE, in1=bias[:, qb - 2, hh, :],
                                                           op0=ALU.mult, op1=ALU.add).then_inc(read, 1)
                        else:
                            nc.vector.tensor_scalar(s_[:, i % 2, 0:T_CTX], S.ps[:, i % 2, 0:T_CTX], NA_SCALE, None,
                                                    ALU.mult).then_inc(read, 1)
                        dve.wait_ge(read, i + 1)
                        nc.vector.tensor_reduce(nmax[:, i:i + 1], s_[:, i % 2, 0:keys(i)], AX.X, ALU.max,
                                                negate=True).then_inc(maxed, 1)
                    if i >= 1:
                        u = i - 1
                        dve.wait_ge(exped, u + 1)
                        link(nc.vector.reciprocal(rinv[:, u:u + 1], ssum[:, u:u + 1]))
                        nc.vector.tensor_scalar(p_[:, u % 2, 0:keys(u)], p_[:, u % 2, 0:keys(u)], rinv[:, u:u + 1], None,
                                                ALU.mult).then_inc(normed, 1)

            @block.scalar
            def _(act):
                n = len(units)
                for i in range(n + 2):
                    if i < n:
                        act.wait_ge(maxed, i + 1)
                        if i >= 2:
                            act.wait_ge(turned, i - 1)
                        nc.scalar.activation(p_[:, i % 2, 0:keys(i)], s_[:, i % 2, 0:keys(i)], ACT.Exp,
                                             bias=nmax[:, i:i + 1], accum_out=ssum[:, i:i + 1]).then_inc(exped, 1)
                    if 0 <= i - 1 < n:
                        u = i - 1
                        act.wait_ge(turned, u + 1)
                        if u >= 2:
                            act.wait_ge(summed, u - 1)
                        nk = keys(u) // P
                        nc.scalar.activation(pt[:, u % 2, 0:nk, :], S.ps[:, 2 + u % 2, 0:nk * P].rearrange("p (b q) -> p b q", q=P),
                                             ACT.Copy).then_inc(copied, 1)
                    if 0 <= i - 2 < n:
                        u = i - 2
                        qb, hh = units[u]
                        act.wait_ge(summed, u + 1)
                        h0 = hh * HD
                        nc.scalar.activation(S.oT[h0:h0 + HD, bass.ds(hp, 1), qb * P:(qb + 1) * P].rearrange("p o t -> p (o t)"),
                                             S.ps[h0:h0 + HD, 4 + u % 2, 0:P], ACT.Copy).then_inc(written, 1)
        clear_block(nc, [bias_full, masked, scored, read, maxed, exped, normed, turned, copied, summed, written, chain])


def toeplitz_copies(nc, g, S):
    na, nb = 15, 31
    flat = g.na_rpb.rearrange("n h a b -> (n h a b)")
    with nc.Block() as block:
        @block.sync
        def _(sp):
            for h in range(2 * HP):
                at = flat[h * na * nb + 4 * nb + 15:h * na * nb + 4 * nb + 16]
                src = bass.AP(tensor=at.tensor, offset=at.offset, ap=[[nb, 7], [-1, GRID_W], [1, GRID_W]])
                sp.dma_start(g.toep[h].rearrange("c a b -> a c b"), src).then_inc(S.toep_written, 16)


NC_ = T_CTX // CH
E_IN, E_EX, E_INV, E_BAR = range(4)
BA, BR, BB, BK, BBB, BKB = range(6)


def rwkv_pair(nc, g, S, hp):
    with ExitStack() as st:
        sb = lambda n, s: st.enter_context(nc.sbuf_tensor("rw_" + n, s, F32))
        R = Tiles()
        R.y = sb("y", [P, T])
        R.bonus = sb("bonus", [P, T])
        R.gate = sb("gate", [P, T])
        R.last = [sb(f"last{d}", [P, P]) for d in range(2)]
        R.bd = [sb(f"bd{d}", [P, 6, NC_, P]) for d in range(2)]
        R.vbd = sb("vbd", [P, NC_, P])
        R.wc = sb("wc", [P, 2, NC_])
        with nc.Block() as block:
            @block.gpsimd
            def _(pool):
                for d in range(2):
                    nc.gpsimd.memset(R.last[d][:, :], 0.0)
                    nc.gpsimd.memset(R.bd[d][:, :, :, :], 0.0)
                nc.gpsimd.memset(R.vbd[:, :, :], 0.0)
        with nc.Fori(0, 2) as half:
            tok = half * T_CTX
            rwkv_prepare(nc, S, R, tok)
            rwkv_chunks(nc, S, R, tok)
        rwkv_finish(nc, S, R, hp)


def rwkv_prepare(nc, S, R, tok):
    n = T_CTX
    with ExitStack() as st:
        sb = lambda m, s: st.enter_context(nc.sbuf_tensor("rp_" + m, s, F32))
        sem = lambda m: st.enter_context(nc.semaphore("rp_" + m))
        sig, av, keff, nka = sb("sig", [P, 2, n]), sb("a", [P, 2, n]), sb("keff", [P, 2, n]), sb("nka", [P, 2, n])
        cinc, y_, z_, w_ = sb("cinc", [P, 2, n]), sb("cexc", [P, 2, n]), sb("cbar", [P, 2, n]), sb("crev", [P, n])
        kraw, sq, kk, ex = sb("kraw", [P, n]), sb("sq", [P, n]), sb("kk", [P, n]), sb("ex", [P, 2, 4, n])
        xl = sb("xl", [P, 2, n])
        rkv = sb("rkv", [P, 3, n])
        staged, loraed, sigmoided, squared, normsum, rooted = (sem("staged"), sem("loraed"), sem("sigmoided"), sem("squared"),
                                                               sem("normsum"), sem("rooted"))
        argued, exped, chain, bonused, summed = sem("argued"), sem("exped"), sem("chain"), sem("bonused"), sem("summed")
        h = S.hcol

        with nc.Block() as block:
            @block.gpsimd
            def _(pool):
                nc.gpsimd.tensor_copy(xl[:, :, :], S.xlora[:, :, bass.ds(tok, n)]).then_inc(staged, 1)
                nc.gpsimd.tensor_copy(rkv[:, :, :], S.prc[:, :, bass.ds(tok, n)]).then_inc(staged, 1)

            @block.tensor
            def _(pe):
                pe.wait_ge(staged, 1)
                for j in range(4):
                    nc.tensor.matmul(S.ps[:, j, 0:n], S.wst[:, j, :], xl[:, 0, :], start=True, stop=True).then_inc(loraed, 1)
                nc.tensor.matmul(S.ps[:, 4, 0:n], S.wst[:, 4, :], xl[:, 1, :], start=True, stop=True).then_inc(loraed, 1)
                pe.wait_ge(squared, 1)
                nc.tensor.matmul(S.ps[:, 5, 0:n], S.cst[:, C_ONES:C_ONES + P], sq[:, :], start=True, stop=True).then_inc(normsum, 1)
                pe.wait_ge(bonused, 1)
                nc.tensor.matmul(S.ps[:, 6, 0:n], S.cst[:, C_ONES:C_ONES + P], kraw[:, :], start=True, stop=True).then_inc(summed, 1)

            @block.scalar
            def _(act):
                for j in range(4):
                    act.wait_ge(loraed, j + 1)
                    nc.scalar.activation((sig if j < 2 else av)[:, j % 2, :], S.ps[:, j, 0:n], ACT.Sigmoid,
                                         bias=h[:, 9 + j:10 + j]).then_inc(sigmoided, 1)
                act.wait_ge(loraed, 5)
                nc.scalar.activation(R.gate[:, bass.ds(tok, n)], S.ps[:, 4, 0:n], ACT.Copy)
                act.wait_ge(normsum, 1)
                nc.scalar.activation(sq[:, :], S.ps[:, 5, 0:n], ACT.Sqrt).then_inc(rooted, 1)
                act.wait_ge(argued, 1)
                args = [[(cinc[:, 0], -1), (y_[:, 0], -1), (cinc[:, 0], 1), (z_[:, 0], -1)],
                        [(w_[:, :], -1), (z_[:, 1], -1), (w_[:, :], 1), (y_[:, 1], -1)]]
                for d in range(2):
                    for e in range(4):
                        a, sign = args[d][e]
                        nc.scalar.activation(ex[:, d, e, :], a, ACT.Exp, scale=sign * DECAY).then_inc(exped, 1)
                    tot = cinc[:, d, :].rearrange("p (c t) -> p c t", t=CH)[:, :, CH - 1:CH]
                    nc.scalar.activation(R.wc[:, d, :].rearrange("p (c o) -> p c o", o=1), tot, ACT.Exp, scale=-DECAY)

            @block.vector
            def _(dve):
                link = Link(dve, chain)
                dve.wait_ge(staged, 2)
                r, k, v = rkv[:, 0, :], rkv[:, 1, :], rkv[:, 2, :]
                link(nc.vector.tensor_scalar(kraw[:, :], k, h[:, 13:14], None, ALU.mult))
                nc.vector.tensor_tensor(sq[:, :], kraw[:, :], kraw[:, :], ALU.mult).then_inc(squared, 1)
                dve.wait_ge(sigmoided, 2)
                for d in range(2):
                    link(nc.vector.tensor_tensor_scan(cinc[:, d, :], S.reset[:, 0:n], sig[:, d, :], 0.0, ALU.mult, ALU.add))
                    nc.vector.tensor_tensor(y_[:, d, :], cinc[:, d, :], sig[:, d, :], ALU.subtract)
                    c4 = cinc[:, d, :].rearrange("p (c t) -> p c t", t=CH)
                    link(nc.vector.tensor_tensor(z_[:, d, :].rearrange("p (c t) -> p c t", t=CH),
                                                 c4[:, :, CH - 1:CH].to_broadcast([P, NC_, CH]), c4, ALU.subtract))
                nc.vector.tensor_tensor(w_[:, :], z_[:, 1, :], sig[:, 1, :], ALU.add).then_inc(argued, 1)
                dve.wait_ge(sigmoided, 4)
                for d in range(2):
                    link(nc.vector.tensor_scalar(keff[:, d, :], av[:, d, :], h[:, 14:15], h[:, 18:19], ALU.mult, ALU.add))
                    link(nc.vector.tensor_tensor(keff[:, d, :], keff[:, d, :], k, ALU.mult))
                dve.wait_ge(rooted, 1)
                link(nc.vector.tensor_scalar(sq[:, :], sq[:, :], 1e-12, None, ALU.max))
                link(nc.vector.reciprocal(sq[:, :], sq[:, :]))
                link(nc.vector.tensor_tensor(kk[:, :], kraw[:, :], sq[:, :], ALU.mult))
                for d in range(2):
                    link(nc.vector.scalar_tensor_tensor(out=nka[:, d, :], in0=kk[:, :], scalar=-1.0, in1=av[:, d, :],
                                                        op0=ALU.mult, op1=ALU.mult))
                link(nc.vector.tensor_tensor(kraw[:, :], keff[:, 0, :], keff[:, 1, :], ALU.add))
                nc.vector.scalar_tensor_tensor(out=kraw[:, :], in0=kraw[:, :], scalar=h[:, 15:16], in1=r,
                                               op0=ALU.mult, op1=ALU.mult).then_inc(bonused, 1)
                for hh in range(2):
                    p0 = hh * CH
                    nc.vector.tensor_copy(R.vbd[p0:p0 + CH, :, p0:p0 + CH], v[p0:p0 + CH, :].rearrange("p (c t) -> p c t", t=CH))
                for d in range(2):
                    terms = ((BA, kk[:, :], E_EX), (BR, r, E_IN), (BB, nka[:, d, :], E_INV), (BK, keff[:, d, :], E_INV),
                             (BBB, nka[:, d, :], E_BAR), (BKB, keff[:, d, :], E_BAR))
                    dve.wait_ge(exped, 4 * d + 4)
                    for which, x, e in terms:
                        for hh in range(2):
                            p0 = hh * CH
                            nc.vector.tensor_tensor(R.bd[d][p0:p0 + CH, which, :, p0:p0 + CH],
                                                    x[p0:p0 + CH, :].rearrange("p (c t) -> p c t", t=CH),
                                                    ex[p0:p0 + CH, d, e, :].rearrange("p (c t) -> p c t", t=CH), ALU.mult)
                dve.wait_ge(summed, 1)
                nc.vector.tensor_tensor(R.bonus[:, bass.ds(tok, n)], S.ps[:, 6, 0:n], v, ALU.mult)
        clear_block(nc, [staged, loraed, sigmoided, squared, normsum, rooted, argued, exped, chain, bonused, summed])


def rwkv_chunks(nc, S, R, tok):
    with ExitStack() as st:
        sem = lambda m: st.enter_context(nc.semaphore("rc_" + m))
        names = ["tn", "An", "Bn", "Kn", "LT", "MbT", "AkT", "MkT", "Et", "Tm", "Z", "F", "G", "U0"]
        M = [{m: st.enter_context(nc.sbuf_tensor(f"rc_{m}{d}", [P, NC_, P], F32)) for m in names[1:]} for d in range(2)]
        Vn = st.enter_context(nc.sbuf_tensor("rc_Vn", [P, NC_, P], F32))
        X = [st.enter_context(nc.sbuf_tensor(f"rc_X{d}", [P, NC_ + 1, P], F32)) for d in range(2)]
        tmp = st.enter_context(nc.sbuf_tensor("rc_tmp", [P, T_CTX], F32))
        turned, turn_cp, grams, masked, leveled = sem("turned"), sem("turn_copied"), sem("grams"), sem("masked"), sem("leveled")
        l0_turned, inv_ready, f_sum, f_copied, tz_sum = sem("l0_turned"), sem("inverse_ready"), sem("f_sum"), sem("f_copied"), sem("tz_sum")
        n1_sum, n1_cp, gu_sum, gu_cp, ph_sum, ph_ready = sem("n1_sum"), sem("n1_copied"), sem("gu_sum"), sem("gu_copied"), sem("ph_sum"), sem("ph_ready")
        x_sum, x_ready, y_sum, chain = sem("x_sum"), sem("x_ready"), sem("y_sum"), sem("chain")
        xinit = sem("x_init")
        ident = S.cst[:, C_ID:C_ID + P]
        order = [list(range(NC_)), list(range(NC_))[::-1]]

        def bank(d, b):
            return S.ps[:, 4 * d + b, :].rearrange("p (c n) -> p c n", n=P)

        def all_chunks(d, b, lhsT, rhs):
            for c in range(NC_):
                last = nc.tensor.matmul(bank(d, b)[:, c, :], lhsT[:, c, :], rhs[:, c, :], start=True, stop=True)
            return last

        with nc.Block() as block:
            @block.tensor
            def _(pe):
                for d in range(2):
                    src = [R.bd[d][:, BA], R.bd[d][:, BBB], R.bd[d][:, BKB]] + ([R.vbd[:, :]] if d == 0 else [])
                    for b, s in enumerate(src):
                        for c in range(NC_):
                            last = nc.tensor.transpose(bank(d, b)[:, c, :], s[:, c, :], ident)
                    last.then_inc(turned, 1)
                for d in range(2):
                    pe.wait_ge(turn_cp, d + 1)
                    all_chunks(d, 0, R.bd[d][:, BB], R.bd[d][:, BA])
                    all_chunks(d, 1, R.bd[d][:, BB], R.bd[d][:, BR])
                    all_chunks(d, 2, R.bd[d][:, BK], R.bd[d][:, BA])
                    all_chunks(d, 3, R.bd[d][:, BK], R.bd[d][:, BR]).then_inc(grams, 1)
                for d in range(2):
                    pe.wait_ge(masked, d + 1)
                    pe.wait_ge(leveled, d + 1)
                    for c in range(NC_):
                        last = nc.tensor.transpose(bank(d, 0)[:, c, :], M[d]["Et"][:, c, :], ident)
                    last.then_inc(l0_turned, 1)
                for n in range(1, 6):
                    for d in range(2):
                        pe.wait_ge(inv_ready, 2 * (n - 1) + d + 1)
                        pe.wait_ge(leveled, 2 * n + d + 1)
                        all_chunks(d, 1, M[d]["Et"], M[d]["Tm"]).then_inc(f_sum, 1)
                    for d in range(2):
                        pe.wait_ge(f_copied, 2 * (n - 1) + d + 1)
                        if n < 5:
                            all_chunks(d, 2, M[d]["Z"], M[d]["F"])
                        all_chunks(d, 3, M[d]["F"], M[d]["Z"]).then_inc(tz_sum, 1)
                for d in range(2):
                    all_chunks(d, 0, M[d]["AkT"], Vn).then_inc(n1_sum, 1)
                for d in range(2):
                    pe.wait_ge(inv_ready, 10 + d + 1)
                    pe.wait_ge(n1_cp, d + 1)
                    all_chunks(d, 1, M[d]["Z"], M[d]["An"])
                    all_chunks(d, 2, M[d]["Z"], M[d]["F"]).then_inc(gu_sum, 1)
                for d in range(2):
                    pe.wait_ge(gu_cp, d + 1)
                    all_chunks(d, 3, M[d]["G"], M[d]["Bn"])
                    all_chunks(d, 0, M[d]["G"], M[d]["MbT"]).then_inc(ph_sum, 1)
                for i in range(NC_):
                    for d in range(2):
                        c = order[d][i]
                        if i >= 2:
                            pe.wait_ge(x_ready, 2 * (i - 2) + d + 1)
                        o = bank(d, 1 + i % 2)[:, 0, :]
                        nc.tensor.matmul(o, M[d]["Bn"][:, c, :], M[d]["U0"][:, c, :], start=True, stop=False)
                        nc.tensor.matmul(o, M[d]["Kn"][:, c, :], Vn[:, c, :], start=False, stop=False)
                        if i == 0:
                            pe.wait_ge(ph_ready, d + 1)
                            pe.wait_ge(xinit, d + 1)
                        else:
                            pe.wait_ge(x_ready, 2 * (i - 1) + d + 1)
                        nc.tensor.matmul(o, M[d]["LT"][:, c, :], X[d][:, i, :], start=False, stop=True).then_inc(x_sum, 1)
                for d in range(2):
                    for i in range(NC_):
                        c = order[d][i]
                        o = bank(d, 3)[:, c, :]
                        nc.tensor.matmul(o, X[d][:, i, :], M[d]["Tm"][:, c, :], start=True, stop=False)
                        nc.tensor.matmul(o, M[d]["U0"][:, c, :], M[d]["MbT"][:, c, :], start=False, stop=False)
                        last = nc.tensor.matmul(o, Vn[:, c, :], M[d]["MkT"][:, c, :], start=False, stop=True)
                    last.then_inc(y_sum, 1)

            @block.scalar
            def _(act):
                for d in range(2):
                    nc.scalar.activation(X[d][:, 0, :], R.last[d][:, :], ACT.Copy).then_inc(xinit, 1)
                for d in range(2):
                    act.wait_ge(turned, d + 1)
                    nc.scalar.activation(M[d]["An"][:, :, :], bank(d, 0), ACT.Copy)
                    nc.scalar.activation(M[d]["Bn"][:, :, :], bank(d, 1), ACT.Copy)
                    last = nc.scalar.activation(M[d]["Kn"][:, :, :], bank(d, 2), ACT.Copy)
                    if d == 0:
                        last = nc.scalar.activation(Vn[:, :, :], bank(d, 3), ACT.Copy)
                    last.then_inc(turn_cp, 1)
                for n in range(1, 6):
                    for d in range(2):
                        act.wait_ge(f_sum, 2 * (n - 1) + d + 1)
                        nc.scalar.activation(M[d]["F"][:, :, :], bank(d, 1), ACT.Copy).then_inc(f_copied, 1)
                for d in range(2):
                    act.wait_ge(n1_sum, d + 1)
                    act.wait_ge(tz_sum, 8 + d + 1)
                    nc.scalar.activation(M[d]["F"][:, :, :], bank(d, 0), ACT.Copy).then_inc(n1_cp, 1)
                for d in range(2):
                    act.wait_ge(gu_sum, d + 1)
                    nc.scalar.activation(M[d]["G"][:, :, :], bank(d, 1), ACT.Copy)
                    nc.scalar.activation(M[d]["U0"][:, :, :], bank(d, 2), ACT.Copy).then_inc(gu_cp, 1)
                for i in range(NC_):
                    for d in range(2):
                        act.wait_ge(x_sum, 2 * i + d + 1)
                        nc.scalar.activation(X[d][:, i + 1, :], bank(d, 1 + i % 2)[:, 0, :], ACT.Copy).then_inc(x_ready, 1)
                act.wait_ge(x_ready, 2 * NC_)
                for d in range(2):
                    nc.scalar.activation(R.last[d][:, :], X[d][:, NC_, :], ACT.Copy)

            @block.gpsimd
            def _(pool):
                for n in range(6):
                    for d in range(2):
                        if n == 0:
                            pool.wait_ge(masked, d + 1)
                        elif n == 1:
                            pool.wait_ge(inv_ready, d + 1)
                        else:
                            pool.wait_ge(f_sum, 2 * (n - 2) + d + 1)
                        lvl = S.cst[:, C_LVL + n * P:C_LVL + (n + 1) * P].unsqueeze(1).to_broadcast([P, NC_, P])
                        nc.gpsimd.tensor_tensor(M[d]["Et"][:, :, :], M[d]["LT"][:, :, :], lvl, ALU.mult).then_inc(leveled, 1)

            @block.vector
            def _(dve):
                link = Link(dve, chain)
                idb = ident.unsqueeze(1).to_broadcast([P, NC_, P])
                for d in range(2):
                    dve.wait_ge(grams, d + 1)
                    for b, (m, inc) in enumerate((("LT", 0), ("MbT", 1), ("AkT", 0), ("MkT", 1))):
                        a = C_MASK + (2 * d + inc) * P
                        last = nc.vector.tensor_tensor(M[d][m][:, :, :], bank(d, b),
                                                       S.cst[:, a:a + P].unsqueeze(1).to_broadcast([P, NC_, P]), ALU.mult)
                    last.then_inc(masked, 1)
                for d in range(2):
                    dve.wait_ge(leveled, d + 1)
                    nc.vector.tensor_tensor(M[d]["Z"][:, :, :], M[d]["Et"][:, :, :], idb, ALU.add)
                    dve.wait_ge(l0_turned, d + 1)
                    nc.vector.tensor_tensor(M[d]["Tm"][:, :, :], bank(d, 0), idb, ALU.add).then_inc(inv_ready, 1)
                for n in range(1, 6):
                    for d in range(2):
                        dve.wait_ge(tz_sum, 2 * (n - 1) + d + 1)
                        dve.wait_ge(inv_ready, 2 * (n - 1) + d + 1)
                        if n < 5:
                            nc.vector.tensor_tensor(M[d]["Tm"][:, :, :], M[d]["Tm"][:, :, :], bank(d, 2), ALU.add)
                        nc.vector.tensor_tensor(M[d]["Z"][:, :, :], M[d]["Z"][:, :, :], bank(d, 3), ALU.add).then_inc(inv_ready, 1)
                for d in range(2):
                    dve.wait_ge(ph_sum, d + 1)
                    for c in range(NC_):
                        nc.vector.scalar_tensor_tensor(out=M[d]["LT"][:, c, :], in0=ident, scalar=R.wc[:, d, c:c + 1],
                                                       in1=bank(d, 3)[:, c, :], op0=ALU.mult, op1=ALU.add)
                    nc.vector.tensor_tensor(M[d]["Tm"][:, :, :], bank(d, 0), R.bd[d][:, BR], ALU.add).then_inc(ph_ready, 1)
                for d in range(2):
                    dve.wait_ge(y_sum, d + 1)
                    both = bank(d, 3).rearrange("p c (h t) -> p c t h", h=2)
                    dst = R.y[:, bass.ds(tok, T_CTX)].rearrange("p (c t) -> p c t", t=CH) if d == 0 else tmp[:, :].rearrange("p (c t) -> p c t", t=CH)
                    link(nc.vector.tensor_reduce(dst, both, AX.X, ALU.add))
                nc.vector.tensor_tensor(R.y[:, bass.ds(tok, T_CTX)], R.y[:, bass.ds(tok, T_CTX)], tmp[:, :], ALU.add)
        clear_block(nc, [turned, turn_cp, grams, masked, leveled, l0_turned, inv_ready, f_sum, f_copied, tz_sum, n1_sum, n1_cp,
                         gu_sum, gu_cp, ph_sum, ph_ready, x_sum, x_ready, y_sum, chain, xinit])


def rwkv_finish(nc, S, R, hp):
    with ExitStack() as st:
        sem = lambda m: st.enter_context(nc.semaphore("rf_" + m))
        sq = st.enter_context(nc.sbuf_tensor("rf_sq", [P, T], F32))
        meaned, centred, squared, vared, rooted, chain = sem("meaned"), sem("centred"), sem("squared"), sem("vared"), sem("rooted"), sem("chain")
        ones = S.cst[:, C_ONES:C_ONES + P]
        with nc.Block() as block:
            @block.tensor
            def _(pe):
                nc.tensor.matmul(S.ps[:, 0, :], ones, R.y[:, :], start=True, stop=True).then_inc(meaned, 1)
                pe.wait_ge(squared, 1)
                nc.tensor.matmul(S.ps[:, 1, :], ones, sq[:, :], start=True, stop=True).then_inc(vared, 1)

            @block.scalar
            def _(act):
                act.wait_ge(centred, 1)
                nc.scalar.activation(sq[:, :], R.y[:, :], ACT.Square).then_inc(squared, 1)
                act.wait_ge(centred, 2)
                nc.scalar.activation(sq[:, :], sq[:, :], ACT.Sqrt).then_inc(rooted, 1)

            @block.vector
            def _(dve):
                link = Link(dve, chain)
                dve.wait_ge(meaned, 1)
                nc.vector.scalar_tensor_tensor(out=R.y[:, :], in0=S.ps[:, 0, :], scalar=-1.0 / CH, in1=R.y[:, :],
                                               op0=ALU.mult, op1=ALU.add).then_inc(centred, 1)
                dve.wait_ge(vared, 1)
                nc.vector.tensor_scalar(sq[:, :], S.ps[:, 1, :], 1.0 / CH, 64e-5, ALU.mult, ALU.add).then_inc(centred, 1)
                dve.wait_ge(rooted, 1)
                link(nc.vector.reciprocal(sq[:, :], sq[:, :]))
                link(nc.vector.tensor_tensor(R.y[:, :], R.y[:, :], sq[:, :], ALU.mult))
                link(nc.vector.tensor_scalar(R.y[:, :], R.y[:, :], S.hcol[:, 16:17], S.hcol[:, 17:18], ALU.mult, ALU.add))
                link(nc.vector.tensor_tensor(R.y[:, :], R.y[:, :], R.bonus[:, :], ALU.add))
                nc.vector.tensor_tensor(S.oT[:, bass.ds(hp + HP, 1), :].rearrange("p o t -> p (o t)"), R.y[:, :], R.gate[:, :], ALU.mult)
        clear_block(nc, [meaned, centred, squared, vared, rooted, chain])


LN_EPS = 1e-5


def post_block(nc, g, S, l, n, blocks, project=None, load_h=False):
    blocks = list(blocks)
    with ExitStack() as st:
        sem = lambda m: st.enter_context(nc.semaphore(f"po{l}{n}_" + m))
        sb = lambda m, s: st.enter_context(nc.sbuf_tensor(f"po{l}{n}_" + m, s, F32))
        gate = sb("gate", [P, 2, D])
        lng, lnb, t_ = sb("ln_g", [P, D]), sb("ln_b", [P, D]), sb("t", [P, 2, D])
        stat, agg, rstd = sb("stat", [P, NB, 2, 6]), sb("agg", [P, NB, 2]), sb("rstd", [P, NB])
        wout = sb("w_out", [P, 2, KD, 512]) if project is not None else None
        hl, lnl, wl = sem("h_loaded"), sem("ln_loaded"), [sem("w_loaded0"), sem("w_loaded1")]
        gsum, gcp, proj, chain, vared, rooted, used, normed = (sem("gate_sum"), sem("gate_copied"), sem("projected"), sem("chain"),
                                                               sem("vared"), sem("rooted"), sem("used"), sem("normed"))
        gidx = 2 if n == 0 else 5
        sides = [0, 1] if blocks[0] == 0 else [1]
        with phase(nc, [hl, lnl, *wl, gsum, gcp, proj, chain, vared, rooted, used, normed]) as block:
            @block.sync
            def _(sp):
                if project is not None:
                    for hf in range(2):
                        sp.dma_start(wout[:, hf], project.rearrange("(k p) n -> p k n", p=P)[:, :, hf * 512:(hf + 1) * 512]).then_inc(wl[hf], 16)
                if load_h:
                    load_tokens(sp, g, S.h, hl)
                sp.dma_start(lng[:, :], g.ln_g[l, n:n + 1, :].to_broadcast([P, D])).then_inc(lnl, 16)
                sp.dma_start(lnb[:, :], g.ln_b[l, n:n + 1, :].to_broadcast([P, D])).then_inc(lnl, 16)

            @block.tensor
            def _(pe):
                for side in sides:
                    for k in range(KD):
                        col = S.mcol[:, l, 1 - side, gidx * KD + k:gidx * KD + k + 1]
                        last = nc.tensor.matmul(S.ps[:, 4 + 2 * side + k // 4, (k % 4) * P:(k % 4 + 1) * P],
                                                col.to_broadcast([P, P]), S.cst[:, C_ID:C_ID + P], start=True, stop=True)
                last.then_inc(gsum, 1)
                if project is not None:
                    pe.wait_ge(wl[0], 16)
                    pe.wait_ge(wl[1], 16)
                    for i, b in enumerate(blocks):
                        if i >= 2:
                            pe.wait_ge(used, i - 1)
                        for hf in range(2):
                            for k in range(KD):
                                last = nc.tensor.matmul(S.ps[:, 2 * (i % 2) + hf, :], S.oT[:, k, b * P:(b + 1) * P],
                                                        wout[:, hf, k, :], start=(k == 0), stop=(k == KD - 1))
                        last.then_inc(proj, 1)

            @block.scalar
            def _(act):
                act.wait_ge(gsum, 1)
                for side in sides:
                    nc.scalar.activation(gate[:, side, :].rearrange("p (a n) -> p a n", a=2),
                                         S.ps[:, 4 + 2 * side:6 + 2 * side, :], ACT.Copy).then_inc(gcp, 1)
                for i in range(len(blocks)):
                    act.wait_ge(vared, i + 1)
                    nc.scalar.activation(rstd[:, i:i + 1], agg[:, i, 1:2], ACT.Sqrt).then_inc(rooted, 1)

            @block.vector
            def _(dve):
                link = Link(dve, chain)
                dve.wait_ge(gcp, len(sides))
                if load_h:
                    dve.wait_ge(hl, 32)
                for i, b in enumerate(blocks):
                    t = t_[:, i % 2, :]
                    if project is not None:
                        dve.wait_ge(proj, i + 1)
                        y = S.ps[:, 2 * (i % 2):2 * (i % 2) + 2, :]
                    else:
                        y = S.acc[:, b, :].rearrange("p (a n) -> p a n", a=2)
                    nc.vector.tensor_tensor(t.rearrange("p (a n) -> p a n", a=2), y,
                                            gate[:, b // 2, :].rearrange("p (a n) -> p a n", a=2), ALU.mult).then_inc(used, 1)
                    dve.wait_ge(used, i + 1)
                    link(nc.vector.scalar_tensor_tensor(out=t, in0=S.h[:, b, :], scalar=ALPHA, in1=t, op0=ALU.mult, op1=ALU.add))
                    for a in range(2):
                        last = nc.vector.bn_stats(stat[:, i, a, :], t[:, a * 512:(a + 1) * 512])
                        link(last)
                    link(nc.vector.bn_aggr(agg[:, i, :], stat[:, i, :, :].rearrange("p a s -> p (a s)")))
                    nc.vector.tensor_scalar(agg[:, i, 1:2], agg[:, i, 1:2], LN_EPS, None, ALU.add).then_inc(vared, 1)
                    dve.wait_ge(rooted, i + 1)
                    link(nc.vector.reciprocal(rstd[:, i:i + 1], rstd[:, i:i + 1]))
                    nc.vector.tensor_scalar(S.h[:, b, :], t, agg[:, i, 0:1], rstd[:, i:i + 1], ALU.subtract, ALU.mult).then_inc(normed, 1)

            @block.gpsimd
            def _(pool):
                pool.wait_ge(lnl, 32)
                for i, b in enumerate(blocks):
                    pool.wait_ge(normed, i + 1)
                    nc.gpsimd.tensor_tensor(S.h[:, b, :], S.h[:, b, :], lng[:, :], ALU.mult).then_inc(hl, 1)
                    pool.wait_ge(hl, (32 if load_h else 0) + i + 1)
                    nc.gpsimd.tensor_tensor(S.h[:, b, :], S.h[:, b, :], lnb[:, :], ALU.add)


def router_block(nc, g, S, l, blocks):
    blocks = list(blocks)
    nb = len(blocks)
    with ExitStack() as st:
        sem = lambda m: st.enter_context(nc.semaphore(f"ro{l}_" + m))
        sb = lambda m, s: st.enter_context(nc.sbuf_tensor(f"ro{l}_" + m, s, F32))
        s_, sel, pair, cmp_, rank = (sb("s", [P, nb, 4, 4]), sb("sel", [P, nb, 4, 4]), sb("pair", [P, nb, 4]), sb("cmp", [P, nb, 4, 4]),
                                     sb("rank", [P, nb, 4, 4]))
        top, grank, gcmp, tot = sb("top", [P, nb, 4]), sb("grank", [P, nb, 4]), sb("gcmp", [P, nb, 4]), sb("tot", [P, nb])
        chosen, most = sb("chosen", [P, nb, N_EXP]), sb("most", [P, 3 + N_ITEM])
        cnt, mine, at, tmp = sb("counts", [P, 3, N_EXP]), sb("mine", [P, N_ITEM, N_EXP]), sb("at", [P, N_ITEM, N_EXP]), sb("tmp", [P, N_ITEM, N_EXP])
        scored, sgm, chain, picked, counted = sem("scored"), sem("sigmoided"), sem("chain"), sem("picked"), sem("counted")
        block = st.enter_context(phase(nc, [scored, sgm, chain, picked, counted]))

        @block.tensor
        def _(pe):
            for i, b in enumerate(blocks):
                for k in range(KD):
                    last = nc.tensor.matmul(S.ps[:, 0, i * N_EXP:(i + 1) * N_EXP], S.uT[:, k, b * P:(b + 1) * P], S.router[:, k, :],
                                            start=(k == 0), stop=(k == KD - 1))
            last.then_inc(scored, 1)
            pe.wait_ge(picked, 1)
            for i in range(nb):
                for j in range(i + 1):
                    m = C_TRI if j == i else C_ALL
                    nc.tensor.matmul(S.ps[:, 1, i * N_EXP:(i + 1) * N_EXP], S.cst[:, m:m + P], chosen[:, j, :], start=(j == 0), stop=(j == i))
            for j in range(nb):
                last = nc.tensor.matmul(S.ps[:, 2, 0:N_EXP], S.cst[:, C_ALL:C_ALL + P], chosen[:, j, :], start=(j == 0), stop=(j == nb - 1))
            last.then_inc(counted, 1)

        @block.scalar
        def _(act):
            act.wait_ge(scored, 1)
            nc.scalar.activation(s_[:, :, :, :], S.ps[:, 0, 0:nb * N_EXP].rearrange("p (b g e) -> p b g e", g=4, e=4),
                                 ACT.Sigmoid).then_inc(sgm, 1)

        @block.vector
        def _(dve):
            link = Link(dve, chain)
            dve.wait_ge(sgm, 1)
            flat = lambda t: t[:, :, :, :].rearrange("p b g e -> p b (g e)")
            link(nc.vector.tensor_tensor(flat(sel), flat(s_), S.rbias[:, :].unsqueeze(1).to_broadcast([P, nb, N_EXP]), ALU.add))
            first = True
            for i in range(4):
                for j in range(i + 1, 4):
                    o = top if first else pair
                    link(nc.vector.tensor_tensor(o[:, :, :], sel[:, :, :, i], sel[:, :, :, j], ALU.add))
                    if not first:
                        link(nc.vector.tensor_tensor(top[:, :, :], top[:, :, :], pair[:, :, :], ALU.max))
                    first = False
            link(nc.vector.memset(grank[:, :, :], 0.0))
            link(nc.vector.memset(rank[:, :, :, :], 0.0))
            for j in range(4):
                for lo, hi, op in ((0, j, ALU.is_gt), (j + 1, 4, ALU.is_ge)):
                    if hi > lo:
                        w = hi - lo
                        link(nc.vector.tensor_tensor(gcmp[:, :, lo:hi], top[:, :, j:j + 1].to_broadcast([P, nb, w]), top[:, :, lo:hi], op))
                        link(nc.vector.tensor_tensor(grank[:, :, lo:hi], grank[:, :, lo:hi], gcmp[:, :, lo:hi], ALU.add))
                        link(nc.vector.tensor_tensor(cmp_[:, :, :, lo:hi], sel[:, :, :, j:j + 1].to_broadcast([P, nb, 4, w]),
                                                     sel[:, :, :, lo:hi], op))
                        link(nc.vector.tensor_tensor(rank[:, :, :, lo:hi], rank[:, :, :, lo:hi], cmp_[:, :, :, lo:hi], ALU.add))
            link(nc.vector.tensor_scalar(grank[:, :, :], grank[:, :, :], 0.5, None, ALU.is_lt))
            link(nc.vector.tensor_scalar(rank[:, :, :, :], rank[:, :, :, :], 1.5, None, ALU.is_lt))
            link(nc.vector.tensor_tensor(rank[:, :, :, :], rank[:, :, :, :], grank[:, :, :].unsqueeze(3).to_broadcast([P, nb, 4, 4]), ALU.mult))
            nc.vector.tensor_copy(chosen[:, :, :], flat(rank)).then_inc(picked, 1)
            dve.wait_ge(picked, 1)
            link(nc.vector.tensor_tensor(flat(rank), flat(rank), flat(s_), ALU.mult))
            link(nc.vector.tensor_reduce(tot[:, :], flat(rank), AX.X, ALU.add))
            link(nc.vector.reciprocal(tot[:, :], tot[:, :]))
            nc.vector.tensor_tensor(S.combine[:, blocks[0]:blocks[-1] + 1, :], flat(rank), tot[:, :].unsqueeze(2).to_broadcast([P, nb, N_EXP]), ALU.mult)
            dve.wait_ge(counted, 1)
            place = S.place[:, blocks[0]:blocks[-1] + 1, :]
            link(nc.vector.scalar_tensor_tensor(out=place, in0=S.ps[:, 1, 0:nb * N_EXP].rearrange("p (b e) -> p b e", b=nb), scalar=1.0,
                                                in1=chosen[:, :, :], op0=ALU.add, op1=ALU.mult))
            link(nc.vector.tensor_scalar(place, place, -1.0, None, ALU.add))
            n_, first_, last_ = cnt[:, 0, :], cnt[:, 1, :], cnt[:, 2, :]
            link(nc.vector.tensor_scalar(n_, S.ps[:, 2, 0:N_EXP], 0.5, None, ALU.is_gt))
            for r in range(1, nb):
                link(nc.vector.tensor_scalar(first_, S.ps[:, 2, 0:N_EXP], r * P + 0.5, None, ALU.is_gt))
                link(nc.vector.tensor_tensor(n_, n_, first_, ALU.add))
            link(nc.vector.tensor_tensor_scan(last_, S.cst[:, C_ALL:C_ALL + N_EXP], n_, 0.0, ALU.mult, ALU.add))
            link(nc.vector.tensor_tensor(first_, last_, n_, ALU.subtract))
            jj = S.cst[:, C_JIDX:C_JIDX + N_ITEM].unsqueeze(2).to_broadcast([P, N_ITEM, N_EXP])
            row = lambda t: t.unsqueeze(1).to_broadcast([P, N_ITEM, N_EXP])
            link(nc.vector.tensor_tensor(mine[:, :, :], jj, row(last_), ALU.is_lt))
            link(nc.vector.tensor_tensor(at[:, :, :], jj, row(first_), ALU.is_ge))
            link(nc.vector.tensor_tensor(mine[:, :, :], mine[:, :, :], at[:, :, :], ALU.mult))
            link(nc.vector.tensor_tensor(at[:, :, :], jj, row(first_), ALU.subtract))
            link(nc.vector.tensor_scalar(at[:, :, :], at[:, :, :], float(-P), 1.0, ALU.mult, ALU.add))
            for i, b in enumerate(blocks):
                link(nc.vector.tensor_tensor(tmp[:, :, :], at[:, :, :], row(S.place[:, b, :]), ALU.add))
                link(nc.vector.tensor_tensor(tmp[:, :, :], tmp[:, :, :], mine[:, :, :], ALU.mult))
                link(nc.vector.tensor_reduce(S.item_place[:, b, :], tmp[:, :, :], AX.X, ALU.add))
                link(nc.vector.tensor_tensor(tmp[:, :, :], mine[:, :, :], row(S.combine[:, b, :]), ALU.mult))
                link(nc.vector.tensor_reduce(S.item_gate[:, b, :], tmp[:, :, :], AX.X, ALU.add))
            link(nc.vector.tensor_scalar(S.item_place[:, blocks[0]:, :], S.item_place[:, blocks[0]:, :], -1.0, None, ALU.add))
            link(nc.vector.tensor_tensor(tmp[:, :, :], mine[:, :, :], row(S.cst[:, C_EIDX:C_EIDX + N_EXP]), ALU.mult))
            link(nc.vector.tensor_reduce(most[:, 3:3 + N_ITEM], tmp[:, :, :], AX.X, ALU.add))
            nc.vector.tensor_copy(S.item_expert[:, :], most[:, 3:3 + N_ITEM])
            link(nc.vector.memset(most[:, 1:2], 1.0))
            for r in range(1, (N_ITEM - 2) // 2):
                link(nc.vector.tensor_scalar(most[:, 2:3], cnt[:, 2, N_EXP - 1:N_EXP], 2 * r + 0.5, None, ALU.is_gt))
                link(nc.vector.tensor_tensor(most[:, 1:2], most[:, 1:2], most[:, 2:3], ALU.add))
            nc.vector.tensor_copy(S.pairs[:, :], most[:, 1:2])


def token_major_block(nc, S, l, blocks):
    blocks = list(blocks)
    with ExitStack() as st:
        turned, copied = [st.enter_context(nc.semaphore(f"tm{l}_{m}")) for m in ("turned", "copied")]
        block = st.enter_context(phase(nc, [turned, copied]))
        jobs = [(b, k4) for b in blocks for k4 in range(KD // 4)]

        @block.tensor
        def _(pe):
            for j, (b, k4) in enumerate(jobs):
                if j >= 4:
                    pe.wait_ge(copied, j - 3)
                for k in range(4):
                    last = nc.tensor.transpose(S.ps[:, j % 4, k * P:(k + 1) * P], S.uT[:, k4 * 4 + k, b * P:(b + 1) * P],
                                               S.cst[:, C_ID:C_ID + P])
                last.then_inc(turned, 1)

        @block.scalar
        def _(act):
            for j, (b, k4) in enumerate(jobs):
                act.wait_ge(turned, j + 1)
                nc.scalar.activation(S.uN[:, b, k4 * 512:(k4 + 1) * 512], S.ps[:, j % 4, :], ACT.Copy).then_inc(copied, 1)

        @block.gpsimd
        def _(pool):
            nc.gpsimd.memset(S.acc[:, blocks[0]:, :], 0.0)


def moe(nc, g, S, l, blocks):
    blocks = list(blocks)
    nb = len(blocks)
    no = 2 * nb
    FC = D_EXP // P
    with ExitStack() as st:
        sem = lambda m: st.enter_context(nc.semaphore(f"mo{l}_" + m))
        sb = lambda m, s: st.enter_context(nc.sbuf_tensor(f"mo{l}_" + m, s, F32))
        wg, wu, wd = sb("w_gate", [P, 2, KD, D_EXP]), sb("w_up", [P, 2, KD, D_EXP]), sb("w_down", [P, 2, FC, D])
        pick, pickg, scat = sb("pick", [P, nb, P]), sb("pick_gated", [P, nb, P]), sb("scatter", [P, 2, nb, P])
        xN, xT, he, heT, sg, y = sb("xN", [P, D]), sb("xT", [P, KD, P]), sb("he", [P, D_EXP]), sb("heT", [P, FC, P]), sb("silu", [P, D_EXP]), sb("y", [P, D])
        pl, cb = sb("place_now", [P, NB, 2]), sb("gate_now", [P, NB, 2])
        gfull, dfull = [sem(f"gate_up_full{x}") for x in range(2)], [sem(f"down_full{x}") for x in range(2)]
        names = ["cols_ready", "pick_ready", "scat_ready", "scat_copied", "x_ready", "x_copied", "xt_ready", "xt_copied", "gate_ready", "up_ready",
                 "silu_done", "he_done", "het_ready", "het_copied", "y_ready", "y_copied", "out_ready", "acc_done"]
        sems = [sem(m) for m in names]
        (cols_ready, pick_ready, scat_ready, scat_copied, x_ready, x_copied, xt_ready, xt_copied, gate_ready, up_ready,
         silu_done, he_done, het_ready, het_copied, y_ready, y_copied, out_ready, acc_done) = sems
        ident = S.cst[:, C_ID:C_ID + P]
        src = [w[l].rearrange("e (k p) n -> e p k n", p=P) for w in (g.exp_w_gate, g.exp_w_up, g.exp_w_down)]

        def load_gate_up(eng, x, e):
            for w, dst in ((0, wg), (1, wu)):
                eng.dma_start(dst[:, x], src[w][bass.ds(e, 1)].rearrange("o p k n -> p (o k) n")).then_inc(gfull[x], 16)

        def load_down(eng, x, e):
            eng.dma_start(wd[:, x], src[2][bass.ds(e, 1)].rearrange("o p k n -> p (o k) n")).then_inc(dfull[x], 16)

        def expert_of(eng, item):
            return eng.value_load(S.item_expert[0:1, bass.ds(item, 1)], min_val=0, max_val=N_EXP - 1)

        def gather(pe, n):
            pe.wait_ge(pick_ready, n + 1)
            for i in range(nb):
                last = nc.tensor.transpose(S.ps[:, 5, i * P:(i + 1) * P], pickg[:, i, :], ident)
            last.then_inc(scat_ready, 1)
            for hf in range(2):
                for i, b in enumerate(blocks):
                    last = nc.tensor.matmul(S.ps[:, 2 + hf, :], pick[:, i, :], S.uN[:, b, hf * 512:(hf + 1) * 512],
                                            start=(i == 0), stop=(i == nb - 1))
                last.then_inc(x_ready, 1)

        def turn_x(pe, n):
            for hf in range(2):
                pe.wait_ge(x_copied, 2 * n + hf + 1)
                for k in range(4):
                    last = nc.tensor.transpose(S.ps[:, 2 + hf, k * P:(k + 1) * P], xN[:, (4 * hf + k) * P:(4 * hf + k + 1) * P], ident)
                last.then_inc(xt_ready, 1)

        def scatter(pe, n, buf):
            if n:
                pe.wait_ge(y_copied, 2 * n)
                pe.wait_ge(scat_copied, n)
            for i in range(nb):
                for hf in range(2):
                    j = 2 * i + hf
                    if j >= 4:
                        pe.wait_ge(acc_done, no * n + j - 3)
                    nc.tensor.matmul(S.ps[:, 2 + j % 4, :], scat[:, buf, i, :], y[:, hf * 512:(hf + 1) * 512],
                                     start=True, stop=True).then_inc(out_ready, 1)

        def take_x(act, n, buf, busy):
            act.wait_ge(scat_ready, n + 1)
            if busy:
                act.wait_ge(out_ready, no * (n + 1))
            nc.scalar.activation(scat[:, buf, :, :], S.ps[:, 5, 0:nb * P].rearrange("p (b t) -> p b t", t=P), ACT.Copy).then_inc(scat_copied, 1)
            for hf in range(2):
                act.wait_ge(x_ready, 2 * n + hf + 1)
                if n:
                    act.wait_ge(xt_ready, 2 * n)
                nc.scalar.activation(xN[:, hf * 512:(hf + 1) * 512], S.ps[:, 2 + hf, :], ACT.Copy).then_inc(x_copied, 1)

        def take_xt(act, n, busy):
            for hf in range(2):
                act.wait_ge(xt_ready, 2 * n + hf + 1)
                if busy:
                    act.wait_ge(up_ready, n + 1)
                nc.scalar.activation(xT[:, 4 * hf:4 * hf + 4, :], S.ps[:, 2 + hf, :].rearrange("p (k t) -> p k t", t=P), ACT.Copy).then_inc(xt_copied, 1)

        def picks(dve, n):
            if n:
                dve.wait_ge(x_ready, 2 * n)
            iota = S.cst[:, C_IOTA:C_IOTA + P]
            for i, b in enumerate(blocks):
                nc.vector.tensor_scalar(pick[:, i, :], iota, pl[:, b, n:n + 1], None, ALU.is_equal)
                last = nc.vector.tensor_scalar(pickg[:, i, :], iota, pl[:, b, n:n + 1], cb[:, b, n:n + 1], ALU.is_equal, ALU.mult)
            last.then_inc(pick_ready, 1)

        def columns(dve, item, n):
            nc.vector.tensor_copy(pl[:, :, 0:n], S.item_place[:, :, bass.ds(item, n)]).then_inc(cols_ready, 1)
            nc.vector.tensor_copy(cb[:, :, 0:n], S.item_gate[:, :, bass.ds(item, n)]).then_inc(cols_ready, 1)
            dve.wait_ge(cols_ready, 2)

        def accumulate(dve, n):
            if n:
                dve.wait_ge(acc_done, no * n)
            for i, b in enumerate(blocks):
                for hf in range(2):
                    j = 2 * i + hf
                    dve.wait_ge(out_ready, no * n + j + 1)
                    a = S.acc[:, b, hf * 512:(hf + 1) * 512]
                    nc.vector.tensor_tensor(a, a, S.ps[:, 2 + j % 4, :], ALU.add).then_inc(acc_done, 1)

        with phase(nc, sems) as block:
            @block.sync
            def _(sp):
                for x in range(2):
                    e = expert_of(sp, x)
                    load_gate_up(sp, x, e)
                    load_down(sp, x, e)

            @block.gpsimd
            def _(pool):
                nc.gpsimd.memset(y[:, :], 0.0)
                nc.gpsimd.memset(scat[:, 1, :, :], 0.0)

            @block.vector
            def _(dve):
                columns(dve, 0, 1)
                picks(dve, 0)

            @block.tensor
            def _(pe):
                gather(pe, 0)
                turn_x(pe, 0)

            @block.scalar
            def _(act):
                take_x(act, 0, 0, False)
                take_xt(act, 0, False)

        pairs = nc.values_load(S.pairs[0:1, 0:1], min_val=1, max_val=(N_ITEM - 2) // 2)
        with nc.Fori(0, pairs) as it:
            with phase(nc, sems) as block:
                @block.sync
                def _(sp):
                    for x in range(2):
                        e = expert_of(sp, it * 2 + (x + 2))
                        sp.wait_ge(up_ready, x + 1)
                        sp.sem_clear(gfull[x])
                        load_gate_up(sp, x, e)
                        sp.wait_ge(y_ready, 2 * (x + 1))
                        sp.sem_clear(dfull[x])
                        load_down(sp, x, e)

                @block.tensor
                def _(pe):
                    for x in range(2):
                        pe.wait_ge(gfull[x], 32)
                        if x:
                            pe.wait_ge(xt_copied, 2 * x)
                        for bank, w, rdy in ((0, wg, gate_ready), (1, wu, up_ready)):
                            for k in range(KD):
                                last = nc.tensor.matmul(S.ps[:, bank, :], xT[:, k, :], w[:, x, k, :], start=(k == 0), stop=(k == KD - 1))
                            last.then_inc(rdy, 1)
                        scatter(pe, x, (x + 1) % 2)
                        pe.wait_ge(acc_done, no * (x + 1))
                        gather(pe, x)
                        pe.wait_ge(he_done, x + 1)
                        for f in range(FC):
                            last = nc.tensor.transpose(S.ps[:, 4, f * P:(f + 1) * P], he[:, f * P:(f + 1) * P], ident)
                        last.then_inc(het_ready, 1)
                        turn_x(pe, x)
                        pe.wait_ge(het_copied, x + 1)
                        pe.wait_ge(dfull[x], 16)
                        for hf in range(2):
                            for f in range(FC):
                                last = nc.tensor.matmul(S.ps[:, 6 + hf, :], heT[:, f, :], wd[:, x, f, hf * 512:(hf + 1) * 512],
                                                        start=(f == 0), stop=(f == FC - 1))
                            last.then_inc(y_ready, 1)

                @block.scalar
                def _(act):
                    for x in range(2):
                        act.wait_ge(gate_ready, x + 1)
                        if x:
                            act.wait_ge(he_done, x)
                        nc.scalar.activation(sg[:, :], S.ps[:, 0, :], ACT.Silu).then_inc(silu_done, 1)
                        take_x(act, x, (x + 1) % 2, True)
                        act.wait_ge(het_ready, x + 1)
                        if x:
                            act.wait_ge(y_ready, 2 * x)
                        nc.scalar.activation(heT[:, :, :], S.ps[:, 4, :].rearrange("p (f t) -> p f t", t=P), ACT.Copy).then_inc(het_copied, 1)
                        take_xt(act, x, True)
                        for hf in range(2):
                            act.wait_ge(y_ready, 2 * x + hf + 1)
                            act.wait_ge(out_ready, no * (x + 1))
                            nc.scalar.activation(y[:, hf * 512:(hf + 1) * 512], S.ps[:, 6 + hf, :], ACT.Copy).then_inc(y_copied, 1)

                @block.vector
                def _(dve):
                    columns(dve, it * 2 + 1, 2)
                    for x in range(2):
                        picks(dve, x)
                        dve.wait_ge(silu_done, x + 1)
                        dve.wait_ge(up_ready, x + 1)
                        if x:
                            dve.wait_ge(het_ready, x)
                        nc.vector.tensor_tensor(he[:, :], sg[:, :], S.ps[:, 1, :], ALU.mult).then_inc(he_done, 1)
                        accumulate(dve, x)

        with phase(nc, sems) as block:
            @block.tensor
            def _(pe):
                scatter(pe, 0, 1)

            @block.vector
            def _(dve):
                accumulate(dve, 0)

            @block.sync
            def _(sp):
                for x in range(2):
                    sp.wait_ge(gfull[x], 32)
                    sp.wait_ge(dfull[x], 16)
        clear_block(nc, gfull + dfull)


def odd_mixer(nc, g, S, l):
    n = T_LAT
    with ExitStack() as st:
        sem = lambda m: st.enter_context(nc.semaphore("da_" + m))
        sb = lambda m, s: st.enter_context(nc.sbuf_tensor("da_" + m, s, F32))
        slab, rope = sb("slab", [P, 3, KD, P]), sb("rope", [P, 2, n])
        lvec, lprod, lam, subln = sb("lambda_vectors", [P, 4, HD]), sb("lprod", [P, HD]), sb("lam", [P, 4]), sb("subln", [P, P])
        qraw, kraw, q, k, v = sb("qraw", [P, n]), sb("kraw", [P, T]), sb("q", [P, n]), sb("k", [P, T]), sb("v", [P, NB, P])
        rt = sb("rotated", [P, 2, n])
        p_, a_, aT, o_ = sb("p", [P, 2, 2, T]), sb("a", [P, 2, T]), sb("aT", [P, 2, NB, P]), sb("o", [P, 2, P])
        junk = sb("junk", [P, P])
        nmax, ssum, rsum, ss, rt_, inv = sb("nmax", [P, 4]), sb("ssum", [P, 4]), sb("rsum", [P, 4]), sb("ss", [P, 2]), sb("root", [P, 2]), sb("inv", [P, 2])
        full = sem("slab_full")
        src = g.odd_w_in[0].rearrange("(k p) n -> p k n", p=P)

        def load(sp, h):
            for j in range(3):
                sp.dma_start(slab[:, j], src[:, :, bass.ds(h * P + j * 2 * DA_H * HD, P)]).then_inc(full, 16)

        once, summed_l, exped_l, ch0 = sem("once"), sem("lambda_sums"), sem("lambda_exps"), sem("lchain")
        with nc.Block() as block:
            @block.sync
            def _(sp):
                load(sp, 0)
                sp.dma_start(rope[:, :, :], g.rope.rearrange("p (a t) -> p a t", a=2)).then_inc(once, 16)
                for i, x in enumerate((g.da_lq1, g.da_lk1, g.da_lq2, g.da_lk2)):
                    sp.dma_start(lvec[:, i, :], x[0:1, :].to_broadcast([P, HD])).then_inc(once, 16)
                sp.dma_start(subln[:, :], g.da_subln_g[0:1, :].to_broadcast([P, P])).then_inc(once, 16)

            @block.vector
            def _(dve):
                link = Link(dve, ch0)
                dve.wait_ge(once, 16 * 6)
                for i in range(2):
                    link(nc.vector.tensor_tensor(lprod[:, :], lvec[:, 2 * i, :], lvec[:, 2 * i + 1, :], ALU.mult))
                    nc.vector.tensor_reduce(lam[:, i:i + 1], lprod[:, :], AX.X, ALU.add).then_inc(summed_l, 1)
                    dve.wait_ge(summed_l, i + 1)
                link(nc.vector.tensor_scalar(subln[:, :], subln[:, :], 2.0 * (1.0 - LAMBDA_INIT), None, ALU.mult))
                dve.wait_ge(exped_l, 1)
                link(nc.vector.tensor_tensor(lam[:, 2:3], lam[:, 0:1], lam[:, 1:2], ALU.subtract))
                link(nc.vector.tensor_scalar(lam[:, 3:4], lam[:, 2:3], LAMBDA_INIT, None, ALU.add))

            @block.scalar
            def _(act):
                act.wait_ge(summed_l, 2)
                nc.scalar.activation(lam[:, 0:2], lam[:, 0:2], ACT.Exp).then_inc(exped_l, 1)

        clear_block(nc, [once, summed_l, exped_l, ch0])
        names = ["ready", "raw", "turned", "mixed", "staged", "scored", "maxed", "exped", "diffed", "a_turned", "a_copied", "summed",
                 "squared", "scaled", "rooted", "normed", "o_turned", "chain"]
        (ready, raw, turned, mixed, staged, scored, maxed, exped, diffed, a_turned, a_copied, summed, squared, scaled, rooted,
         normed, o_turned, chain) = [sem(m) for m in names]
        ident = S.cst[:, C_ID:C_ID + P]

        def body(h, prefetch):
            with nc.Block() as block:
                @block.sync
                def _(sp):
                    sp.wait_ge(ready, 3)
                    sp.sem_clear(full)
                    if prefetch:
                        load(sp, h + 1)

                @block.tensor
                def _(pe):
                    pe.wait_ge(full, 16 * 3)
                    for kk in range(KD):
                        last = nc.tensor.matmul(S.ps[:, 0, 0:n], slab[:, 0, kk, :], S.uT[:, kk, T_CTX:T], start=(kk == 0), stop=(kk == KD - 1))
                    last.then_inc(ready, 1)
                    for kk in range(KD):
                        last = nc.tensor.matmul(S.ps[:, 1, :], slab[:, 1, kk, :], S.uT[:, kk, :], start=(kk == 0), stop=(kk == KD - 1))
                    last.then_inc(ready, 1)
                    for b in range(NB):
                        for kk in range(KD):
                            last = nc.tensor.matmul(S.ps[:, 2, b * P:(b + 1) * P], S.uT[:, kk, b * P:(b + 1) * P], slab[:, 2, kk, :],
                                                    start=(kk == 0), stop=(kk == KD - 1))
                    last.then_inc(ready, 1)
                    rot = S.cst[:, C_ROT:C_ROT + P]
                    pe.wait_ge(raw, 1)
                    nc.tensor.matmul(S.ps[:, 3, 0:n], rot, qraw[:, :], start=True, stop=True).then_inc(turned, 1)
                    pe.wait_ge(raw, 2)
                    nc.tensor.matmul(S.ps[:, 4, 0:n], rot, kraw[:, T_CTX:T], start=True, stop=True).then_inc(turned, 1)
                    pe.wait_ge(staged, 1)
                    pe.wait_ge(mixed, 2)
                    for u in range(2):
                        for m in range(2):
                            nc.tensor.matmul(S.ps[:, 2 * u + m, :], q[m * HD:(m + 1) * HD, u * P:(u + 1) * P], k[m * HD:(m + 1) * HD, :],
                                             start=True, stop=True).then_inc(scored, 1)
                    for u in range(2):
                        pe.wait_ge(diffed, u + 1)
                        for b in range(NB):
                            last = nc.tensor.transpose(S.ps[:, 4 + u, b * P:(b + 1) * P], a_[:, u, b * P:(b + 1) * P], ident)
                        last.then_inc(a_turned, 1)
                    for u in range(2):
                        pe.wait_ge(a_copied, u + 1)
                        for b in range(NB):
                            last = nc.tensor.matmul(S.ps[:, 6 + u, 0:P], aT[:, u, b, :], v[:, b, :], start=(b == 0), stop=(b == NB - 1))
                        last.then_inc(summed, 1)
                    for u in range(2):
                        pe.wait_ge(normed, u + 1)
                        nc.tensor.transpose(S.ps[:, 4 + u, 0:P], o_[:, u, :], ident).then_inc(o_turned, 1)

                @block.scalar
                def _(act):
                    act.wait_ge(ready, 1)
                    nc.scalar.activation(qraw[:, :], S.ps[:, 0, 0:n], ACT.Copy).then_inc(raw, 1)
                    act.wait_ge(ready, 2)
                    nc.scalar.activation(kraw[:, :], S.ps[:, 1, :], ACT.Copy).then_inc(raw, 1)
                    act.wait_ge(ready, 3)
                    nc.scalar.activation(v[:, :, :], S.ps[:, 2, :].rearrange("p (b e) -> p b e", b=NB), ACT.Copy).then_inc(staged, 1)
                    for j in range(4):
                        act.wait_ge(maxed, j + 1)
                        nc.scalar.activation(p_[:, j // 2, j % 2, :], S.ps[:, j, :], ACT.Exp, bias=nmax[:, j:j + 1], scale=NA_SCALE,
                                             accum_out=ssum[:, j:j + 1]).then_inc(exped, 1)
                    for u in range(2):
                        act.wait_ge(a_turned, u + 1)
                        nc.scalar.activation(aT[:, u, :, :], S.ps[:, 4 + u, :].rearrange("p (b q) -> p b q", b=NB), ACT.Copy).then_inc(a_copied, 1)
                    for u in range(2):
                        act.wait_ge(summed, u + 1)
                        if u:
                            act.wait_ge(squared, 1)
                        nc.scalar.activation(junk[:, :], S.ps[:, 6 + u, 0:P], ACT.Square, accum_out=ss[:, u:u + 1]).then_inc(squared, 1)
                        act.wait_ge(scaled, u + 1)
                        nc.scalar.activation(rt_[:, u:u + 1], ss[:, u:u + 1], ACT.Sqrt).then_inc(rooted, 1)
                    for u in range(2):
                        act.wait_ge(o_turned, u + 1)
                        nc.scalar.activation(S.oT[:, bass.ds(h, 1), T_CTX + u * P:T_CTX + (u + 1) * P].rearrange("p o t -> p (o t)"),
                                             S.ps[:, 4 + u, 0:P], ACT.Copy)

                @block.vector
                def _(dve):
                    link = Link(dve, chain)
                    for i, (r, t, out) in enumerate(((qraw[:, :], 0, q[:, :]), (kraw[:, T_CTX:T], 1, k[:, T_CTX:T]))):
                        dve.wait_ge(turned, i + 1)
                        if i:
                            nc.vector.tensor_copy(k[:, 0:T_CTX], kraw[:, 0:T_CTX])
                        nc.vector.tensor_tensor(rt[:, t, :], S.ps[:, 3 + i, 0:n], rope[:, 1, :], ALU.mult)
                        link(nc.vector.tensor_tensor(out, r, rope[:, 0, :], ALU.mult))
                        nc.vector.tensor_tensor(out, out, rt[:, t, :], ALU.add).then_inc(mixed, 1)
                    for j in range(4):
                        dve.wait_ge(scored, j + 1)
                        link(nc.vector.tensor_reduce(nmax[:, j:j + 1], S.ps[:, j, :], AX.X, ALU.max, negate=True))
                        nc.vector.tensor_scalar(nmax[:, j:j + 1], nmax[:, j:j + 1], NA_SCALE, None, ALU.mult).then_inc(maxed, 1)
                    for u in range(2):
                        dve.wait_ge(exped, 2 * u + 2)
                        link(nc.vector.reciprocal(rsum[:, 2 * u:2 * u + 2], ssum[:, 2 * u:2 * u + 2]))
                        link(nc.vector.tensor_scalar(rsum[:, 2 * u + 1:2 * u + 2], rsum[:, 2 * u + 1:2 * u + 2], lam[:, 3:4], None, ALU.mult))
                        link(nc.vector.tensor_scalar(p_[:, u, 1, :], p_[:, u, 1, :], rsum[:, 2 * u + 1:2 * u + 2], None, ALU.mult))
                        nc.vector.scalar_tensor_tensor(out=a_[:, u, :], in0=p_[:, u, 0, :], scalar=rsum[:, 2 * u:2 * u + 1], in1=p_[:, u, 1, :],
                                                       op0=ALU.mult, op1=ALU.subtract).then_inc(diffed, 1)
                    for u in range(2):
                        dve.wait_ge(squared, u + 1)
                        nc.vector.tensor_scalar(ss[:, u:u + 1], ss[:, u:u + 1], 1.0 / P, 1e-5, ALU.mult, ALU.add).then_inc(scaled, 1)
                        dve.wait_ge(rooted, u + 1)
                        r_, i_ = rt_[:, u:u + 1], inv[:, u:u + 1]
                        link(nc.vector.reciprocal(i_, r_))
                        link(nc.vector.scalar_tensor_tensor(out=r_, in0=i_, scalar=ss[:, u:u + 1], in1=r_, op0=ALU.mult, op1=ALU.add))
                        link(nc.vector.reciprocal(i_, r_))
                        nc.vector.scalar_tensor_tensor(out=o_[:, u, :], in0=S.ps[:, 6 + u, 0:P], scalar=i_, in1=subln[:, :],
                                                       op0=ALU.mult, op1=ALU.mult).then_inc(normed, 1)
            clear_block(nc, [ready, raw, turned, mixed, staged, scored, maxed, exped, diffed, a_turned, a_copied, summed, squared,
                             scaled, rooted, normed, o_turned, chain])

        with nc.Fori(0, DA_H - 1) as h:
            body(h, True)
        body(DA_H - 1, False)


def even_mixer(nc, g, S, sb, ctx):
    S.slab_full = ctx.enter_context(nc.semaphore("pair_slabs_full"))
    S.wall_full = ctx.enter_context(nc.semaphore("lora_weights_full"))
    S.xlora, S.wall, S.wst, S.wslab = sb("xlora", [P, 2, T]), sb("lora_w", [P, 5, W_NA]), sb("lora_w_pair", [P, 5, P]), sb("pair_slabs", [P, 6, KD, P])
    S.reset, S.hcol, S.prc = sb("scan_reset", [P, T]), sb("pair_columns", [P, 19]), sb("rkv", [P, 3, T])
    lora_block(nc, g, S)
    with nc.Block() as block:
        @block.sync
        def _(sp):
            sp.wait_ge(S.wall_full, 16 * 5)
            sp.wait_ge(S.toep_written, 16 * 2 * HP)
    with nc.Fori(0, HP) as hp:
        with ExitStack() as st:
            sb2 = lambda n, s: st.enter_context(nc.sbuf_tensor(n, s, F32))
            A = Tiles()
            A.qT, A.kT, A.v = sb2("qT", [P, T]), sb2("kT", [P, T]), sb2("v", [P, NB, P])
            project_block(nc, g, S, hp, A)
            na_block(nc, g, S, hp, A)
        rwkv_pair(nc, g, S, hp)
    with nc.Block() as block:
        @block.sync
        def _(sp):
            sp.wait_ge(S.slab_full, 16 * 6)





class Inputs:

    def __init__(self, x, c, ctx, c_ctx, ada_w, ada_b, ln_g, ln_b, even_w_in, even_w_out, shift_w, na_rpb,
                 rw_w0, rw_w_up, rw_a0, rw_a_up, rw_g_up, rw_k_k, rw_k_a, rw_r_k, rw_gn_g, rw_gn_b,
                 odd_w_in, odd_w_out, da_lq1, da_lk1, da_lq2, da_lk2, da_subln_g, router_w, router_b,
                 exp_w_gate, exp_w_up, exp_w_down, const, rope):
        self.x, self.c, self.ctx, self.c_ctx = x, c, ctx, c_ctx
        self.ada_w, self.ada_b, self.ln_g, self.ln_b = ada_w, ada_b, ln_g, ln_b
        self.even_w_in, self.even_w_out, self.shift_w, self.na_rpb = even_w_in, even_w_out, shift_w, na_rpb
        self.rw_w0, self.rw_w_up, self.rw_a0, self.rw_a_up, self.rw_g_up = rw_w0, rw_w_up, rw_a0, rw_a_up, rw_g_up
        self.rw_k_k, self.rw_k_a, self.rw_r_k, self.rw_gn_g, self.rw_gn_b = rw_k_k, rw_k_a, rw_r_k, rw_gn_g, rw_gn_b
        self.odd_w_in, self.odd_w_out, self.da_subln_g = odd_w_in, odd_w_out, da_subln_g
        self.da_lq1, self.da_lk1, self.da_lq2, self.da_lk2 = da_lq1, da_lk1, da_lq2, da_lk2
        self.router_w, self.router_b = router_w, router_b
        self.exp_w_gate, self.exp_w_up, self.exp_w_down = exp_w_gate, exp_w_up, exp_w_down
        self.const, self.rope = const, rope


def program(nc, g, outs):
    with ExitStack() as ctx:
        def sb(name, shape):
            return ctx.enter_context(nc.sbuf_tensor(name, shape, F32))
        S = Tiles()
        S.cst = sb("constants", [P, C_END])
        S.col = sb("vector_columns", [P, R_END])
        S.adab = sb("ada_b_columns", [P, 96])
        S.csil = sb("silu_c", [P, 16])
        S.mcol = sb("modulation_columns", [P, DEPTH, 2, 48])
        S.router = sb("router", [P, KD, N_EXP])
        S.rbias = sb("router_bias", [P, N_EXP])
        S.ps = ctx.enter_context(nc.psum_tensor("psum", [P, 8, 512], F32))
        S.uT = sb("uT", [P, KD, T])
        g.toep = nc.dram_tensor("na_bias_toeplitz", (2 * HP, GRID_W, 7, GRID_W), F32).ap()
        S.toep_written = ctx.enter_context(nc.semaphore("toeplitz_written"))
        toeplitz_copies(nc, g, S)
        stages(nc, g, S, outs)


_INS = ["x", "c", "ctx", "c_ctx", "ada_w", "ada_b", "ln_g", "ln_b", "even_w_in", "even_w_out", "shift_w", "na_rpb",
        "rw_w0", "rw_w_up", "rw_a0", "rw_a_up", "rw_g_up", "rw_k_k", "rw_k_a", "rw_r_k", "rw_gn_g", "rw_gn_b",
        "odd_w_in", "odd_w_out", "da_lq1", "da_lk1", "da_lq2", "da_lk2", "da_subln_g", "router_w", "router_b",
        "exp_w_gate", "exp_w_up", "exp_w_down"]


def kernel(**inputs):
    import numpy as np
    import concourse.bacc as bacc
    from concourse.bass_utils import run_bass_kernel_spmd as run

    nc = bacc.Bacc("TRN2", target_bir_lowering=False, num_devices=1)
    arrays = {"in_" + name: np.ascontiguousarray(inputs[name]) for name in _INS}
    arrays["in_const"], arrays["in_rope"] = shape_constants(np)
    aps = [nc.dram_tensor(name, a.shape, F32, kind="ExternalInput").ap() for name, a in arrays.items()]
    outs = [nc.dram_tensor(f"out_{i}", s, F32, kind="ExternalOutput").ap() for i, s in enumerate(OUTS)]
    program(nc, Inputs(*aps), outs)
    r = run(nc, [arrays], core_ids=[0])
    got = tuple(r.results[0][f"out_{i}"] for i in range(len(OUTS)))
    return got[0] if len(got) == 1 else got


OUTS = [(1, T_LAT, D)]


def stages(nc, g, S, outs):
    with nc.sbuf_tensor("h_in", [P, NB, D], F32) as h:
        S.h = h
        setup_block(nc, g, S)
        ada_blocks(nc, g, S)
        modulate_block(nc, g, S, 0, 0, load_h=True)
    with ExitStack() as ctx:
        sb = lambda n, s: ctx.enter_context(nc.sbuf_tensor(n, s, F32))
        S.combine, S.place = sb("combine", [P, NB, N_EXP]), sb("place", [P, NB, N_EXP])
        S.item_place, S.item_gate = sb("item_place", [P, NB, N_ITEM]), sb("item_gate", [P, NB, N_ITEM])
        S.item_expert = ctx.enter_context(nc.sbuf_tensor("item_expert", [P, N_ITEM], mybir.dt.int32))
        S.pairs = ctx.enter_context(nc.sbuf_tensor("item_pairs", [P, 1], mybir.dt.int32))
        with nc.Block() as block:
            @block.gpsimd
            def _(pool):
                nc.gpsimd.memset(S.item_gate[:, :, :], 0.0)
                nc.gpsimd.memset(S.item_place[:, :, :], -1.0)
        S.h = sb("h", [P, NB, D])
        with nc.sbuf_tensor("oT0", [P, 2 * HP, T], F32) as S.oT:
            with ExitStack() as mx:
                even_mixer(nc, g, S, lambda n, s: mx.enter_context(nc.sbuf_tensor(n, s, F32)), ctx)
            post_block(nc, g, S, 0, 0, range(NB), project=g.even_w_out[0], load_h=True)
        experts(nc, g, S, 0, range(NB))
        latent = range(T_CTX // P, NB)
        modulate_block(nc, g, S, 1, 0)
        with nc.sbuf_tensor("oT1", [P, 2 * HP, T], F32) as S.oT:
            odd_mixer(nc, g, S, 1)
            post_block(nc, g, S, 1, 0, latent, project=g.odd_w_out[0])
        experts(nc, g, S, 1, latent)
        written = ctx.enter_context(nc.semaphore("output_written"))
        with nc.Block() as block:
            @block.sync
            def _(sp):
                sp.dma_start(outs[0][0].rearrange("(b p) d -> p b d", p=P), S.h[:, T_CTX // P:NB, :]).then_inc(written, 16)
                sp.wait_ge(written, 16)


def experts(nc, g, S, l, blocks):
    modulate_block(nc, g, S, l, 3, blocks=blocks)
    router_block(nc, g, S, l, blocks)
    with nc.sbuf_tensor(f"acc{l}", [P, NB, D], F32) as S.acc:
        with nc.sbuf_tensor(f"uN{l}", [P, NB, D], F32) as S.uN:
            token_major_block(nc, S, l, blocks)
            moe(nc, g, S, l, blocks)
        post_block(nc, g, S, l, 1, blocks)
```

```python
from contextlib import ExitStack, contextmanager

import concourse.bass as bass
from concourse import mybir

F32 = mybir.dt.float32
ACT = mybir.ActivationFunctionType
ALU = mybir.AluOpType
AX = mybir.AxisListType

P = 128
D = 1024
KD = D // P
T_CTX, T_LAT = 256, 256
T = T_CTX + T_LAT
NB = T // P
DEPTH = 2
GRID_W = 64
HP = 4
CH = 64
RW_IN = 1792
N_EXP, D_EXP = 16, 512
ALPHA = (2 * DEPTH) ** 0.25
DECAY = 0.6065306597126334
HD = 64
WIN_C = 16
DA_H = 8
LAMBDA_INIT = 0.3555090675909693
NEG = -1.0e30

C_ID, C_ONES, C_MASK, C_LVL, C_WIN, C_ROT, C_IOTA, C_TRI, C_ALL, C_END = 0, 128, 256, 768, 1536, 1600, 1728, 1856, 1984, 2112
C_EIDX = C_END
C_JIDX = C_END + 16
C_END += 16 + 32
N_ITEM = 26
ROWS = N_ITEM * P
R_C, R_CC, R_SW, R_W0, R_A0, R_KK, R_KA, R_RK, R_GG, R_GB, R_END = 0, 8, 16, 58, 66, 74, 78, 82, 86, 90, 94


class Tiles:

    ndump = 0


class Link:

    def __init__(self, eng, sem):
        self.eng, self.sem, self.n = eng, sem, 0

    def __call__(self, ins):
        self.n += 1
        ins.then_inc(self.sem, 1)
        self.eng.wait_ge(self.sem, self.n)


def clear_block(nc, sems):
    with nc.Block() as block:
        @block.sync
        def _(sp):
            for s in sems:
                sp.sem_clear(s)


@contextmanager
def phase(nc, sems):
    with nc.Block() as block:
        yield block
    clear_block(nc, sems)


def shape_constants(np):
    c = np.zeros((P, C_END), np.float32)
    i = np.arange(P)
    c[:, C_ID:C_ID + P] = np.eye(P)
    same_head = (i[:, None] // CH) == (i[None] // CH)
    c[:, C_ONES:C_ONES + P] = same_head
    s, t = i[:, None] % CH, i[None] % CH
    for n, m in enumerate((s < t, s <= t, s > t, s >= t)):
        c[:, C_MASK + n * P:C_MASK + (n + 1) * P] = m & same_head
    for n in range(6):
        b = 1 << n
        c[:, C_LVL + n * P:C_LVL + (n + 1) * P] = same_head & (s // (2 * b) == t // (2 * b)) & (s // b != t // b)
    c[:, C_IOTA:C_IOTA + P] = i[None]
    c[:, C_EIDX:C_EIDX + 16] = np.arange(16)[None]
    c[:, C_JIDX:C_JIDX + 32] = np.arange(32)[None]
    c[:, C_TRI:C_TRI + P] = i[:, None] < i[None]
    c[:, C_ALL:C_ALL + P] = 1.0
    q, k = i[:, None] % GRID_W, np.arange(GRID_W)[None]
    lo = np.clip(q - WIN_C // 2, 0, GRID_W - WIN_C)
    c[:, C_WIN:C_WIN + GRID_W] = np.where((k >= lo) & (k < lo + WIN_C), 0.0, NEG)
    for r in range(P):
        m = r % 32
        if m < 16:
            c[r + 16, C_ROT + r] = -1.0
        else:
            c[r - 16, C_ROT + r] = 1.0
    rope = np.zeros((P, 2, T_LAT), np.float32)
    tok = np.arange(T_LAT)
    inv = (np.float32(10000.0) ** (-np.arange(16, dtype=np.float32) / np.float32(16))).astype(np.float32)
    for r in range(P):
        pos = tok // GRID_W if (r % 64) < 32 else tok % GRID_W
        ang = pos.astype(np.float32) * inv[r % 16]
        rope[r, 0], rope[r, 1] = np.cos(ang), np.sin(ang)
    return c, rope.reshape(P, 2 * T_LAT)


def setup_block(nc, g, S):
    with ExitStack() as ctx:
        rows = ctx.enter_context(nc.sbuf_tensor("rows", [R_END, P], F32))
        abrows = ctx.enter_context(nc.sbuf_tensor("abrows", [96, P], F32))
        loaded = ctx.enter_context(nc.semaphore("consts_loaded"))
        turned = ctx.enter_context(nc.semaphore("columns_turned"))
        copied = ctx.enter_context(nc.semaphore("columns_copied"))
        block = ctx.enter_context(phase(nc, [loaded, turned, copied]))
        loads = [
            (S.cst[:, :], g.const),
            (abrows[:, :], g.ada_b.rearrange("l (j p) -> (l j) p", p=P)),
            (rows[R_C:R_CC, :], g.c.rearrange("b (k p) -> (b k) p", p=P)),
            (rows[R_CC:R_SW, :], g.c_ctx.rearrange("(k p) -> k p", p=P)),
            (rows[R_SW:R_W0, :], g.shift_w.rearrange("n j (k p) -> (n j k) p", p=P)),
            (rows[R_W0:R_A0, :], g.rw_w0.rearrange("n d (k p) -> (n d k) p", p=P)),
            (rows[R_A0:R_KK, :], g.rw_a0.rearrange("n d (k p) -> (n d k) p", p=P)),
            (rows[R_KK:R_KA, :], g.rw_k_k.rearrange("n (k p) -> (n k) p", p=P)),
            (rows[R_KA:R_RK, :], g.rw_k_a.rearrange("n (k p) -> (n k) p", p=P)),
            (rows[R_RK:R_GG, :], g.rw_r_k.rearrange("n (k a) p -> (n k) (a p)", a=2)),
            (rows[R_GG:R_GB, :], g.rw_gn_g.rearrange("n (k p) -> (n k) p", p=P)),
            (rows[R_GB:R_END, :], g.rw_gn_b.rearrange("n (k p) -> (n k) p", p=P)),
            (S.router[:, :, :], g.router_w.rearrange("(k p) e -> p k e", p=P)),
            (S.rbias[:, :], g.router_b.rearrange("(a e) -> a e", a=1).to_broadcast([P, N_EXP])),
        ]

        @block.sync
        def _(sp):
            for dst, src in loads:
                sp.dma_start(dst, src).then_inc(loaded, 16)

        @block.tensor
        def _(pe):
            pe.wait_ge(loaded, 16 * len(loads))
            nc.tensor.transpose(S.ps[:, 0, 0:R_END], rows[:, :], S.cst[0:R_END, C_ID:C_ID + R_END]).then_inc(turned, 1)
            nc.tensor.transpose(S.ps[:, 1, 0:96], abrows[:, :], S.cst[0:96, C_ID:C_ID + 96]).then_inc(turned, 1)

        @block.vector
        def _(dve):
            dve.wait_ge(turned, 1)
            nc.vector.tensor_copy(S.col[:, :], S.ps[:, 0, 0:R_END]).then_inc(copied, 1)
            dve.wait_ge(turned, 2)
            nc.vector.tensor_copy(S.adab[:, :], S.ps[:, 1, 0:96])

        @block.scalar
        def _(act):
            act.wait_ge(copied, 1)
            nc.scalar.activation(S.csil[:, :], S.col[:, R_C:R_SW], ACT.Silu)


ADA_J = 4
ADA_W = 512


def ada_blocks(nc, g, S):
    per = ADA_J * ADA_W // P
    groups = [(l, i) for l in range(DEPTH) for i in range(6 * D // (ADA_J * ADA_W))]
    with ExitStack() as ctx:
        slab = ctx.enter_context(nc.sbuf_tensor("ada_slab", [P, 2, ADA_J, KD, ADA_W], F32))
        rows = ctx.enter_context(nc.sbuf_tensor("ada_rows", [P, 2, ADA_W], F32))
        full = [ctx.enter_context(nc.semaphore(f"ada_slabs_full{u}")) for u in range(2)]
        cleared, summed, copied, turned, added = [ctx.enter_context(nc.semaphore("ada_" + m))
                                                  for m in ("rows_cleared", "summed", "rows_copied", "turned", "bias_added")]
        csil = S.csil[:, :].rearrange("p (w k) -> p k w", w=2)
        with phase(nc, full + [cleared, summed, copied, turned, added]) as block:
            def load(eng, n, js):
                l, i = groups[n]
                src = g.ada_w[l].rearrange("(k p) n -> p k n", p=P)
                for j in js:
                    c0 = (i * ADA_J + j) * ADA_W
                    eng.dma_start(slab[:, n % 2, j], src[:, :, c0:c0 + ADA_W]).then_inc(full[n % 2], 16)

            @block.sync
            def _(sp):
                for n in range(len(groups)):
                    if n >= 2:
                        sp.wait_ge(summed, n - 1)
                    load(sp, n, range(ADA_J))

            @block.gpsimd
            def _(pool):
                nc.gpsimd.memset(rows[:, :, :], 0.0).then_inc(cleared, 1)

            @block.tensor
            def _(pe):
                def turn(n):
                    pe.wait_ge(copied, ADA_J * (n + 1))
                    if n >= 2:
                        pe.wait_ge(added, n - 1)
                    for q in range(ADA_W // P):
                        last = nc.tensor.transpose(S.ps[:, 2 + n % 2, q * P:(q + 1) * P], rows[:, n % 2, q * P:(q + 1) * P],
                                                   S.cst[:, C_ID:C_ID + P])
                    last.then_inc(turned, 1)

                for n in range(len(groups)):
                    pe.wait_ge(full[n % 2], 16 * ADA_J * (n // 2 + 1))
                    if n >= 2:
                        pe.wait_ge(copied, ADA_J * (n - 1))
                    for k in range(KD):
                        for j in range(ADA_J):
                            last = nc.tensor.matmul(S.ps[32 * j:32 * j + 2, n % 2, :], csil[:, k, :], slab[:, n % 2, j, k, :],
                                                    start=(k == 0), stop=(k == KD - 1))
                    last.then_inc(summed, 1)
                    if n:
                        turn(n - 1)
                turn(len(groups) - 1)

            @block.scalar
            def _(act):
                act.wait_ge(cleared, 1)
                for n in range(len(groups)):
                    act.wait_ge(summed, n + 1)
                    if n >= 2:
                        act.wait_ge(turned, n - 1)
                    for j in range(ADA_J):
                        nc.scalar.activation(rows[32 * j:32 * j + 2, n % 2, :], S.ps[32 * j:32 * j + 2, n % 2, :], ACT.Copy).then_inc(copied, 1)

            @block.vector
            def _(dve):
                for n, (l, i) in enumerate(groups):
                    dve.wait_ge(turned, n + 1)
                    c0 = i * per
                    for w in range(2):
                        out = S.mcol[:, l, w, c0:c0 + per].rearrange("p (j q) -> p j q", j=ADA_J)
                        got = S.ps[:, 2 + n % 2, :].rearrange("p (q j r) -> p j q r", j=ADA_J, r=32)[:, :, :, w]
                        bias = S.adab[:, l * 48 + c0:l * 48 + c0 + per].rearrange("p (j q) -> p j q", j=ADA_J)
                        last = nc.vector.tensor_tensor(out, got, bias, ALU.add)
                    last.then_inc(added, 1)
        with nc.Block() as block:
            @block.vector
            def _(dve):
                for l in range(DEPTH):
                    for m in (1, 4):
                        nc.vector.tensor_scalar(S.mcol[:, l, :, m * KD:(m + 1) * KD], S.mcol[:, l, :, m * KD:(m + 1) * KD],
                                                1.0, None, ALU.add)


def modulate_block(nc, g, S, l, m, load_h=False, blocks=range(NB)):
    tag = f"{l}_{m}"
    blocks = list(blocks)
    with ExitStack() as ctx:
        loaded = ctx.enter_context(nc.semaphore("h_loaded" + tag))
        turned = ctx.enter_context(nc.semaphore("h_turned" + tag))
        lat_done = ctx.enter_context(nc.semaphore("u_lat_done" + tag))
        ctx_done = ctx.enter_context(nc.semaphore("u_ctx_done" + tag))
        block = ctx.enter_context(phase(nc, [loaded, turned, lat_done, ctx_done]))

        @block.sync
        def _(sp):
            if load_h:
                load_tokens(sp, g, S.h, loaded)

        @block.tensor
        def _(pe):
            if load_h:
                pe.wait_ge(loaded, 32)
            for k in range(KD):
                for half, done in ((0, ctx_done), (1, lat_done)):
                    mine = [b for b in blocks if b // 2 == half]
                    if mine and k >= 4:
                        pe.wait_ge(done, k - 3)
                    for b in mine:
                        last = nc.tensor.transpose(S.ps[:, 4 * half + k % 4, (b % 2) * P:(b % 2 + 1) * P],
                                                   S.h[:, b, k * P:(k + 1) * P], S.cst[:, C_ID:C_ID + P])
                last.then_inc(turned, 1)

        def col(w, r, k):
            return S.mcol[:, l, w, (m + r) * KD + k:(m + r) * KD + k + 1]

        @block.scalar
        def _(act):
            for k in range(KD):
                act.wait_ge(turned, k + 1)
                nc.scalar.activation(S.uT[:, k, T_CTX:T], S.ps[:, 4 + k % 4, 0:T_LAT], ACT.Identity,
                                     bias=col(0, 0, k), scale=col(0, 1, k)).then_inc(lat_done, 1)

        @block.vector
        def _(dve):
            if blocks[0] == 0:
                for k in range(KD):
                    dve.wait_ge(turned, k + 1)
                    nc.vector.tensor_scalar(S.uT[:, k, 0:T_CTX], S.ps[:, k % 4, 0:T_CTX],
                                            col(1, 1, k), col(1, 0, k), ALU.mult, ALU.add).then_inc(ctx_done, 1)


def load_tokens(sp, g, h, sem):
    sp.dma_start(h[:, 0:2, :], g.ctx[0].rearrange("(b p) d -> p b d", p=P)).then_inc(sem, 16)
    sp.dma_start(h[:, 2:4, :], g.x[0].rearrange("(b p) d -> p b d", p=P)).then_inc(sem, 16)


def dump_block(nc, S, dst, src):
    with ExitStack() as ctx:
        S.ndump += 1
        sem = ctx.enter_context(nc.semaphore(f"dumped{S.ndump}"))
        block = ctx.enter_context(nc.Block())

        @block.sync
        def _(sp):
            sp.dma_start(dst, src).then_inc(sem, 16)
            sp.wait_ge(sem, 16)


NA_SCALE = float(HD) ** -0.5
PAIR = 2 * HD
W_NA = 512


def load_pair_slabs(sp, g, S, hp):
    src = g.even_w_in[0].rearrange("(k p) n -> p k n", p=P)
    for n in range(6):
        sp.dma_start(S.wslab[:, n], src[:, :, bass.ds(hp * PAIR + n * W_NA, PAIR)]).then_inc(S.slab_full, 16)


def lora_block(nc, g, S):
    with ExitStack() as ctx:
        slab = ctx.enter_context(nc.sbuf_tensor("lora_slab", [P, KD, 256], F32))
        loaded = ctx.enter_context(nc.semaphore("lora_loaded"))
        cleared = ctx.enter_context(nc.semaphore("lora_cleared"))
        projected = ctx.enter_context(nc.semaphore("lora_projected"))
        scaled = ctx.enter_context(nc.semaphore("lora_scaled"))
        chain = ctx.enter_context(nc.semaphore("lora_conv_chain"))
        conved = ctx.enter_context(nc.semaphore("lora_conved"))
        block = ctx.enter_context(phase(nc, [loaded, cleared, projected, scaled, chain, conved]))

        @block.sync
        def _(sp):
            src = g.even_w_in[0].rearrange("(k p) n -> p k n", p=P)
            sp.dma_start(slab[:, :, :], src[:, :, 3072:3328]).then_inc(loaded, 16)
            load_pair_slabs(sp, g, S, 0)
            sp.wait_ge(cleared, 1)
            for d in range(2):
                sp.dma_start(S.wall[0:64, d, :], g.rw_w_up[0, d]).then_inc(S.wall_full, 16)
                sp.dma_start(S.wall[64:128, 2 + d, :], g.rw_a_up[0, d]).then_inc(S.wall_full, 16)
            sp.dma_start(S.wall[:, 4, :], g.rw_g_up[0]).then_inc(S.wall_full, 16)

        @block.gpsimd
        def _(pool):
            nc.gpsimd.memset(S.wall[:, :, :], 0.0).then_inc(cleared, 1)

        @block.tensor
        def _(pe):
            pe.wait_ge(loaded, 16)
            for j in range(2):
                for k in range(KD):
                    last = nc.tensor.matmul(S.ps[:, j, :], slab[:, k, j * P:(j + 1) * P], S.uT[:, k, :],
                                            start=(k == 0), stop=(k == KD - 1))
                last.then_inc(projected, 1)

        @block.scalar
        def _(act):
            for j in range(2):
                act.wait_ge(projected, j + 1)
                w1 = R_SW + 14 + 12 + j
                nc.scalar.activation(S.xlora[:, j, :], S.ps[:, j, :], ACT.Copy, scale=S.col[:, w1:w1 + 1]).then_inc(scaled, 1)
            act.wait_ge(conved, 1)
            nc.scalar.activation(S.xlora[0:64, 0, :], S.xlora[0:64, 0, :], ACT.Tanh)
            act.wait_ge(conved, 2)
            nc.scalar.activation(S.xlora[:, 1, :], S.xlora[:, 1, :], ACT.Sigmoid)

        @block.vector
        def _(dve):
            link = Link(dve, chain)
            nc.vector.memset(S.reset[:, :], 1.0)
            for j in range(2):
                dve.wait_ge(scaled, j + 1)
                conv_taps(nc, link, S.xlora[:, j, :], S.ps[:, j, :],
                          S.col[:, R_SW + 12 + j:R_SW + 13 + j], S.col[:, R_SW + 28 + 12 + j:R_SW + 28 + 13 + j], conved)
            nc.vector.memset(S.reset[:, :].rearrange("p (c t) -> p c t", t=CH)[:, :, 0:1], 0.0)


def conv_taps(nc, link, out, raw, w0, w2, done):
    o = out.rearrange("p (g t) -> p g t", g=2)
    r = raw.rearrange("p (g t) -> p g t", g=2)
    n = T_CTX
    link(nc.vector.scalar_tensor_tensor(out=o[:, :, 1:n], in0=r[:, :, 0:n - 1], scalar=w0, in1=o[:, :, 1:n],
                                        op0=ALU.mult, op1=ALU.add))
    nc.vector.scalar_tensor_tensor(out=o[:, :, 0:n - 1], in0=r[:, :, 1:n], scalar=w2, in1=o[:, :, 0:n - 1],
                                   op0=ALU.mult, op1=ALU.add).then_inc(done, 1)


def project_block(nc, g, S, hp, A):
    with ExitStack() as ctx:
        sem = lambda n: ctx.enter_context(nc.semaphore("pj_" + n))
        ready, scaled, chain, picked, conved = sem("ready"), sem("scaled"), sem("chain"), sem("picked"), sem("conved")
        with nc.Block() as block:
            @block.tensor
            def _(pe):
                pe.wait_ge(S.slab_full, 16 * 6)
                for n in (0, 1, 3, 4, 5):
                    for k in range(KD):
                        last = nc.tensor.matmul(S.ps[:, n, :], S.wslab[:, n, k, :], S.uT[:, k, :],
                                                start=(k == 0), stop=(k == KD - 1))
                    last.then_inc(ready, 1)
                for b in range(NB):
                    for k in range(KD):
                        last = nc.tensor.matmul(S.ps[:, 2, b * P:(b + 1) * P], S.uT[:, k, b * P:(b + 1) * P],
                                                S.wslab[:, 2, k, :], start=(k == 0), stop=(k == KD - 1))
                last.then_inc(ready, 1)

            @block.scalar
            def _(act):
                act.wait_ge(ready, 1)
                nc.scalar.activation(A.qT[:, :], S.ps[:, 0, :], ACT.Copy)
                act.wait_ge(picked, 1)
                for j in range(3):
                    act.wait_ge(ready, 3 + j)
                    nc.scalar.activation(S.prc[:, j, :], S.ps[:, 3 + j, :], ACT.Copy, scale=S.hcol[:, 3 + j:4 + j]).then_inc(scaled, 1)
                act.wait_ge(ready, 6)
                nc.scalar.activation(A.v[:, :, :], S.ps[:, 2, :].rearrange("p (b n) -> p b n", b=NB), ACT.Copy)

            @block.vector
            def _(dve):
                link = Link(dve, chain)
                for j in range(3):
                    a = R_SW + 14 * j
                    nc.vector.tensor_copy(S.hcol[:, 3 * j:3 * j + 3].rearrange("p (n o) -> p n o", o=1),
                                          S.col[:, a:a + 12].rearrange("p (n h) -> p n h", h=HP)[:, :, bass.ds(hp, 1)])
                link(nc.vector.tensor_copy(S.hcol[:, 9:18].rearrange("p (n o) -> p n o", o=1),
                                           S.col[:, R_W0:R_END].rearrange("p (n h) -> p n h", h=HP)[:, :, bass.ds(hp, 1)]))
                link(nc.vector.tensor_scalar(S.hcol[:, 18:19], S.hcol[:, 14:15], -1.0, 1.0, ALU.mult, ALU.add))
                nc.vector.tensor_copy(S.wst[:, :, :], S.wall[:, :, bass.ds(hp * PAIR, PAIR)]).then_inc(picked, 1)
                dve.wait_ge(ready, 2)
                nc.vector.tensor_copy(A.kT[:, :], S.ps[:, 1, :])
                for j in range(3):
                    dve.wait_ge(scaled, j + 1)
                    conv_taps(nc, link, S.prc[:, j, :], S.ps[:, 3 + j, :], S.hcol[:, j:j + 1], S.hcol[:, 6 + j:7 + j], conved)
        clear_block(nc, [ready, scaled, chain, picked, conved])


def na_block(nc, g, S, hp, A):
    units = [(qb, hh) for qb in (2, 3, 0, 1) for hh in (0, 1)]
    with ExitStack() as ctx:
        sem = lambda n: ctx.enter_context(nc.semaphore("na_" + n))
        bias_full, masked = sem("bias_full"), sem("bias_masked")
        scored, read, maxed, exped = sem("scored"), sem("scores_read"), sem("maxed"), sem("exped")
        normed, turned, copied, summed, written, chain = (sem("normed"), sem("turned"), sem("pt_copied"), sem("av_summed"),
                                                          sem("o_written"), sem("chain"))
        sb = lambda n, s: ctx.enter_context(nc.sbuf_tensor("na_" + n, s, F32))
        bias = sb("bias", [P, 2, 2, T_LAT])
        s_, p_, pt = sb("s", [P, 2, T]), sb("p", [P, 2, T]), sb("pt", [P, 2, NB, P])
        nmax, ssum, rinv = sb("nmax", [P, 8]), sb("ssum", [P, 8]), sb("rinv", [P, 8])

        def keys(u):
            return T if units[u][0] >= 2 else T_CTX

        with nc.Block() as block:
            @block.sync
            def _(sp):
                for qt in range(2):
                    for r2 in range(2):
                        for hh in range(2):
                            sp.dma_start(bias[r2 * 64:(r2 + 1) * 64, qt, hh, :].rearrange("p (a b) -> p a b", a=4),
                                         g.toep[bass.ds(hp * 2 + hh, 1), :, 3 - 2 * qt - r2:7 - 2 * qt - r2, :].rearrange("o c a b -> (o c) a b")).then_inc(bias_full, 16)
                sp.sem_clear(S.slab_full)
                load_pair_slabs(sp, g, S, hp + 1)

            @block.gpsimd
            def _(pool):
                pool.wait_ge(bias_full, 16 * 8)
                b = bias[:, :, :, :].rearrange("p q h (r c) -> p (q h r) c", c=GRID_W)
                nc.gpsimd.tensor_tensor(b, b, S.cst[:, C_WIN:C_WIN + GRID_W].unsqueeze(1).to_broadcast([P, 16, GRID_W]),
                                        ALU.add).then_inc(masked, 1)

            @block.tensor
            def _(pe):
                n = len(units)
                for i in range(n + 2):
                    if i < n:
                        qb, hh = units[i]
                        if i >= 2:
                            pe.wait_ge(read, i - 1)
                        h0 = hh * HD
                        nc.tensor.matmul(S.ps[:, i % 2, 0:keys(i)], A.qT[h0:h0 + HD, qb * P:(qb + 1) * P],
                                         A.kT[h0:h0 + HD, 0:keys(i)], start=True, stop=True).then_inc(scored, 1)
                    if 0 <= i - 1 < n:
                        u = i - 1
                        pe.wait_ge(normed, u + 1)
                        if u >= 2:
                            pe.wait_ge(copied, u - 1)
                        for b in range(keys(u) // P):
                            last = nc.tensor.transpose(S.ps[:, 2 + u % 2, b * P:(b + 1) * P], p_[:, u % 2, b * P:(b + 1) * P],
                                                       S.cst[:, C_ID:C_ID + P])
                        last.then_inc(turned, 1)
                    if 0 <= i - 2 < n:
                        u = i - 2
                        qb, hh = units[u]
                        pe.wait_ge(copied, u + 1)
                        if u >= 2:
                            pe.wait_ge(written, u - 1)
                        h0 = hh * HD
                        nk = keys(u) // P
                        for b in range(nk):
                            last = nc.tensor.matmul(S.ps[h0:h0 + HD, 4 + u % 2, 0:P], A.v[:, b, h0:h0 + HD], pt[:, u % 2, b, :],
                                                    start=(b == 0), stop=(b == nk - 1))
                        last.then_inc(summed, 1)

            @block.vector
            def _(dve):
                link = Link(dve, chain)
                n = len(units)
                dve.wait_ge(masked, 1)
                for i in range(n + 1):
                    if i < n:
                        qb, hh = units[i]
                        dve.wait_ge(scored, i + 1)
                        if i >= 2:
                            dve.wait_ge(exped, i - 1)
                        if keys(i) == T:
                            nc.vector.tensor_scalar(s_[:, i % 2, 0:T_CTX], S.ps[:, i % 2, 0:T_CTX], NA_SCALE, None, ALU.mult)
                            nc.vector.scalar_tensor_tensor(out=s_[:, i % 2, T_CTX:T], in0=S.ps[:, i % 2, T_CTX:T],
                                                           scalar=NA_SCALE, in1=bias[:, qb - 2, hh, :],
                                                           op0=ALU.mult, op1=ALU.add).then_inc(read, 1)
                        else:
                            nc.vector.tensor_scalar(s_[:, i % 2, 0:T_CTX], S.ps[:, i % 2, 0:T_CTX], NA_SCALE, None,
                                                    ALU.mult).then_inc(read, 1)
                        dve.wait_ge(read, i + 1)
                        nc.vector.tensor_reduce(nmax[:, i:i + 1], s_[:, i % 2, 0:keys(i)], AX.X, ALU.max,
                                                negate=True).then_inc(maxed, 1)
                    if i >= 1:
                        u = i - 1
                        dve.wait_ge(exped, u + 1)
                        link(nc.vector.reciprocal(rinv[:, u:u + 1], ssum[:, u:u + 1]))
                        nc.vector.tensor_scalar(p_[:, u % 2, 0:keys(u)], p_[:, u % 2, 0:keys(u)], rinv[:, u:u + 1], None,
                                                ALU.mult).then_inc(normed, 1)

            @block.scalar
            def _(act):
                n = len(units)
                for i in range(n + 2):
                    if i < n:
                        act.wait_ge(maxed, i + 1)
                        if i >= 2:
                            act.wait_ge(turned, i - 1)
                        nc.scalar.activation(p_[:, i % 2, 0:keys(i)], s_[:, i % 2, 0:keys(i)], ACT.Exp,
                                             bias=nmax[:, i:i + 1], accum_out=ssum[:, i:i + 1]).then_inc(exped, 1)
                    if 0 <= i - 1 < n:
                        u = i - 1
                        act.wait_ge(turned, u + 1)
                        if u >= 2:
                            act.wait_ge(summed, u - 1)
                        nk = keys(u) // P
                        nc.scalar.activation(pt[:, u % 2, 0:nk, :], S.ps[:, 2 + u % 2, 0:nk * P].rearrange("p (b q) -> p b q", q=P),
                                             ACT.Copy).then_inc(copied, 1)
                    if 0 <= i - 2 < n:
                        u = i - 2
                        qb, hh = units[u]
                        act.wait_ge(summed, u + 1)
                        h0 = hh * HD
                        nc.scalar.activation(S.oT[h0:h0 + HD, bass.ds(hp, 1), qb * P:(qb + 1) * P].rearrange("p o t -> p (o t)"),
                                             S.ps[h0:h0 + HD, 4 + u % 2, 0:P], ACT.Copy).then_inc(written, 1)
        clear_block(nc, [bias_full, masked, scored, read, maxed, exped, normed, turned, copied, summed, written, chain])


def toeplitz_copies(nc, g, S):
    na, nb = 15, 31
    flat = g.na_rpb.rearrange("n h a b -> (n h a b)")
    with nc.Block() as block:
        @block.sync
        def _(sp):
            for h in range(2 * HP):
                at = flat[h * na * nb + 4 * nb + 15:h * na * nb + 4 * nb + 16]
                src = bass.AP(tensor=at.tensor, offset=at.offset, ap=[[nb, 7], [-1, GRID_W], [1, GRID_W]])
                sp.dma_start(g.toep[h].rearrange("c a b -> a c b"), src).then_inc(S.toep_written, 16)


NC_ = T_CTX // CH
E_IN, E_EX, E_INV, E_BAR = range(4)
BA, BR, BB, BK, BBB, BKB = range(6)


def rwkv_pair(nc, g, S, hp):
    with ExitStack() as st:
        sb = lambda n, s: st.enter_context(nc.sbuf_tensor("rw_" + n, s, F32))
        R = Tiles()
        R.y = sb("y", [P, T])
        R.bonus = sb("bonus", [P, T])
        R.gate = sb("gate", [P, T])
        R.last = [sb(f"last{d}", [P, P]) for d in range(2)]
        R.bd = [sb(f"bd{d}", [P, 6, NC_, P]) for d in range(2)]
        R.vbd = sb("vbd", [P, NC_, P])
        R.wc = sb("wc", [P, 2, NC_])
        with nc.Block() as block:
            @block.gpsimd
            def _(pool):
                for d in range(2):
                    nc.gpsimd.memset(R.last[d][:, :], 0.0)
                    nc.gpsimd.memset(R.bd[d][:, :, :, :], 0.0)
                nc.gpsimd.memset(R.vbd[:, :, :], 0.0)
        with nc.Fori(0, 2) as half:
            tok = half * T_CTX
            rwkv_prepare(nc, S, R, tok)
            rwkv_chunks(nc, S, R, tok)
        rwkv_finish(nc, S, R, hp)


def rwkv_prepare(nc, S, R, tok):
    n = T_CTX
    with ExitStack() as st:
        sb = lambda m, s: st.enter_context(nc.sbuf_tensor("rp_" + m, s, F32))
        sem = lambda m: st.enter_context(nc.semaphore("rp_" + m))
        sig, av, keff, nka = sb("sig", [P, 2, n]), sb("a", [P, 2, n]), sb("keff", [P, 2, n]), sb("nka", [P, 2, n])
        cinc, y_, z_, w_ = sb("cinc", [P, 2, n]), sb("cexc", [P, 2, n]), sb("cbar", [P, 2, n]), sb("crev", [P, n])
        kraw, sq, kk, ex = sb("kraw", [P, n]), sb("sq", [P, n]), sb("kk", [P, n]), sb("ex", [P, 2, 4, n])
        xl = sb("xl", [P, 2, n])
        rkv = sb("rkv", [P, 3, n])
        staged, loraed, sigmoided, squared, normsum, rooted = (sem("staged"), sem("loraed"), sem("sigmoided"), sem("squared"),
                                                               sem("normsum"), sem("rooted"))
        argued, exped, chain, bonused, summed = sem("argued"), sem("exped"), sem("chain"), sem("bonused"), sem("summed")
        h = S.hcol

        with nc.Block() as block:
            @block.gpsimd
            def _(pool):
                nc.gpsimd.tensor_copy(xl[:, :, :], S.xlora[:, :, bass.ds(tok, n)]).then_inc(staged, 1)
                nc.gpsimd.tensor_copy(rkv[:, :, :], S.prc[:, :, bass.ds(tok, n)]).then_inc(staged, 1)

            @block.tensor
            def _(pe):
                pe.wait_ge(staged, 1)
                for j in range(4):
                    nc.tensor.matmul(S.ps[:, j, 0:n], S.wst[:, j, :], xl[:, 0, :], start=True, stop=True).then_inc(loraed, 1)
                nc.tensor.matmul(S.ps[:, 4, 0:n], S.wst[:, 4, :], xl[:, 1, :], start=True, stop=True).then_inc(loraed, 1)
                pe.wait_ge(squared, 1)
                nc.tensor.matmul(S.ps[:, 5, 0:n], S.cst[:, C_ONES:C_ONES + P], sq[:, :], start=True, stop=True).then_inc(normsum, 1)
                pe.wait_ge(bonused, 1)
                nc.tensor.matmul(S.ps[:, 6, 0:n], S.cst[:, C_ONES:C_ONES + P], kraw[:, :], start=True, stop=True).then_inc(summed, 1)

            @block.scalar
            def _(act):
                for j in range(4):
                    act.wait_ge(loraed, j + 1)
                    nc.scalar.activation((sig if j < 2 else av)[:, j % 2, :], S.ps[:, j, 0:n], ACT.Sigmoid,
                                         bias=h[:, 9 + j:10 + j]).then_inc(sigmoided, 1)
                act.wait_ge(loraed, 5)
                nc.scalar.activation(R.gate[:, bass.ds(tok, n)], S.ps[:, 4, 0:n], ACT.Copy)
                act.wait_ge(normsum, 1)
                nc.scalar.activation(sq[:, :], S.ps[:, 5, 0:n], ACT.Sqrt).then_inc(rooted, 1)
                act.wait_ge(argued, 1)
                args = [[(cinc[:, 0], -1), (y_[:, 0], -1), (cinc[:, 0], 1), (z_[:, 0], -1)],
                        [(w_[:, :], -1), (z_[:, 1], -1), (w_[:, :], 1), (y_[:, 1], -1)]]
                for d in range(2):
                    for e in range(4):
                        a, sign = args[d][e]
                        nc.scalar.activation(ex[:, d, e, :], a, ACT.Exp, scale=sign * DECAY).then_inc(exped, 1)
                    tot = cinc[:, d, :].rearrange("p (c t) -> p c t", t=CH)[:, :, CH - 1:CH]
                    nc.scalar.activation(R.wc[:, d, :].rearrange("p (c o) -> p c o", o=1), tot, ACT.Exp, scale=-DECAY)

            @block.vector
            def _(dve):
                link = Link(dve, chain)
                dve.wait_ge(staged, 2)
                r, k, v = rkv[:, 0, :], rkv[:, 1, :], rkv[:, 2, :]
                link(nc.vector.tensor_scalar(kraw[:, :], k, h[:, 13:14], None, ALU.mult))
                nc.vector.tensor_tensor(sq[:, :], kraw[:, :], kraw[:, :], ALU.mult).then_inc(squared, 1)
                dve.wait_ge(sigmoided, 2)
                for d in range(2):
                    link(nc.vector.tensor_tensor_scan(cinc[:, d, :], S.reset[:, 0:n], sig[:, d, :], 0.0, ALU.mult, ALU.add))
                    nc.vector.tensor_tensor(y_[:, d, :], cinc[:, d, :], sig[:, d, :], ALU.subtract)
                    c4 = cinc[:, d, :].rearrange("p (c t) -> p c t", t=CH)
                    link(nc.vector.tensor_tensor(z_[:, d, :].rearrange("p (c t) -> p c t", t=CH),
                                                 c4[:, :, CH - 1:CH].to_broadcast([P, NC_, CH]), c4, ALU.subtract))
                nc.vector.tensor_tensor(w_[:, :], z_[:, 1, :], sig[:, 1, :], ALU.add).then_inc(argued, 1)
                dve.wait_ge(sigmoided, 4)
                for d in range(2):
                    link(nc.vector.tensor_scalar(keff[:, d, :], av[:, d, :], h[:, 14:15], h[:, 18:19], ALU.mult, ALU.add))
                    link(nc.vector.tensor_tensor(keff[:, d, :], keff[:, d, :], k, ALU.mult))
                dve.wait_ge(rooted, 1)
                link(nc.vector.tensor_scalar(sq[:, :], sq[:, :], 1e-12, None, ALU.max))
                link(nc.vector.reciprocal(sq[:, :], sq[:, :]))
                link(nc.vector.tensor_tensor(kk[:, :], kraw[:, :], sq[:, :], ALU.mult))
                for d in range(2):
                    link(nc.vector.scalar_tensor_tensor(out=nka[:, d, :], in0=kk[:, :], scalar=-1.0, in1=av[:, d, :],
                                                        op0=ALU.mult, op1=ALU.mult))
                link(nc.vector.tensor_tensor(kraw[:, :], keff[:, 0, :], keff[:, 1, :], ALU.add))
                nc.vector.scalar_tensor_tensor(out=kraw[:, :], in0=kraw[:, :], scalar=h[:, 15:16], in1=r,
                                               op0=ALU.mult, op1=ALU.mult).then_inc(bonused, 1)
                for hh in range(2):
                    p0 = hh * CH
                    nc.vector.tensor_copy(R.vbd[p0:p0 + CH, :, p0:p0 + CH], v[p0:p0 + CH, :].rearrange("p (c t) -> p c t", t=CH))
                for d in range(2):
                    terms = ((BA, kk[:, :], E_EX), (BR, r, E_IN), (BB, nka[:, d, :], E_INV), (BK, keff[:, d, :], E_INV),
                             (BBB, nka[:, d, :], E_BAR), (BKB, keff[:, d, :], E_BAR))
                    dve.wait_ge(exped, 4 * d + 4)
                    for which, x, e in terms:
                        for hh in range(2):
                            p0 = hh * CH
                            nc.vector.tensor_tensor(R.bd[d][p0:p0 + CH, which, :, p0:p0 + CH],
                                                    x[p0:p0 + CH, :].rearrange("p (c t) -> p c t", t=CH),
                                                    ex[p0:p0 + CH, d, e, :].rearrange("p (c t) -> p c t", t=CH), ALU.mult)
                dve.wait_ge(summed, 1)
                nc.vector.tensor_tensor(R.bonus[:, bass.ds(tok, n)], S.ps[:, 6, 0:n], v, ALU.mult)
        clear_block(nc, [staged, loraed, sigmoided, squared, normsum, rooted, argued, exped, chain, bonused, summed])


def rwkv_chunks(nc, S, R, tok):
    with ExitStack() as st:
        sem = lambda m: st.enter_context(nc.semaphore("rc_" + m))
        names = ["tn", "An", "Bn", "Kn", "LT", "MbT", "AkT", "MkT", "Et", "Tm", "Z", "F", "G", "U0"]
        M = [{m: st.enter_context(nc.sbuf_tensor(f"rc_{m}{d}", [P, NC_, P], F32)) for m in names[1:]} for d in range(2)]
        Vn = st.enter_context(nc.sbuf_tensor("rc_Vn", [P, NC_, P], F32))
        X = [st.enter_context(nc.sbuf_tensor(f"rc_X{d}", [P, NC_ + 1, P], F32)) for d in range(2)]
        tmp = st.enter_context(nc.sbuf_tensor("rc_tmp", [P, T_CTX], F32))
        turned, turn_cp, grams, masked, leveled = sem("turned"), sem("turn_copied"), sem("grams"), sem("masked"), sem("leveled")
        l0_turned, inv_ready, f_sum, f_copied, tz_sum = sem("l0_turned"), sem("inverse_ready"), sem("f_sum"), sem("f_copied"), sem("tz_sum")
        n1_sum, n1_cp, gu_sum, gu_cp, ph_sum, ph_ready = sem("n1_sum"), sem("n1_copied"), sem("gu_sum"), sem("gu_copied"), sem("ph_sum"), sem("ph_ready")
        x_sum, x_ready, y_sum, chain = sem("x_sum"), sem("x_ready"), sem("y_sum"), sem("chain")
        xinit = sem("x_init")
        ident = S.cst[:, C_ID:C_ID + P]
        order = [list(range(NC_)), list(range(NC_))[::-1]]

        def bank(d, b):
            return S.ps[:, 4 * d + b, :].rearrange("p (c n) -> p c n", n=P)

        def all_chunks(d, b, lhsT, rhs):
            for c in range(NC_):
                last = nc.tensor.matmul(bank(d, b)[:, c, :], lhsT[:, c, :], rhs[:, c, :], start=True, stop=True)
            return last

        with nc.Block() as block:
            @block.tensor
            def _(pe):
                for d in range(2):
                    src = [R.bd[d][:, BA], R.bd[d][:, BBB], R.bd[d][:, BKB]] + ([R.vbd[:, :]] if d == 0 else [])
                    for b, s in enumerate(src):
                        for c in range(NC_):
                            last = nc.tensor.transpose(bank(d, b)[:, c, :], s[:, c, :], ident)
                    last.then_inc(turned, 1)
                for d in range(2):
                    pe.wait_ge(turn_cp, d + 1)
                    all_chunks(d, 0, R.bd[d][:, BB], R.bd[d][:, BA])
                    all_chunks(d, 1, R.bd[d][:, BB], R.bd[d][:, BR])
                    all_chunks(d, 2, R.bd[d][:, BK], R.bd[d][:, BA])
                    all_chunks(d, 3, R.bd[d][:, BK], R.bd[d][:, BR]).then_inc(grams, 1)
                for d in range(2):
                    pe.wait_ge(masked, d + 1)
                    pe.wait_ge(leveled, d + 1)
                    for c in range(NC_):
                        last = nc.tensor.transpose(bank(d, 0)[:, c, :], M[d]["Et"][:, c, :], ident)
                    last.then_inc(l0_turned, 1)
                for n in range(1, 6):
                    for d in range(2):
                        pe.wait_ge(inv_ready, 2 * (n - 1) + d + 1)
                        pe.wait_ge(leveled, 2 * n + d + 1)
                        all_chunks(d, 1, M[d]["Et"], M[d]["Tm"]).then_inc(f_sum, 1)
                    for d in range(2):
                        pe.wait_ge(f_copied, 2 * (n - 1) + d + 1)
                        if n < 5:
                            all_chunks(d, 2, M[d]["Z"], M[d]["F"])
                        all_chunks(d, 3, M[d]["F"], M[d]["Z"]).then_inc(tz_sum, 1)
                for d in range(2):
                    all_chunks(d, 0, M[d]["AkT"], Vn).then_inc(n1_sum, 1)
                for d in range(2):
                    pe.wait_ge(inv_ready, 10 + d + 1)
                    pe.wait_ge(n1_cp, d + 1)
                    all_chunks(d, 1, M[d]["Z"], M[d]["An"])
                    all_chunks(d, 2, M[d]["Z"], M[d]["F"]).then_inc(gu_sum, 1)
                for d in range(2):
                    pe.wait_ge(gu_cp, d + 1)
                    all_chunks(d, 3, M[d]["G"], M[d]["Bn"])
                    all_chunks(d, 0, M[d]["G"], M[d]["MbT"]).then_inc(ph_sum, 1)
                for i in range(NC_):
                    for d in range(2):
                        c = order[d][i]
                        if i >= 2:
                            pe.wait_ge(x_ready, 2 * (i - 2) + d + 1)
                        o = bank(d, 1 + i % 2)[:, 0, :]
                        nc.tensor.matmul(o, M[d]["Bn"][:, c, :], M[d]["U0"][:, c, :], start=True, stop=False)
                        nc.tensor.matmul(o, M[d]["Kn"][:, c, :], Vn[:, c, :], start=False, stop=False)
                        if i == 0:
                            pe.wait_ge(ph_ready, d + 1)
                            pe.wait_ge(xinit, d + 1)
                        else:
                            pe.wait_ge(x_ready, 2 * (i - 1) + d + 1)
                        nc.tensor.matmul(o, M[d]["LT"][:, c, :], X[d][:, i, :], start=False, stop=True).then_inc(x_sum, 1)
                for d in range(2):
                    for i in range(NC_):
                        c = order[d][i]
                        o = bank(d, 3)[:, c, :]
                        nc.tensor.matmul(o, X[d][:, i, :], M[d]["Tm"][:, c, :], start=True, stop=False)
                        nc.tensor.matmul(o, M[d]["U0"][:, c, :], M[d]["MbT"][:, c, :], start=False, stop=False)
                        last = nc.tensor.matmul(o, Vn[:, c, :], M[d]["MkT"][:, c, :], start=False, stop=True)
                    last.then_inc(y_sum, 1)

            @block.scalar
            def _(act):
                for d in range(2):
                    nc.scalar.activation(X[d][:, 0, :], R.last[d][:, :], ACT.Copy).then_inc(xinit, 1)
                for d in range(2):
                    act.wait_ge(turned, d + 1)
                    nc.scalar.activation(M[d]["An"][:, :, :], bank(d, 0), ACT.Copy)
                    nc.scalar.activation(M[d]["Bn"][:, :, :], bank(d, 1), ACT.Copy)
                    last = nc.scalar.activation(M[d]["Kn"][:, :, :], bank(d, 2), ACT.Copy)
                    if d == 0:
                        last = nc.scalar.activation(Vn[:, :, :], bank(d, 3), ACT.Copy)
                    last.then_inc(turn_cp, 1)
                for n in range(1, 6):
                    for d in range(2):
                        act.wait_ge(f_sum, 2 * (n - 1) + d + 1)
                        nc.scalar.activation(M[d]["F"][:, :, :], bank(d, 1), ACT.Copy).then_inc(f_copied, 1)
                for d in range(2):
                    act.wait_ge(n1_sum, d + 1)
                    act.wait_ge(tz_sum, 8 + d + 1)
                    nc.scalar.activation(M[d]["F"][:, :, :], bank(d, 0), ACT.Copy).then_inc(n1_cp, 1)
                for d in range(2):
                    act.wait_ge(gu_sum, d + 1)
                    nc.scalar.activation(M[d]["G"][:, :, :], bank(d, 1), ACT.Copy)
                    nc.scalar.activation(M[d]["U0"][:, :, :], bank(d, 2), ACT.Copy).then_inc(gu_cp, 1)
                for i in range(NC_):
                    for d in range(2):
                        act.wait_ge(x_sum, 2 * i + d + 1)
                        nc.scalar.activation(X[d][:, i + 1, :], bank(d, 1 + i % 2)[:, 0, :], ACT.Copy).then_inc(x_ready, 1)
                act.wait_ge(x_ready, 2 * NC_)
                for d in range(2):
                    nc.scalar.activation(R.last[d][:, :], X[d][:, NC_, :], ACT.Copy)

            @block.gpsimd
            def _(pool):
                for n in range(6):
                    for d in range(2):
                        if n == 0:
                            pool.wait_ge(masked, d + 1)
                        elif n == 1:
                            pool.wait_ge(inv_ready, d + 1)
                        else:
                            pool.wait_ge(f_sum, 2 * (n - 2) + d + 1)
                        lvl = S.cst[:, C_LVL + n * P:C_LVL + (n + 1) * P].unsqueeze(1).to_broadcast([P, NC_, P])
                        nc.gpsimd.tensor_tensor(M[d]["Et"][:, :, :], M[d]["LT"][:, :, :], lvl, ALU.mult).then_inc(leveled, 1)

            @block.vector
            def _(dve):
                link = Link(dve, chain)
                idb = ident.unsqueeze(1).to_broadcast([P, NC_, P])
                for d in range(2):
                    dve.wait_ge(grams, d + 1)
                    for b, (m, inc) in enumerate((("LT", 0), ("MbT", 1), ("AkT", 0), ("MkT", 1))):
                        a = C_MASK + (2 * d + inc) * P
                        last = nc.vector.tensor_tensor(M[d][m][:, :, :], bank(d, b),
                                                       S.cst[:, a:a + P].unsqueeze(1).to_broadcast([P, NC_, P]), ALU.mult)
                    last.then_inc(masked, 1)
                for d in range(2):
                    dve.wait_ge(leveled, d + 1)
                    nc.vector.tensor_tensor(M[d]["Z"][:, :, :], M[d]["Et"][:, :, :], idb, ALU.add)
                    dve.wait_ge(l0_turned, d + 1)
                    nc.vector.tensor_tensor(M[d]["Tm"][:, :, :], bank(d, 0), idb, ALU.add).then_inc(inv_ready, 1)
                for n in range(1, 6):
                    for d in range(2):
                        dve.wait_ge(tz_sum, 2 * (n - 1) + d + 1)
                        dve.wait_ge(inv_ready, 2 * (n - 1) + d + 1)
                        if n < 5:
                            nc.vector.tensor_tensor(M[d]["Tm"][:, :, :], M[d]["Tm"][:, :, :], bank(d, 2), ALU.add)
                        nc.vector.tensor_tensor(M[d]["Z"][:, :, :], M[d]["Z"][:, :, :], bank(d, 3), ALU.add).then_inc(inv_ready, 1)
                for d in range(2):
                    dve.wait_ge(ph_sum, d + 1)
                    for c in range(NC_):
                        nc.vector.scalar_tensor_tensor(out=M[d]["LT"][:, c, :], in0=ident, scalar=R.wc[:, d, c:c + 1],
                                                       in1=bank(d, 3)[:, c, :], op0=ALU.mult, op1=ALU.add)
                    nc.vector.tensor_tensor(M[d]["Tm"][:, :, :], bank(d, 0), R.bd[d][:, BR], ALU.add).then_inc(ph_ready, 1)
                for d in range(2):
                    dve.wait_ge(y_sum, d + 1)
                    both = bank(d, 3).rearrange("p c (h t) -> p c t h", h=2)
                    dst = R.y[:, bass.ds(tok, T_CTX)].rearrange("p (c t) -> p c t", t=CH) if d == 0 else tmp[:, :].rearrange("p (c t) -> p c t", t=CH)
                    link(nc.vector.tensor_reduce(dst, both, AX.X, ALU.add))
                nc.vector.tensor_tensor(R.y[:, bass.ds(tok, T_CTX)], R.y[:, bass.ds(tok, T_CTX)], tmp[:, :], ALU.add)
        clear_block(nc, [turned, turn_cp, grams, masked, leveled, l0_turned, inv_ready, f_sum, f_copied, tz_sum, n1_sum, n1_cp,
                         gu_sum, gu_cp, ph_sum, ph_ready, x_sum, x_ready, y_sum, chain, xinit])


def rwkv_finish(nc, S, R, hp):
    with ExitStack() as st:
        sem = lambda m: st.enter_context(nc.semaphore("rf_" + m))
        sq = st.enter_context(nc.sbuf_tensor("rf_sq", [P, T], F32))
        meaned, centred, squared, vared, rooted, chain = sem("meaned"), sem("centred"), sem("squared"), sem("vared"), sem("rooted"), sem("chain")
        ones = S.cst[:, C_ONES:C_ONES + P]
        with nc.Block() as block:
            @block.tensor
            def _(pe):
                nc.tensor.matmul(S.ps[:, 0, :], ones, R.y[:, :], start=True, stop=True).then_inc(meaned, 1)
                pe.wait_ge(squared, 1)
                nc.tensor.matmul(S.ps[:, 1, :], ones, sq[:, :], start=True, stop=True).then_inc(vared, 1)

            @block.scalar
            def _(act):
                act.wait_ge(centred, 1)
                nc.scalar.activation(sq[:, :], R.y[:, :], ACT.Square).then_inc(squared, 1)
                act.wait_ge(centred, 2)
                nc.scalar.activation(sq[:, :], sq[:, :], ACT.Sqrt).then_inc(rooted, 1)

            @block.vector
            def _(dve):
                link = Link(dve, chain)
                dve.wait_ge(meaned, 1)
                nc.vector.scalar_tensor_tensor(out=R.y[:, :], in0=S.ps[:, 0, :], scalar=-1.0 / CH, in1=R.y[:, :],
                                               op0=ALU.mult, op1=ALU.add).then_inc(centred, 1)
                dve.wait_ge(vared, 1)
                nc.vector.tensor_scalar(sq[:, :], S.ps[:, 1, :], 1.0 / CH, 64e-5, ALU.mult, ALU.add).then_inc(centred, 1)
                dve.wait_ge(rooted, 1)
                link(nc.vector.reciprocal(sq[:, :], sq[:, :]))
                link(nc.vector.tensor_tensor(R.y[:, :], R.y[:, :], sq[:, :], ALU.mult))
                link(nc.vector.tensor_scalar(R.y[:, :], R.y[:, :], S.hcol[:, 16:17], S.hcol[:, 17:18], ALU.mult, ALU.add))
                link(nc.vector.tensor_tensor(R.y[:, :], R.y[:, :], R.bonus[:, :], ALU.add))
                nc.vector.tensor_tensor(S.oT[:, bass.ds(hp + HP, 1), :].rearrange("p o t -> p (o t)"), R.y[:, :], R.gate[:, :], ALU.mult)
        clear_block(nc, [meaned, centred, squared, vared, rooted, chain])


LN_EPS = 1e-5


def post_block(nc, g, S, l, n, blocks, project=None, load_h=False):
    blocks = list(blocks)
    with ExitStack() as st:
        sem = lambda m: st.enter_context(nc.semaphore(f"po{l}{n}_" + m))
        sb = lambda m, s: st.enter_context(nc.sbuf_tensor(f"po{l}{n}_" + m, s, F32))
        gate = sb("gate", [P, 2, D])
        lng, lnb, t_ = sb("ln_g", [P, D]), sb("ln_b", [P, D]), sb("t", [P, 2, D])
        stat, agg, rstd = sb("stat", [P, NB, 2, 6]), sb("agg", [P, NB, 2]), sb("rstd", [P, NB])
        wout = sb("w_out", [P, 2, KD, 512]) if project is not None else None
        hl, lnl, wl = sem("h_loaded"), sem("ln_loaded"), [sem("w_loaded0"), sem("w_loaded1")]
        gsum, gcp, proj, chain, vared, rooted, used, normed = (sem("gate_sum"), sem("gate_copied"), sem("projected"), sem("chain"),
                                                               sem("vared"), sem("rooted"), sem("used"), sem("normed"))
        gidx = 2 if n == 0 else 5
        sides = [0, 1] if blocks[0] == 0 else [1]
        with phase(nc, [hl, lnl, *wl, gsum, gcp, proj, chain, vared, rooted, used, normed]) as block:
            @block.sync
            def _(sp):
                if project is not None:
                    for hf in range(2):
                        sp.dma_start(wout[:, hf], project.rearrange("(k p) n -> p k n", p=P)[:, :, hf * 512:(hf + 1) * 512]).then_inc(wl[hf], 16)
                if load_h:
                    load_tokens(sp, g, S.h, hl)
                sp.dma_start(lng[:, :], g.ln_g[l, n:n + 1, :].to_broadcast([P, D])).then_inc(lnl, 16)
                sp.dma_start(lnb[:, :], g.ln_b[l, n:n + 1, :].to_broadcast([P, D])).then_inc(lnl, 16)

            @block.tensor
            def _(pe):
                for side in sides:
                    for k in range(KD):
                        col = S.mcol[:, l, 1 - side, gidx * KD + k:gidx * KD + k + 1]
                        last = nc.tensor.matmul(S.ps[:, 4 + 2 * side + k // 4, (k % 4) * P:(k % 4 + 1) * P],
                                                col.to_broadcast([P, P]), S.cst[:, C_ID:C_ID + P], start=True, stop=True)
                last.then_inc(gsum, 1)
                if project is not None:
                    pe.wait_ge(wl[0], 16)
                    pe.wait_ge(wl[1], 16)
                    for i, b in enumerate(blocks):
                        if i >= 2:
                            pe.wait_ge(used, i - 1)
                        for hf in range(2):
                            for k in range(KD):
                                last = nc.tensor.matmul(S.ps[:, 2 * (i % 2) + hf, :], S.oT[:, k, b * P:(b + 1) * P],
                                                        wout[:, hf, k, :], start=(k == 0), stop=(k == KD - 1))
                        last.then_inc(proj, 1)

            @block.scalar
            def _(act):
                act.wait_ge(gsum, 1)
                for side in sides:
                    nc.scalar.activation(gate[:, side, :].rearrange("p (a n) -> p a n", a=2),
                                         S.ps[:, 4 + 2 * side:6 + 2 * side, :], ACT.Copy).then_inc(gcp, 1)
                for i in range(len(blocks)):
                    act.wait_ge(vared, i + 1)
                    nc.scalar.activation(rstd[:, i:i + 1], agg[:, i, 1:2], ACT.Sqrt).then_inc(rooted, 1)

            @block.vector
            def _(dve):
                link = Link(dve, chain)
                dve.wait_ge(gcp, len(sides))
                if load_h:
                    dve.wait_ge(hl, 32)
                for i, b in enumerate(blocks):
                    t = t_[:, i % 2, :]
                    if project is not None:
                        dve.wait_ge(proj, i + 1)
                        y = S.ps[:, 2 * (i % 2):2 * (i % 2) + 2, :]
                    else:
                        y = S.acc[:, b, :].rearrange("p (a n) -> p a n", a=2)
                    nc.vector.tensor_tensor(t.rearrange("p (a n) -> p a n", a=2), y,
                                            gate[:, b // 2, :].rearrange("p (a n) -> p a n", a=2), ALU.mult).then_inc(used, 1)
                    dve.wait_ge(used, i + 1)
                    link(nc.vector.scalar_tensor_tensor(out=t, in0=S.h[:, b, :], scalar=ALPHA, in1=t, op0=ALU.mult, op1=ALU.add))
                    for a in range(2):
                        last = nc.vector.bn_stats(stat[:, i, a, :], t[:, a * 512:(a + 1) * 512])
                        link(last)
                    link(nc.vector.bn_aggr(agg[:, i, :], stat[:, i, :, :].rearrange("p a s -> p (a s)")))
                    nc.vector.tensor_scalar(agg[:, i, 1:2], agg[:, i, 1:2], LN_EPS, None, ALU.add).then_inc(vared, 1)
                    dve.wait_ge(rooted, i + 1)
                    link(nc.vector.reciprocal(rstd[:, i:i + 1], rstd[:, i:i + 1]))
                    nc.vector.tensor_scalar(S.h[:, b, :], t, agg[:, i, 0:1], rstd[:, i:i + 1], ALU.subtract, ALU.mult).then_inc(normed, 1)

            @block.gpsimd
            def _(pool):
                pool.wait_ge(lnl, 32)
                for i, b in enumerate(blocks):
                    pool.wait_ge(normed, i + 1)
                    nc.gpsimd.tensor_tensor(S.h[:, b, :], S.h[:, b, :], lng[:, :], ALU.mult).then_inc(hl, 1)
                    pool.wait_ge(hl, (32 if load_h else 0) + i + 1)
                    nc.gpsimd.tensor_tensor(S.h[:, b, :], S.h[:, b, :], lnb[:, :], ALU.add)


def router_block(nc, g, S, l, blocks):
    blocks = list(blocks)
    nb = len(blocks)
    with ExitStack() as st:
        sem = lambda m: st.enter_context(nc.semaphore(f"ro{l}_" + m))
        sb = lambda m, s: st.enter_context(nc.sbuf_tensor(f"ro{l}_" + m, s, F32))
        s_, sel, pair, cmp_, rank = (sb("s", [P, nb, 4, 4]), sb("sel", [P, nb, 4, 4]), sb("pair", [P, nb, 4]), sb("cmp", [P, nb, 4, 4]),
                                     sb("rank", [P, nb, 4, 4]))
        top, grank, gcmp, tot = sb("top", [P, nb, 4]), sb("grank", [P, nb, 4]), sb("gcmp", [P, nb, 4]), sb("tot", [P, nb])
        chosen, most = sb("chosen", [P, nb, N_EXP]), sb("most", [P, 3 + N_ITEM])
        cnt, tmp = sb("counts", [P, 3, N_EXP]), sb("tmp", [P, N_ITEM, N_EXP])
        row, rest, most2 = sb("row", [P, nb, N_EXP]), sb("rest", [P, nb, N_EXP]), sb("most2", [P, 2, nb])
        scored, sgm, chain, picked, counted = sem("scored"), sem("sigmoided"), sem("chain"), sem("picked"), sem("counted")
        block = st.enter_context(phase(nc, [scored, sgm, chain, picked, counted]))

        @block.tensor
        def _(pe):
            for i, b in enumerate(blocks):
                for k in range(KD):
                    last = nc.tensor.matmul(S.ps[:, 0, i * N_EXP:(i + 1) * N_EXP], S.uT[:, k, b * P:(b + 1) * P], S.router[:, k, :],
                                            start=(k == 0), stop=(k == KD - 1))
            last.then_inc(scored, 1)
            pe.wait_ge(picked, 1)
            for i in range(nb):
                for j in range(i + 1):
                    m = C_TRI if j == i else C_ALL
                    nc.tensor.matmul(S.ps[:, 1, i * N_EXP:(i + 1) * N_EXP], S.cst[:, m:m + P], chosen[:, j, :], start=(j == 0), stop=(j == i))
            for j in range(nb):
                last = nc.tensor.matmul(S.ps[:, 2, 0:N_EXP], S.cst[:, C_ALL:C_ALL + P], chosen[:, j, :], start=(j == 0), stop=(j == nb - 1))
            last.then_inc(counted, 1)

        @block.scalar
        def _(act):
            act.wait_ge(scored, 1)
            nc.scalar.activation(s_[:, :, :, :], S.ps[:, 0, 0:nb * N_EXP].rearrange("p (b g e) -> p b g e", g=4, e=4),
                                 ACT.Sigmoid).then_inc(sgm, 1)

        @block.vector
        def _(dve):
            link = Link(dve, chain)
            dve.wait_ge(sgm, 1)
            flat = lambda t: t[:, :, :, :].rearrange("p b g e -> p b (g e)")
            link(nc.vector.tensor_tensor(flat(sel), flat(s_), S.rbias[:, :].unsqueeze(1).to_broadcast([P, nb, N_EXP]), ALU.add))
            first = True
            for i in range(4):
                for j in range(i + 1, 4):
                    o = top if first else pair
                    link(nc.vector.tensor_tensor(o[:, :, :], sel[:, :, :, i], sel[:, :, :, j], ALU.add))
                    if not first:
                        link(nc.vector.tensor_tensor(top[:, :, :], top[:, :, :], pair[:, :, :], ALU.max))
                    first = False
            link(nc.vector.memset(grank[:, :, :], 0.0))
            link(nc.vector.memset(rank[:, :, :, :], 0.0))
            for j in range(4):
                for lo, hi, op in ((0, j, ALU.is_gt), (j + 1, 4, ALU.is_ge)):
                    if hi > lo:
                        w = hi - lo
                        link(nc.vector.tensor_tensor(gcmp[:, :, lo:hi], top[:, :, j:j + 1].to_broadcast([P, nb, w]), top[:, :, lo:hi], op))
                        link(nc.vector.tensor_tensor(grank[:, :, lo:hi], grank[:, :, lo:hi], gcmp[:, :, lo:hi], ALU.add))
                        link(nc.vector.tensor_tensor(cmp_[:, :, :, lo:hi], sel[:, :, :, j:j + 1].to_broadcast([P, nb, 4, w]),
                                                     sel[:, :, :, lo:hi], op))
                        link(nc.vector.tensor_tensor(rank[:, :, :, lo:hi], rank[:, :, :, lo:hi], cmp_[:, :, :, lo:hi], ALU.add))
            link(nc.vector.tensor_scalar(grank[:, :, :], grank[:, :, :], 0.5, None, ALU.is_lt))
            link(nc.vector.tensor_scalar(rank[:, :, :, :], rank[:, :, :, :], 1.5, None, ALU.is_lt))
            link(nc.vector.tensor_tensor(rank[:, :, :, :], rank[:, :, :, :], grank[:, :, :].unsqueeze(3).to_broadcast([P, nb, 4, 4]), ALU.mult))
            nc.vector.tensor_copy(chosen[:, :, :], flat(rank)).then_inc(picked, 1)
            dve.wait_ge(picked, 1)
            link(nc.vector.tensor_tensor(flat(rank), flat(rank), flat(s_), ALU.mult))
            link(nc.vector.tensor_reduce(tot[:, :], flat(rank), AX.X, ALU.add))
            link(nc.vector.reciprocal(tot[:, :], tot[:, :]))
            nc.vector.tensor_tensor(S.combine[:, blocks[0]:blocks[-1] + 1, :], flat(rank), tot[:, :].unsqueeze(2).to_broadcast([P, nb, N_EXP]), ALU.mult)
            dve.wait_ge(counted, 1)
            place = S.place[:, blocks[0]:blocks[-1] + 1, :]
            link(nc.vector.scalar_tensor_tensor(out=place, in0=S.ps[:, 1, 0:nb * N_EXP].rearrange("p (b e) -> p b e", b=nb), scalar=1.0,
                                                in1=chosen[:, :, :], op0=ALU.add, op1=ALU.mult))
            link(nc.vector.tensor_scalar(place, place, -1.0, None, ALU.add))
            n_, first_, last_ = cnt[:, 0, :], cnt[:, 1, :], cnt[:, 2, :]
            link(nc.vector.tensor_scalar(n_, S.ps[:, 2, 0:N_EXP], 0.5, None, ALU.is_gt))
            for r in range(1, nb):
                link(nc.vector.tensor_scalar(first_, S.ps[:, 2, 0:N_EXP], r * P + 0.5, None, ALU.is_gt))
                link(nc.vector.tensor_tensor(n_, n_, first_, ALU.add))
            link(nc.vector.tensor_tensor_scan(last_, S.cst[:, C_ALL:C_ALL + N_EXP], n_, 0.0, ALU.mult, ALU.add))
            link(nc.vector.tensor_tensor(first_, last_, n_, ALU.subtract))
            link(nc.vector.tensor_scalar(first_, first_, float(P), None, ALU.mult))
            link(nc.vector.tensor_tensor(row[:, :, :], place, first_.unsqueeze(1).to_broadcast([P, nb, N_EXP]), ALU.add))
            link(nc.vector.tensor_scalar(rest[:, :, :], row[:, :, :], -1.0, float(ROWS), ALU.mult, ALU.add))
            link(nc.vector.tensor_tensor(rest[:, :, :], rest[:, :, :], chosen[:, :, :], ALU.mult))
            link(nc.vector.scalar_tensor_tensor(out=row[:, :, :], in0=row[:, :, :], scalar=1.0, in1=chosen[:, :, :], op0=ALU.add, op1=ALU.mult))
            for n, r in ((0, row), (1, rest)):
                best = most2[:, n, :]
                link(nc.vector.tensor_reduce(best, r[:, :, :], AX.X, ALU.max))
                link(nc.vector.tensor_tensor(r[:, :, :], r[:, :, :], best.unsqueeze(2).to_broadcast([P, nb, N_EXP]), ALU.is_equal))
                link(nc.vector.tensor_tensor(r[:, :, :], r[:, :, :], S.combine[:, blocks[0]:blocks[-1] + 1, :], ALU.mult))
                link(nc.vector.tensor_reduce(S.two_gates[:, n, blocks[0]:blocks[-1] + 1], r[:, :, :], AX.X, ALU.add))
            link(nc.vector.tensor_scalar(most2[:, 0, :], most2[:, 0, :], -1.0, None, ALU.add))
            link(nc.vector.tensor_scalar(most2[:, 1, :], most2[:, 1, :], -1.0, float(ROWS), ALU.mult, ALU.add))
            nc.vector.tensor_copy(S.two_rows[:, :, blocks[0]:blocks[-1] + 1], most2[:, :, :])
            link(nc.vector.tensor_tensor(tmp[:, :, :], S.cst[:, C_JIDX:C_JIDX + N_ITEM].unsqueeze(2).to_broadcast([P, N_ITEM, N_EXP]),
                                         last_.unsqueeze(1).to_broadcast([P, N_ITEM, N_EXP]), ALU.is_ge))
            link(nc.vector.tensor_reduce(most[:, 3:3 + N_ITEM], tmp[:, :, :], AX.X, ALU.add))
            link(nc.vector.tensor_scalar(most[:, 3:3 + N_ITEM], most[:, 3:3 + N_ITEM], float(N_EXP - 1), None, ALU.min))
            nc.vector.tensor_copy(S.item_expert[:, :], most[:, 3:3 + N_ITEM])
            link(nc.vector.memset(most[:, 1:2], 1.0))
            for r in range(1, (N_ITEM - 2) // 2):
                link(nc.vector.tensor_scalar(most[:, 2:3], cnt[:, 2, N_EXP - 1:N_EXP], 2 * r + 0.5, None, ALU.is_gt))
                link(nc.vector.tensor_tensor(most[:, 1:2], most[:, 1:2], most[:, 2:3], ALU.add))
            nc.vector.tensor_copy(S.pairs[:, :], most[:, 1:2])


def dispatch_block(nc, g, S, l, blocks):
    blocks = list(blocks)
    with ExitStack() as st:
        turned, copied, sent = [st.enter_context(nc.semaphore(f"tm{l}_{m}")) for m in ("turned", "copied", "sent")]
        uN = st.enter_context(nc.sbuf_tensor(f"tm{l}_tokens", [P, NB, D], F32))
        block = st.enter_context(phase(nc, [turned, copied, sent]))
        jobs = [(b, k4) for b in blocks for k4 in range(KD // 4)]

        @block.tensor
        def _(pe):
            for j, (b, k4) in enumerate(jobs):
                if j >= 4:
                    pe.wait_ge(copied, j - 3)
                for k in range(4):
                    last = nc.tensor.transpose(S.ps[:, j % 4, k * P:(k + 1) * P], S.uT[:, k4 * 4 + k, b * P:(b + 1) * P],
                                               S.cst[:, C_ID:C_ID + P])
                last.then_inc(turned, 1)

        @block.scalar
        def _(act):
            for j, (b, k4) in enumerate(jobs):
                act.wait_ge(turned, j + 1)
                nc.scalar.activation(uN[:, b, k4 * 512:(k4 + 1) * 512], S.ps[:, j % 4, :], ACT.Copy).then_inc(copied, 1)

        @block.gpsimd
        def _(pool):
            for i, b in enumerate(blocks):
                pool.wait_ge(copied, 2 * (i + 1))
                for n in range(2):
                    nc.gpsimd.indirect_dma_start(out=g.item_x[:, :], out_offset=bass.IndirectOffsetOnAxis(ap=S.two_rows[:, n, b:b + 1], axis=0),
                                                 in_=uN[:, b, :], in_offset=None).then_inc(sent, 16)
            pool.wait_ge(sent, 16 * 2 * len(blocks))


def combine_block(nc, g, S, l, blocks):
    blocks = list(blocks)
    with ExitStack() as st:
        got, first, chain = [st.enter_context(nc.semaphore(f"cb{l}_{m}")) for m in ("got", "first_done", "chain")]
        yg = st.enter_context(nc.sbuf_tensor(f"cb{l}_y", [P, len(blocks), 2, D], F32))
        block = st.enter_context(phase(nc, [got, first]))

        @block.gpsimd
        def _(pool):
            for i, b in enumerate(blocks):
                for n in range(2):
                    if i or n:
                        pool.wait_ge(got, 16 * (2 * i + n))
                    nc.gpsimd.indirect_dma_start(out=yg[:, i, n, :], out_offset=None, in_=g.item_y[:, :],
                                                 in_offset=bass.IndirectOffsetOnAxis(ap=S.two_rows[:, n, b:b + 1], axis=0)).then_inc(got, 16)

        @block.vector
        def _(dve):
            for i, b in enumerate(blocks):
                dve.wait_ge(got, 16 * (2 * i + 2))
                nc.vector.tensor_scalar(S.acc[:, b, :], yg[:, i, 0, :], S.two_gates[:, 0, b:b + 1], None, ALU.mult).then_inc(first, 1)
                dve.wait_ge(first, i + 1)
                nc.vector.scalar_tensor_tensor(out=S.acc[:, b, :], in0=yg[:, i, 1, :], scalar=S.two_gates[:, 1, b:b + 1], in1=S.acc[:, b, :],
                                               op0=ALU.mult, op1=ALU.add)


def moe(nc, g, S, l):
    FC = D_EXP // P
    with ExitStack() as st:
        sem = lambda m: st.enter_context(nc.semaphore(f"mo{l}_" + m))
        sb = lambda m, s: st.enter_context(nc.sbuf_tensor(f"mo{l}_" + m, s, F32))
        wg, wu, wd = sb("w_gate", [P, 2, KD, D_EXP]), sb("w_up", [P, 2, KD, D_EXP]), sb("w_down", [P, 2, FC, D])
        xN, xT, y = sb("xN", [P, 2, D]), sb("xT", [P, 2, KD, P]), sb("y", [P, 2, D])
        he, heT, sg = sb("he", [P, D_EXP]), sb("heT", [P, FC, P]), sb("silu", [P, D_EXP])
        gfull, dfull = [sem(f"gate_up_full{x}") for x in range(2)], [sem(f"down_full{x}") for x in range(2)]
        stored = [sem(f"y_stored{x}") for x in range(2)]
        xfull1 = sem("x_full1")
        names = ["x_full0", "xt_ready", "xt_copied", "gate_ready", "up_ready", "silu_done", "he_done", "het_ready", "het_copied",
                 "y_ready", "y_copied"]
        sems = [sem(m) for m in names]
        (xfull0, xt_ready, xt_copied, gate_ready, up_ready, silu_done, he_done, het_ready, het_copied, y_ready, y_copied) = sems
        xfull = [xfull0, xfull1]
        ident = S.cst[:, C_ID:C_ID + P]
        src = [w[l].rearrange("e (k p) n -> e p k n", p=P) for w in (g.exp_w_gate, g.exp_w_up, g.exp_w_down)]

        def load_gate_up(eng, x, e):
            for w, dst in ((0, wg), (1, wu)):
                eng.dma_start(dst[:, x], src[w][bass.ds(e, 1)].rearrange("o p k n -> p (o k) n")).then_inc(gfull[x], 16)

        def load_down(eng, x, e):
            eng.dma_start(wd[:, x], src[2][bass.ds(e, 1)].rearrange("o p k n -> p (o k) n")).then_inc(dfull[x], 16)

        def load_x(eng, x, item):
            eng.dma_start(xN[:, x, :], g.item_x[bass.ds(item * P, P), :]).then_inc(xfull[x], 16)

        def expert_of(eng, item):
            return eng.value_load(S.item_expert[0:1, bass.ds(item, 1)], min_val=0, max_val=N_EXP - 1)

        def turn_x(pe, n, buf):
            pe.wait_ge(xfull[buf], 16)
            for hf in range(2):
                for k in range(4):
                    last = nc.tensor.transpose(S.ps[:, 2 + 2 * n + hf, k * P:(k + 1) * P],
                                               xN[:, buf, (4 * hf + k) * P:(4 * hf + k + 1) * P], ident)
                last.then_inc(xt_ready, 1)

        def take_xt(act, n, buf):
            for hf in range(2):
                act.wait_ge(xt_ready, 2 * n + hf + 1)
                nc.scalar.activation(xT[:, buf, 4 * hf:4 * hf + 4, :], S.ps[:, 2 + 2 * n + hf, :].rearrange("p (k t) -> p k t", t=P),
                                     ACT.Copy).then_inc(xt_copied, 1)

        with phase(nc, sems) as block:
            @block.sync
            def _(sp):
                for x in range(2):
                    e = expert_of(sp, x)
                    load_x(sp, x, x)
                    load_gate_up(sp, x, e)
                    load_down(sp, x, e)

            @block.gpsimd
            def _(pool):
                nc.gpsimd.memset(y[:, :, :], 0.0).then_inc(y_ready, 1)

            @block.tensor
            def _(pe):
                turn_x(pe, 0, 0)

            @block.scalar
            def _(act):
                act.wait_ge(y_ready, 1)
                for x in range(2):
                    act.dma_start(g.item_y[(N_ITEM - 2 + x) * P:(N_ITEM - 1 + x) * P, :], y[:, x, :]).then_inc(stored[x], 16)
                take_xt(act, 0, 0)

        pairs = nc.values_load(S.pairs[0:1, 0:1], min_val=1, max_val=(N_ITEM - 2) // 2)
        with nc.Fori(0, pairs) as it:
            with phase(nc, sems) as block:
                @block.sync
                def _(sp):
                    load_x(sp, 0, it * 2 + 2)
                    for x in range(2):
                        e = expert_of(sp, it * 2 + (x + 2))
                        sp.wait_ge(up_ready, x + 1)
                        sp.sem_clear(gfull[x])
                        load_gate_up(sp, x, e)
                        if x == 0:
                            sp.wait_ge(xt_ready, 2)
                            sp.sem_clear(xfull[1])
                            load_x(sp, 1, it * 2 + 3)
                        sp.wait_ge(y_ready, 2 * (x + 1))
                        sp.sem_clear(dfull[x])
                        load_down(sp, x, e)

                @block.tensor
                def _(pe):
                    for x in range(2):
                        pe.wait_ge(gfull[x], 32)
                        if x:
                            pe.wait_ge(xt_copied, 2)
                            pe.wait_ge(he_done, 1)
                        for bank, w, rdy in ((0, wg, gate_ready), (1, wu, up_ready)):
                            for k in range(KD):
                                last = nc.tensor.matmul(S.ps[:, bank, :], xT[:, x, k, :], w[:, x, k, :], start=(k == 0), stop=(k == KD - 1))
                            last.then_inc(rdy, 1)
                        turn_x(pe, x, 1 - x)
                        pe.wait_ge(he_done, x + 1)
                        if x:
                            pe.wait_ge(y_copied, 2)
                        for f in range(FC):
                            last = nc.tensor.transpose(S.ps[:, 6, f * P:(f + 1) * P], he[:, f * P:(f + 1) * P], ident)
                        last.then_inc(het_ready, 1)
                        pe.wait_ge(het_copied, x + 1)
                        pe.wait_ge(dfull[x], 16)
                        for hf in range(2):
                            for f in range(FC):
                                last = nc.tensor.matmul(S.ps[:, 7 - hf, :], heT[:, f, :], wd[:, x, f, hf * 512:(hf + 1) * 512],
                                                        start=(f == 0), stop=(f == FC - 1))
                            last.then_inc(y_ready, 1)

                @block.scalar
                def _(act):
                    for x in range(2):
                        act.wait_ge(gate_ready, x + 1)
                        if x:
                            act.wait_ge(he_done, x)
                        nc.scalar.activation(sg[:, :], S.ps[:, 0, :], ACT.Silu).then_inc(silu_done, 1)
                        act.wait_ge(het_ready, x + 1)
                        if x:
                            act.wait_ge(y_ready, 2 * x)
                        nc.scalar.activation(heT[:, :, :], S.ps[:, 6, :].rearrange("p (f t) -> p f t", t=P), ACT.Copy).then_inc(het_copied, 1)
                        take_xt(act, x, 1 - x)
                        act.wait_ge(stored[x], 16)
                        act.sem_clear(stored[x])
                        for hf in range(2):
                            act.wait_ge(y_ready, 2 * x + hf + 1)
                            nc.scalar.activation(y[:, x, hf * 512:(hf + 1) * 512], S.ps[:, 7 - hf, :], ACT.Copy).then_inc(y_copied, 1)
                        act.wait_ge(y_copied, 2 * x + 2)
                        act.dma_start(g.item_y[bass.ds((it * 2 + x) * P, P), :], y[:, x, :]).then_inc(stored[x], 16)

                @block.vector
                def _(dve):
                    for x in range(2):
                        dve.wait_ge(silu_done, x + 1)
                        dve.wait_ge(up_ready, x + 1)
                        if x:
                            dve.wait_ge(het_ready, x)
                        nc.vector.tensor_tensor(he[:, :], sg[:, :], S.ps[:, 1, :], ALU.mult).then_inc(he_done, 1)

        with nc.Block() as block:
            @block.sync
            def _(sp):
                sp.wait_ge(xfull[1], 16)
                for x in range(2):
                    sp.wait_ge(stored[x], 16)
                    sp.wait_ge(gfull[x], 32)
                    sp.wait_ge(dfull[x], 16)
        clear_block(nc, gfull + dfull + stored + [xfull1])


def odd_mixer(nc, g, S, l):
    n = T_LAT
    with ExitStack() as st:
        sem = lambda m: st.enter_context(nc.semaphore("da_" + m))
        sb = lambda m, s: st.enter_context(nc.sbuf_tensor("da_" + m, s, F32))
        slab, rope = sb("slab", [P, 3, KD, P]), sb("rope", [P, 2, n])
        lvec, lprod, lam, subln = sb("lambda_vectors", [P, 4, HD]), sb("lprod", [P, HD]), sb("lam", [P, 4]), sb("subln", [P, P])
        qraw, kraw, q, k, v = sb("qraw", [P, n]), sb("kraw", [P, T]), sb("q", [P, n]), sb("k", [P, T]), sb("v", [P, NB, P])
        rt = sb("rotated", [P, 2, n])
        p_, a_, aT, o_ = sb("p", [P, 2, 2, T]), sb("a", [P, 2, T]), sb("aT", [P, 2, NB, P]), sb("o", [P, 2, P])
        junk = sb("junk", [P, P])
        nmax, ssum, rsum, ss, rt_, inv = sb("nmax", [P, 4]), sb("ssum", [P, 4]), sb("rsum", [P, 4]), sb("ss", [P, 2]), sb("root", [P, 2]), sb("inv", [P, 2])
        full = sem("slab_full")
        src = g.odd_w_in[0].rearrange("(k p) n -> p k n", p=P)

        def load(sp, h):
            for j in range(3):
                sp.dma_start(slab[:, j], src[:, :, bass.ds(h * P + j * 2 * DA_H * HD, P)]).then_inc(full, 16)

        once, summed_l, exped_l, ch0 = sem("once"), sem("lambda_sums"), sem("lambda_exps"), sem("lchain")
        with nc.Block() as block:
            @block.sync
            def _(sp):
                load(sp, 0)
                sp.dma_start(rope[:, :, :], g.rope.rearrange("p (a t) -> p a t", a=2)).then_inc(once, 16)
                for i, x in enumerate((g.da_lq1, g.da_lk1, g.da_lq2, g.da_lk2)):
                    sp.dma_start(lvec[:, i, :], x[0:1, :].to_broadcast([P, HD])).then_inc(once, 16)
                sp.dma_start(subln[:, :], g.da_subln_g[0:1, :].to_broadcast([P, P])).then_inc(once, 16)

            @block.vector
            def _(dve):
                link = Link(dve, ch0)
                dve.wait_ge(once, 16 * 6)
                for i in range(2):
                    link(nc.vector.tensor_tensor(lprod[:, :], lvec[:, 2 * i, :], lvec[:, 2 * i + 1, :], ALU.mult))
                    nc.vector.tensor_reduce(lam[:, i:i + 1], lprod[:, :], AX.X, ALU.add).then_inc(summed_l, 1)
                    dve.wait_ge(summed_l, i + 1)
                link(nc.vector.tensor_scalar(subln[:, :], subln[:, :], 2.0 * (1.0 - LAMBDA_INIT), None, ALU.mult))
                dve.wait_ge(exped_l, 1)
                link(nc.vector.tensor_tensor(lam[:, 2:3], lam[:, 0:1], lam[:, 1:2], ALU.subtract))
                link(nc.vector.tensor_scalar(lam[:, 3:4], lam[:, 2:3], LAMBDA_INIT, None, ALU.add))

            @block.scalar
            def _(act):
                act.wait_ge(summed_l, 2)
                nc.scalar.activation(lam[:, 0:2], lam[:, 0:2], ACT.Exp).then_inc(exped_l, 1)

        clear_block(nc, [once, summed_l, exped_l, ch0])
        names = ["ready", "raw", "turned", "mixed", "staged", "scored", "maxed", "exped", "diffed", "a_turned", "a_copied", "summed",
                 "squared", "scaled", "rooted", "normed", "o_turned", "chain"]
        (ready, raw, turned, mixed, staged, scored, maxed, exped, diffed, a_turned, a_copied, summed, squared, scaled, rooted,
         normed, o_turned, chain) = [sem(m) for m in names]
        ident = S.cst[:, C_ID:C_ID + P]

        def body(h, prefetch):
            with nc.Block() as block:
                @block.sync
                def _(sp):
                    sp.wait_ge(ready, 3)
                    sp.sem_clear(full)
                    if prefetch:
                        load(sp, h + 1)

                @block.tensor
                def _(pe):
                    pe.wait_ge(full, 16 * 3)
                    for kk in range(KD):
                        last = nc.tensor.matmul(S.ps[:, 0, 0:n], slab[:, 0, kk, :], S.uT[:, kk, T_CTX:T], start=(kk == 0), stop=(kk == KD - 1))
                    last.then_inc(ready, 1)
                    for kk in range(KD):
                        last = nc.tensor.matmul(S.ps[:, 1, :], slab[:, 1, kk, :], S.uT[:, kk, :], start=(kk == 0), stop=(kk == KD - 1))
                    last.then_inc(ready, 1)
                    for b in range(NB):
                        for kk in range(KD):
                            last = nc.tensor.matmul(S.ps[:, 2, b * P:(b + 1) * P], S.uT[:, kk, b * P:(b + 1) * P], slab[:, 2, kk, :],
                                                    start=(kk == 0), stop=(kk == KD - 1))
                    last.then_inc(ready, 1)
                    rot = S.cst[:, C_ROT:C_ROT + P]
                    pe.wait_ge(raw, 1)
                    nc.tensor.matmul(S.ps[:, 3, 0:n], rot, qraw[:, :], start=True, stop=True).then_inc(turned, 1)
                    pe.wait_ge(raw, 2)
                    nc.tensor.matmul(S.ps[:, 4, 0:n], rot, kraw[:, T_CTX:T], start=True, stop=True).then_inc(turned, 1)
                    pe.wait_ge(staged, 1)
                    pe.wait_ge(mixed, 2)
                    for u in range(2):
                        for m in range(2):
                            nc.tensor.matmul(S.ps[:, 2 * u + m, :], q[m * HD:(m + 1) * HD, u * P:(u + 1) * P], k[m * HD:(m + 1) * HD, :],
                                             start=True, stop=True).then_inc(scored, 1)
                    for u in range(2):
                        pe.wait_ge(diffed, u + 1)
                        for b in range(NB):
                            last = nc.tensor.transpose(S.ps[:, 4 + u, b * P:(b + 1) * P], a_[:, u, b * P:(b + 1) * P], ident)
                        last.then_inc(a_turned, 1)
                    for u in range(2):
                        pe.wait_ge(a_copied, u + 1)
                        for b in range(NB):
                            last = nc.tensor.matmul(S.ps[:, 6 + u, 0:P], aT[:, u, b, :], v[:, b, :], start=(b == 0), stop=(b == NB - 1))
                        last.then_inc(summed, 1)
                    for u in range(2):
                        pe.wait_ge(normed, u + 1)
                        nc.tensor.transpose(S.ps[:, 4 + u, 0:P], o_[:, u, :], ident).then_inc(o_turned, 1)

                @block.scalar
                def _(act):
                    act.wait_ge(ready, 1)
                    nc.scalar.activation(qraw[:, :], S.ps[:, 0, 0:n], ACT.Copy).then_inc(raw, 1)
                    act.wait_ge(ready, 2)
                    nc.scalar.activation(kraw[:, :], S.ps[:, 1, :], ACT.Copy).then_inc(raw, 1)
                    act.wait_ge(ready, 3)
                    nc.scalar.activation(v[:, :, :], S.ps[:, 2, :].rearrange("p (b e) -> p b e", b=NB), ACT.Copy).then_inc(staged, 1)
                    for j in range(4):
                        act.wait_ge(maxed, j + 1)
                        nc.scalar.activation(p_[:, j // 2, j % 2, :], S.ps[:, j, :], ACT.Exp, bias=nmax[:, j:j + 1], scale=NA_SCALE,
                                             accum_out=ssum[:, j:j + 1]).then_inc(exped, 1)
                    for u in range(2):
                        act.wait_ge(a_turned, u + 1)
                        nc.scalar.activation(aT[:, u, :, :], S.ps[:, 4 + u, :].rearrange("p (b q) -> p b q", b=NB), ACT.Copy).then_inc(a_copied, 1)
                    for u in range(2):
                        act.wait_ge(summed, u + 1)
                        if u:
                            act.wait_ge(squared, 1)
                        nc.scalar.activation(junk[:, :], S.ps[:, 6 + u, 0:P], ACT.Square, accum_out=ss[:, u:u + 1]).then_inc(squared, 1)
                        act.wait_ge(scaled, u + 1)
                        nc.scalar.activation(rt_[:, u:u + 1], ss[:, u:u + 1], ACT.Sqrt).then_inc(rooted, 1)
                    for u in range(2):
                        act.wait_ge(o_turned, u + 1)
                        nc.scalar.activation(S.oT[:, bass.ds(h, 1), T_CTX + u * P:T_CTX + (u + 1) * P].rearrange("p o t -> p (o t)"),
                                             S.ps[:, 4 + u, 0:P], ACT.Copy)

                @block.vector
                def _(dve):
                    link = Link(dve, chain)
                    for i, (r, t, out) in enumerate(((qraw[:, :], 0, q[:, :]), (kraw[:, T_CTX:T], 1, k[:, T_CTX:T]))):
                        dve.wait_ge(turned, i + 1)
                        if i:
                            nc.vector.tensor_copy(k[:, 0:T_CTX], kraw[:, 0:T_CTX])
                        nc.vector.tensor_tensor(rt[:, t, :], S.ps[:, 3 + i, 0:n], rope[:, 1, :], ALU.mult)
                        link(nc.vector.tensor_tensor(out, r, rope[:, 0, :], ALU.mult))
                        nc.vector.tensor_tensor(out, out, rt[:, t, :], ALU.add).then_inc(mixed, 1)
                    for j in range(4):
                        dve.wait_ge(scored, j + 1)
                        link(nc.vector.tensor_reduce(nmax[:, j:j + 1], S.ps[:, j, :], AX.X, ALU.max, negate=True))
                        nc.vector.tensor_scalar(nmax[:, j:j + 1], nmax[:, j:j + 1], NA_SCALE, None, ALU.mult).then_inc(maxed, 1)
                    for u in range(2):
                        dve.wait_ge(exped, 2 * u + 2)
                        link(nc.vector.reciprocal(rsum[:, 2 * u:2 * u + 2], ssum[:, 2 * u:2 * u + 2]))
                        link(nc.vector.tensor_scalar(rsum[:, 2 * u + 1:2 * u + 2], rsum[:, 2 * u + 1:2 * u + 2], lam[:, 3:4], None, ALU.mult))
                        link(nc.vector.tensor_scalar(p_[:, u, 1, :], p_[:, u, 1, :], rsum[:, 2 * u + 1:2 * u + 2], None, ALU.mult))
                        nc.vector.scalar_tensor_tensor(out=a_[:, u, :], in0=p_[:, u, 0, :], scalar=rsum[:, 2 * u:2 * u + 1], in1=p_[:, u, 1, :],
                                                       op0=ALU.mult, op1=ALU.subtract).then_inc(diffed, 1)
                    for u in range(2):
                        dve.wait_ge(squared, u + 1)
                        nc.vector.tensor_scalar(ss[:, u:u + 1], ss[:, u:u + 1], 1.0 / P, 1e-5, ALU.mult, ALU.add).then_inc(scaled, 1)
                        dve.wait_ge(rooted, u + 1)
                        r_, i_ = rt_[:, u:u + 1], inv[:, u:u + 1]
                        link(nc.vector.reciprocal(i_, r_))
                        link(nc.vector.scalar_tensor_tensor(out=r_, in0=i_, scalar=ss[:, u:u + 1], in1=r_, op0=ALU.mult, op1=ALU.add))
                        link(nc.vector.reciprocal(i_, r_))
                        nc.vector.scalar_tensor_tensor(out=o_[:, u, :], in0=S.ps[:, 6 + u, 0:P], scalar=i_, in1=subln[:, :],
                                                       op0=ALU.mult, op1=ALU.mult).then_inc(normed, 1)
            clear_block(nc, [ready, raw, turned, mixed, staged, scored, maxed, exped, diffed, a_turned, a_copied, summed, squared,
                             scaled, rooted, normed, o_turned, chain])

        with nc.Fori(0, DA_H - 1) as h:
            body(h, True)
        body(DA_H - 1, False)


def even_mixer(nc, g, S, sb, ctx):
    S.slab_full = ctx.enter_context(nc.semaphore("pair_slabs_full"))
    S.wall_full = ctx.enter_context(nc.semaphore("lora_weights_full"))
    S.xlora, S.wall, S.wst, S.wslab = sb("xlora", [P, 2, T]), sb("lora_w", [P, 5, W_NA]), sb("lora_w_pair", [P, 5, P]), sb("pair_slabs", [P, 6, KD, P])
    S.reset, S.hcol, S.prc = sb("scan_reset", [P, T]), sb("pair_columns", [P, 19]), sb("rkv", [P, 3, T])
    zero = sb("zero", [P, 256])
    zeroed, item_x_cleared, item_y_cleared = [ctx.enter_context(nc.semaphore(m)) for m in ("zero_tile_set", "item_tokens_cleared", "item_outputs_cleared")]
    lora_block(nc, g, S)
    with nc.Block() as block:
        @block.sync
        def _(sp):
            sp.wait_ge(S.wall_full, 16 * 5)
            sp.wait_ge(S.toep_written, 16 * 2 * HP)
            sp.wait_ge(zeroed, 1)
            for rows, cleared in ((g.item_x, item_x_cleared), (g.item_y, item_y_cleared)):
                sp.dma_start(rows.rearrange("(p r) d -> p r d", p=P).rearrange("p r (a d) -> p (r a) d", d=256),
                             zero[:, :].unsqueeze(1).to_broadcast([P, ROWS // P * D // 256, 256])).then_inc(cleared, 16)

        @block.gpsimd
        def _(pool):
            nc.gpsimd.memset(zero[:, :], 0.0).then_inc(zeroed, 1)
    with nc.Fori(0, HP) as hp:
        with ExitStack() as st:
            sb2 = lambda n, s: st.enter_context(nc.sbuf_tensor(n, s, F32))
            A = Tiles()
            A.qT, A.kT, A.v = sb2("qT", [P, T]), sb2("kT", [P, T]), sb2("v", [P, NB, P])
            project_block(nc, g, S, hp, A)
            na_block(nc, g, S, hp, A)
        rwkv_pair(nc, g, S, hp)
    with nc.Block() as block:
        @block.sync
        def _(sp):
            sp.wait_ge(S.slab_full, 16 * 6)
            sp.wait_ge(item_x_cleared, 16)
            sp.wait_ge(item_y_cleared, 16)





class Inputs:

    def __init__(self, x, c, ctx, c_ctx, ada_w, ada_b, ln_g, ln_b, even_w_in, even_w_out, shift_w, na_rpb,
                 rw_w0, rw_w_up, rw_a0, rw_a_up, rw_g_up, rw_k_k, rw_k_a, rw_r_k, rw_gn_g, rw_gn_b,
                 odd_w_in, odd_w_out, da_lq1, da_lk1, da_lq2, da_lk2, da_subln_g, router_w, router_b,
                 exp_w_gate, exp_w_up, exp_w_down, const, rope):
        self.x, self.c, self.ctx, self.c_ctx = x, c, ctx, c_ctx
        self.ada_w, self.ada_b, self.ln_g, self.ln_b = ada_w, ada_b, ln_g, ln_b
        self.even_w_in, self.even_w_out, self.shift_w, self.na_rpb = even_w_in, even_w_out, shift_w, na_rpb
        self.rw_w0, self.rw_w_up, self.rw_a0, self.rw_a_up, self.rw_g_up = rw_w0, rw_w_up, rw_a0, rw_a_up, rw_g_up
        self.rw_k_k, self.rw_k_a, self.rw_r_k, self.rw_gn_g, self.rw_gn_b = rw_k_k, rw_k_a, rw_r_k, rw_gn_g, rw_gn_b
        self.odd_w_in, self.odd_w_out, self.da_subln_g = odd_w_in, odd_w_out, da_subln_g
        self.da_lq1, self.da_lk1, self.da_lq2, self.da_lk2 = da_lq1, da_lk1, da_lq2, da_lk2
        self.router_w, self.router_b = router_w, router_b
        self.exp_w_gate, self.exp_w_up, self.exp_w_down = exp_w_gate, exp_w_up, exp_w_down
        self.const, self.rope = const, rope


def program(nc, g, outs):
    with ExitStack() as ctx:
        def sb(name, shape):
            return ctx.enter_context(nc.sbuf_tensor(name, shape, F32))
        S = Tiles()
        S.cst = sb("constants", [P, C_END])
        S.col = sb("vector_columns", [P, R_END])
        S.adab = sb("ada_b_columns", [P, 96])
        S.csil = sb("silu_c", [P, 16])
        S.mcol = sb("modulation_columns", [P, DEPTH, 2, 48])
        S.router = sb("router", [P, KD, N_EXP])
        S.rbias = sb("router_bias", [P, N_EXP])
        S.ps = ctx.enter_context(nc.psum_tensor("psum", [P, 8, 512], F32))
        S.uT = sb("uT", [P, KD, T])
        g.toep = nc.dram_tensor("na_bias_toeplitz", (2 * HP, GRID_W, 7, GRID_W), F32).ap()
        g.item_x = nc.dram_tensor("item_tokens", (ROWS, D), F32).ap()
        g.item_y = nc.dram_tensor("item_outputs", (ROWS, D), F32).ap()
        S.toep_written = ctx.enter_context(nc.semaphore("toeplitz_written"))
        toeplitz_copies(nc, g, S)
        stages(nc, g, S, outs)


_INS = ["x", "c", "ctx", "c_ctx", "ada_w", "ada_b", "ln_g", "ln_b", "even_w_in", "even_w_out", "shift_w", "na_rpb",
        "rw_w0", "rw_w_up", "rw_a0", "rw_a_up", "rw_g_up", "rw_k_k", "rw_k_a", "rw_r_k", "rw_gn_g", "rw_gn_b",
        "odd_w_in", "odd_w_out", "da_lq1", "da_lk1", "da_lq2", "da_lk2", "da_subln_g", "router_w", "router_b",
        "exp_w_gate", "exp_w_up", "exp_w_down"]


def kernel(**inputs):
    import numpy as np
    import concourse.bacc as bacc
    from concourse.bass_utils import run_bass_kernel_spmd as run

    nc = bacc.Bacc("TRN2", target_bir_lowering=False, num_devices=1)
    arrays = {"in_" + name: np.ascontiguousarray(inputs[name]) for name in _INS}
    arrays["in_const"], arrays["in_rope"] = shape_constants(np)
    aps = [nc.dram_tensor(name, a.shape, F32, kind="ExternalInput").ap() for name, a in arrays.items()]
    outs = [nc.dram_tensor(f"out_{i}", s, F32, kind="ExternalOutput").ap() for i, s in enumerate(OUTS)]
    program(nc, Inputs(*aps), outs)
    r = run(nc, [arrays], core_ids=[0])
    got = tuple(r.results[0][f"out_{i}"] for i in range(len(OUTS)))
    return got[0] if len(got) == 1 else got


OUTS = [(1, T_LAT, D)]


def stages(nc, g, S, outs):
    with nc.sbuf_tensor("h_in", [P, NB, D], F32) as h:
        S.h = h
        setup_block(nc, g, S)
        ada_blocks(nc, g, S)
        modulate_block(nc, g, S, 0, 0, load_h=True)
    with ExitStack() as ctx:
        sb = lambda n, s: ctx.enter_context(nc.sbuf_tensor(n, s, F32))
        S.combine, S.place = sb("combine", [P, NB, N_EXP]), sb("place", [P, NB, N_EXP])
        S.two_gates = sb("two_gates", [P, 2, NB])
        S.two_rows = ctx.enter_context(nc.sbuf_tensor("two_rows", [P, 2, NB], mybir.dt.uint32))
        S.item_expert = ctx.enter_context(nc.sbuf_tensor("item_expert", [P, N_ITEM], mybir.dt.int32))
        S.pairs = ctx.enter_context(nc.sbuf_tensor("item_pairs", [P, 1], mybir.dt.int32))
        S.h = sb("h", [P, NB, D])
        with nc.sbuf_tensor("oT0", [P, 2 * HP, T], F32) as S.oT:
            with ExitStack() as mx:
                even_mixer(nc, g, S, lambda n, s: mx.enter_context(nc.sbuf_tensor(n, s, F32)), ctx)
            post_block(nc, g, S, 0, 0, range(NB), project=g.even_w_out[0], load_h=True)
        experts(nc, g, S, 0, range(NB))
        latent = range(T_CTX // P, NB)
        modulate_block(nc, g, S, 1, 0)
        with nc.sbuf_tensor("oT1", [P, 2 * HP, T], F32) as S.oT:
            odd_mixer(nc, g, S, 1)
            post_block(nc, g, S, 1, 0, latent, project=g.odd_w_out[0])
        experts(nc, g, S, 1, latent)
        written = ctx.enter_context(nc.semaphore("output_written"))
        with nc.Block() as block:
            @block.sync
            def _(sp):
                sp.dma_start(outs[0][0].rearrange("(b p) d -> p b d", p=P), S.h[:, T_CTX // P:NB, :]).then_inc(written, 16)
                sp.wait_ge(written, 16)


def experts(nc, g, S, l, blocks):
    modulate_block(nc, g, S, l, 3, blocks=blocks)
    router_block(nc, g, S, l, blocks)
    dispatch_block(nc, g, S, l, blocks)
    moe(nc, g, S, l)
    with nc.sbuf_tensor(f"acc{l}", [P, NB, D], F32) as S.acc:
        combine_block(nc, g, S, l, blocks)
        post_block(nc, g, S, l, 1, blocks)
```

```python
from contextlib import ExitStack, contextmanager

import concourse.bass as bass
from concourse import mybir

F32 = mybir.dt.float32
ACT = mybir.ActivationFunctionType
ALU = mybir.AluOpType
AX = mybir.AxisListType

P = 128
D = 1024
KD = D // P
T_CTX, T_LAT = 256, 256
T = T_CTX + T_LAT
NB = T // P
DEPTH = 2
GRID_W = 64
HP = 4
CH = 64
RW_IN = 1792
N_EXP, D_EXP = 16, 512
ALPHA = (2 * DEPTH) ** 0.25
DECAY = 0.6065306597126334
HD = 64
WIN_C = 16
DA_H = 8
LAMBDA_INIT = 0.3555090675909693
NEG = -1.0e30

C_ID, C_ONES, C_MASK, C_LVL, C_WIN, C_ROT, C_IOTA, C_TRI, C_ALL, C_END = 0, 128, 256, 768, 1536, 1600, 1728, 1856, 1984, 2112
C_EIDX = C_END
C_JIDX = C_END + 16
C_END += 16 + 32
N_ITEM = 26
ROWS = N_ITEM * P
TAIL = (3, 2)
MAX_STEPS = (N_ITEM - 2) // 2 - 1
R_C, R_CC, R_SW, R_W0, R_A0, R_KK, R_KA, R_RK, R_GG, R_GB, R_END = 0, 8, 16, 58, 66, 74, 78, 82, 86, 90, 94


class Tiles:

    pass


class Link:

    def __init__(self, eng, sem):
        self.eng, self.sem, self.n = eng, sem, 0

    def __call__(self, ins):
        self.n += 1
        ins.then_inc(self.sem, 1)
        self.eng.wait_ge(self.sem, self.n)


def clear_block(nc, sems):
    with nc.Block() as block:
        @block.sync
        def _(sp):
            for s in sems:
                sp.sem_clear(s)


@contextmanager
def phase(nc, sems):
    with nc.Block() as block:
        yield block
    clear_block(nc, sems)


def shape_constants(np):
    c = np.zeros((P, C_END), np.float32)
    i = np.arange(P)
    c[:, C_ID:C_ID + P] = np.eye(P)
    same_head = (i[:, None] // CH) == (i[None] // CH)
    c[:, C_ONES:C_ONES + P] = same_head
    s, t = i[:, None] % CH, i[None] % CH
    for n, m in enumerate((s < t, s <= t, s > t, s >= t)):
        c[:, C_MASK + n * P:C_MASK + (n + 1) * P] = m & same_head
    for n in range(6):
        b = 1 << n
        c[:, C_LVL + n * P:C_LVL + (n + 1) * P] = same_head & (s // (2 * b) == t // (2 * b)) & (s // b != t // b)
    c[:, C_IOTA:C_IOTA + P] = i[None]
    c[:, C_EIDX:C_EIDX + 16] = np.arange(16)[None]
    c[:, C_JIDX:C_JIDX + 32] = np.arange(32)[None]
    c[:, C_TRI:C_TRI + P] = i[:, None] < i[None]
    c[:, C_ALL:C_ALL + P] = 1.0
    q, k = i[:, None] % GRID_W, np.arange(GRID_W)[None]
    lo = np.clip(q - WIN_C // 2, 0, GRID_W - WIN_C)
    c[:, C_WIN:C_WIN + GRID_W] = np.where((k >= lo) & (k < lo + WIN_C), 0.0, NEG)
    for r in range(P):
        m = r % 32
        if m < 16:
            c[r + 16, C_ROT + r] = -1.0
        else:
            c[r - 16, C_ROT + r] = 1.0
    rope = np.zeros((P, 2, T_LAT), np.float32)
    tok = np.arange(T_LAT)
    inv = (np.float32(10000.0) ** (-np.arange(16, dtype=np.float32) / np.float32(16))).astype(np.float32)
    for r in range(P):
        pos = tok // GRID_W if (r % 64) < 32 else tok % GRID_W
        ang = pos.astype(np.float32) * inv[r % 16]
        rope[r, 0], rope[r, 1] = np.cos(ang), np.sin(ang)
    return c, rope.reshape(P, 2 * T_LAT)


def setup_block(nc, g, S):
    with ExitStack() as ctx:
        rows = ctx.enter_context(nc.sbuf_tensor("rows", [R_END, P], F32))
        abrows = ctx.enter_context(nc.sbuf_tensor("abrows", [96, P], F32))
        loaded = ctx.enter_context(nc.semaphore("consts_loaded"))
        turned = ctx.enter_context(nc.semaphore("columns_turned"))
        copied = ctx.enter_context(nc.semaphore("columns_copied"))
        block = ctx.enter_context(phase(nc, [loaded, turned, copied]))
        loads = [
            (S.cst[:, :], g.const),
            (abrows[:, :], g.ada_b.rearrange("l (j p) -> (l j) p", p=P)),
            (rows[R_C:R_CC, :], g.c.rearrange("b (k p) -> (b k) p", p=P)),
            (rows[R_CC:R_SW, :], g.c_ctx.rearrange("(k p) -> k p", p=P)),
            (rows[R_SW:R_W0, :], g.shift_w.rearrange("n j (k p) -> (n j k) p", p=P)),
            (rows[R_W0:R_A0, :], g.rw_w0.rearrange("n d (k p) -> (n d k) p", p=P)),
            (rows[R_A0:R_KK, :], g.rw_a0.rearrange("n d (k p) -> (n d k) p", p=P)),
            (rows[R_KK:R_KA, :], g.rw_k_k.rearrange("n (k p) -> (n k) p", p=P)),
            (rows[R_KA:R_RK, :], g.rw_k_a.rearrange("n (k p) -> (n k) p", p=P)),
            (rows[R_RK:R_GG, :], g.rw_r_k.rearrange("n (k a) p -> (n k) (a p)", a=2)),
            (rows[R_GG:R_GB, :], g.rw_gn_g.rearrange("n (k p) -> (n k) p", p=P)),
            (rows[R_GB:R_END, :], g.rw_gn_b.rearrange("n (k p) -> (n k) p", p=P)),
            (S.router[:, :, :], g.router_w.rearrange("(k p) e -> p k e", p=P)),
            (S.rbias[:, :], g.router_b.rearrange("(a e) -> a e", a=1).to_broadcast([P, N_EXP])),
        ]

        @block.sync
        def _(sp):
            for dst, src in loads:
                sp.dma_start(dst, src).then_inc(loaded, 16)

        @block.tensor
        def _(pe):
            pe.wait_ge(loaded, 16 * len(loads))
            nc.tensor.transpose(S.ps[:, 0, 0:R_END], rows[:, :], S.cst[0:R_END, C_ID:C_ID + R_END]).then_inc(turned, 1)
            nc.tensor.transpose(S.ps[:, 1, 0:96], abrows[:, :], S.cst[0:96, C_ID:C_ID + 96]).then_inc(turned, 1)

        @block.vector
        def _(dve):
            dve.wait_ge(turned, 1)
            nc.vector.tensor_copy(S.col[:, :], S.ps[:, 0, 0:R_END]).then_inc(copied, 1)
            dve.wait_ge(turned, 2)
            nc.vector.tensor_copy(S.adab[:, :], S.ps[:, 1, 0:96])

        @block.scalar
        def _(act):
            act.wait_ge(copied, 1)
            nc.scalar.activation(S.csil[:, :], S.col[:, R_C:R_SW], ACT.Silu)


ADA_J = 4
ADA_W = 512


def ada_blocks(nc, g, S):
    per = ADA_J * ADA_W // P
    groups = [(l, i) for l in range(DEPTH) for i in range(6 * D // (ADA_J * ADA_W))]
    with ExitStack() as ctx:
        slab = ctx.enter_context(nc.sbuf_tensor("ada_slab", [P, 2, ADA_J, KD, ADA_W], F32))
        rows = ctx.enter_context(nc.sbuf_tensor("ada_rows", [P, 2, ADA_W], F32))
        full = [ctx.enter_context(nc.semaphore(f"ada_slabs_full{u}")) for u in range(2)]
        cleared, summed, copied, turned, added = [ctx.enter_context(nc.semaphore("ada_" + m))
                                                  for m in ("rows_cleared", "summed", "rows_copied", "turned", "bias_added")]
        csil = S.csil[:, :].rearrange("p (w k) -> p k w", w=2)
        with phase(nc, full + [cleared, summed, copied, turned, added]) as block:
            def load(eng, n, js):
                l, i = groups[n]
                src = g.ada_w[l].rearrange("(k p) n -> p k n", p=P)
                for j in js:
                    c0 = (i * ADA_J + j) * ADA_W
                    eng.dma_start(slab[:, n % 2, j], src[:, :, c0:c0 + ADA_W]).then_inc(full[n % 2], 16)

            @block.sync
            def _(sp):
                for n in range(len(groups)):
                    if n >= 2:
                        sp.wait_ge(summed, n - 1)
                    load(sp, n, range(ADA_J))
                load_tokens(sp, g, S.h, S.tokens_in)
                sp.dma_start(S.lora_slab, g.even_w_in[0].rearrange("(k p) n -> p k n", p=P)[:, :, 3072:3328]).then_inc(S.lora_in, 16)

            @block.gpsimd
            def _(pool):
                nc.gpsimd.memset(rows[:, :, :], 0.0).then_inc(cleared, 1)

            @block.tensor
            def _(pe):
                def turn(n):
                    pe.wait_ge(copied, ADA_J * (n + 1))
                    if n >= 2:
                        pe.wait_ge(added, n - 1)
                    for q in range(ADA_W // P):
                        last = nc.tensor.transpose(S.ps[:, 2 + n % 2, q * P:(q + 1) * P], rows[:, n % 2, q * P:(q + 1) * P],
                                                   S.cst[:, C_ID:C_ID + P])
                    last.then_inc(turned, 1)

                for n in range(len(groups)):
                    pe.wait_ge(full[n % 2], 16 * ADA_J * (n // 2 + 1))
                    if n >= 2:
                        pe.wait_ge(copied, ADA_J * (n - 1))
                    for k in range(KD):
                        for j in range(ADA_J):
                            last = nc.tensor.matmul(S.ps[32 * j:32 * j + 2, n % 2, :], csil[:, k, :], slab[:, n % 2, j, k, :],
                                                    start=(k == 0), stop=(k == KD - 1))
                    last.then_inc(summed, 1)
                    if n:
                        turn(n - 1)
                turn(len(groups) - 1)

            @block.scalar
            def _(act):
                act.wait_ge(cleared, 1)
                for n in range(len(groups)):
                    act.wait_ge(summed, n + 1)
                    if n >= 2:
                        act.wait_ge(turned, n - 1)
                    for j in range(ADA_J):
                        nc.scalar.activation(rows[32 * j:32 * j + 2, n % 2, :], S.ps[32 * j:32 * j + 2, n % 2, :], ACT.Copy).then_inc(copied, 1)

            @block.vector
            def _(dve):
                for n, (l, i) in enumerate(groups):
                    dve.wait_ge(turned, n + 1)
                    c0 = i * per
                    for w in range(2):
                        out = S.mcol[:, l, w, c0:c0 + per].rearrange("p (j q) -> p j q", j=ADA_J)
                        got = S.ps[:, 2 + n % 2, :].rearrange("p (q j r) -> p j q r", j=ADA_J, r=32)[:, :, :, w]
                        bias = S.adab[:, l * 48 + c0:l * 48 + c0 + per].rearrange("p (j q) -> p j q", j=ADA_J)
                        last = nc.vector.tensor_tensor(out, got, bias, ALU.add)
                    last.then_inc(added, 1)
        with nc.Block() as block:
            @block.vector
            def _(dve):
                for l in range(DEPTH):
                    for m in (1, 4):
                        nc.vector.tensor_scalar(S.mcol[:, l, :, m * KD:(m + 1) * KD], S.mcol[:, l, :, m * KD:(m + 1) * KD],
                                                1.0, None, ALU.add)


def modulate_block(nc, g, S, l, m, first=False, blocks=range(NB)):
    tag = f"{l}_{m}"
    blocks = list(blocks)
    with ExitStack() as ctx:
        turned = ctx.enter_context(nc.semaphore("h_turned" + tag))
        lat_done = ctx.enter_context(nc.semaphore("u_lat_done" + tag))
        ctx_done = ctx.enter_context(nc.semaphore("u_ctx_done" + tag))
        block = ctx.enter_context(phase(nc, [turned, lat_done, ctx_done]))

        @block.sync
        def _(sp):
            if first:
                load_pair_slabs(sp, g, S, 0)

        @block.tensor
        def _(pe):
            if first:
                pe.wait_ge(S.tokens_in, 32)
            for k in range(KD):
                for half, done in ((0, ctx_done), (1, lat_done)):
                    mine = [b for b in blocks if b // 2 == half]
                    if mine and k >= 4:
                        pe.wait_ge(done, k - 3)
                    for b in mine:
                        last = nc.tensor.transpose(S.ps[:, 4 * half + k % 4, (b % 2) * P:(b % 2 + 1) * P],
                                                   S.h[:, b, k * P:(k + 1) * P], S.cst[:, C_ID:C_ID + P])
                last.then_inc(turned, 1)

        def col(w, r, k):
            return S.mcol[:, l, w, (m + r) * KD + k:(m + r) * KD + k + 1]

        @block.scalar
        def _(act):
            for k in range(KD):
                act.wait_ge(turned, k + 1)
                nc.scalar.activation(S.uT[:, k, T_CTX:T], S.ps[:, 4 + k % 4, 0:T_LAT], ACT.Identity,
                                     bias=col(0, 0, k), scale=col(0, 1, k)).then_inc(lat_done, 1)

        @block.vector
        def _(dve):
            if blocks[0] == 0:
                for k in range(KD):
                    dve.wait_ge(turned, k + 1)
                    nc.vector.tensor_scalar(S.uT[:, k, 0:T_CTX], S.ps[:, k % 4, 0:T_CTX],
                                            col(1, 1, k), col(1, 0, k), ALU.mult, ALU.add).then_inc(ctx_done, 1)


def load_tokens(sp, g, h, sem):
    sp.dma_start(h[:, 0:2, :], g.ctx[0].rearrange("(b p) d -> p b d", p=P)).then_inc(sem, 16)
    sp.dma_start(h[:, 2:4, :], g.x[0].rearrange("(b p) d -> p b d", p=P)).then_inc(sem, 16)


NA_SCALE = float(HD) ** -0.5
ZERO_W = 256
PAIR = 2 * HD
W_NA = 512


def load_pair_slabs(sp, g, S, hp):
    src = g.even_w_in[0].rearrange("(k p) n -> p k n", p=P)
    for n in range(6):
        sp.dma_start(S.wslab[:, n], src[:, :, bass.ds(hp * PAIR + n * W_NA, PAIR)]).then_inc(S.slab_full, 16)


def lora_block(nc, g, S, R):
    with ExitStack() as ctx:
        slab = S.lora_slab
        cleared = ctx.enter_context(nc.semaphore("lora_cleared"))
        projected = ctx.enter_context(nc.semaphore("lora_projected"))
        scaled = ctx.enter_context(nc.semaphore("lora_scaled"))
        chain = ctx.enter_context(nc.semaphore("lora_conv_chain"))
        conved = ctx.enter_context(nc.semaphore("lora_conved"))
        block = ctx.enter_context(phase(nc, [cleared, projected, scaled, chain, conved]))

        @block.sync
        def _(sp):
            sp.wait_ge(cleared, 1)
            for d in range(2):
                sp.dma_start(S.wall[0:64, d, :], g.rw_w_up[0, d]).then_inc(S.wall_full, 16)
                sp.dma_start(S.wall[64:128, 2 + d, :], g.rw_a_up[0, d]).then_inc(S.wall_full, 16)
            sp.dma_start(S.wall[:, 4, :], g.rw_g_up[0]).then_inc(S.wall_full, 16)

        @block.gpsimd
        def _(pool):
            nc.gpsimd.memset(S.wall[:, :, :], 0.0).then_inc(cleared, 1)
            nc.gpsimd.memset(R.bd[1][:, :, :, :], 0.0)
            nc.gpsimd.memset(R.vbd[:, :, :], 0.0)
            for d in range(2):
                nc.gpsimd.memset(R.last[d][:, :], 0.0)

        @block.tensor
        def _(pe):
            pe.wait_ge(S.lora_in, 16)
            for j in range(2):
                for k in range(KD):
                    last = nc.tensor.matmul(S.ps[:, j, :], slab[:, k, j * P:(j + 1) * P], S.uT[:, k, :],
                                            start=(k == 0), stop=(k == KD - 1))
                last.then_inc(projected, 1)

        @block.scalar
        def _(act):
            for j in range(2):
                act.wait_ge(projected, j + 1)
                w1 = R_SW + 14 + 12 + j
                nc.scalar.activation(S.xlora[:, j, :], S.ps[:, j, :], ACT.Copy, scale=S.col[:, w1:w1 + 1]).then_inc(scaled, 1)
            act.wait_ge(conved, 1)
            nc.scalar.activation(S.xlora[0:64, 0, :], S.xlora[0:64, 0, :], ACT.Tanh)
            act.wait_ge(conved, 2)
            nc.scalar.activation(S.xlora[:, 1, :], S.xlora[:, 1, :], ACT.Sigmoid)

        @block.vector
        def _(dve):
            link = Link(dve, chain)
            nc.vector.memset(S.reset[:, :], 1.0)
            nc.vector.memset(R.bd[0][:, :, :, :], 0.0)
            for j in range(2):
                dve.wait_ge(scaled, j + 1)
                conv_taps(nc, link, S.xlora[:, j, :], S.ps[:, j, :],
                          S.col[:, R_SW + 12 + j:R_SW + 13 + j], S.col[:, R_SW + 28 + 12 + j:R_SW + 28 + 13 + j], conved)
            nc.vector.memset(S.reset[:, :].rearrange("p (c t) -> p c t", t=CH)[:, :, 0:1], 0.0)


def conv_taps(nc, link, out, raw, w0, w2, done):
    o = out.rearrange("p (g t) -> p g t", g=2)
    r = raw.rearrange("p (g t) -> p g t", g=2)
    n = T_CTX
    link(nc.vector.scalar_tensor_tensor(out=o[:, :, 1:n], in0=r[:, :, 0:n - 1], scalar=w0, in1=o[:, :, 1:n],
                                        op0=ALU.mult, op1=ALU.add))
    nc.vector.scalar_tensor_tensor(out=o[:, :, 0:n - 1], in0=r[:, :, 1:n], scalar=w2, in1=o[:, :, 0:n - 1],
                                   op0=ALU.mult, op1=ALU.add).then_inc(done, 1)


def project_block(nc, g, S, hp, A):
    with ExitStack() as ctx:
        sem = lambda n: ctx.enter_context(nc.semaphore("pj_" + n))
        ready, scaled, chain, picked, conved = sem("ready"), sem("scaled"), sem("chain"), sem("picked"), sem("conved")
        with nc.Block() as block:
            @block.sync
            def _(sp):
                sp.wait_ge(S.toep_written, 16 * 2 * HP)
                for qt in range(2):
                    for r2 in range(2):
                        for hh in range(2):
                            sp.dma_start(A.bias[r2 * 64:(r2 + 1) * 64, qt, hh, :].rearrange("p (a b) -> p a b", a=4),
                                         g.toep[bass.ds(hp * 2 + hh, 1), :, 3 - 2 * qt - r2:7 - 2 * qt - r2, :].rearrange("o c a b -> (o c) a b")).then_inc(A.bias_full, 16)

            @block.tensor
            def _(pe):
                pe.wait_ge(S.slab_full, 16 * 6)
                for n in (0, 1, 3, 4, 5):
                    for k in range(KD):
                        last = nc.tensor.matmul(S.ps[:, n, :], S.wslab[:, n, k, :], S.uT[:, k, :],
                                                start=(k == 0), stop=(k == KD - 1))
                    last.then_inc(ready, 1)
                for b in range(NB):
                    for k in range(KD):
                        last = nc.tensor.matmul(S.ps[:, 2, b * P:(b + 1) * P], S.uT[:, k, b * P:(b + 1) * P],
                                                S.wslab[:, 2, k, :], start=(k == 0), stop=(k == KD - 1))
                last.then_inc(ready, 1)

            @block.scalar
            def _(act):
                act.wait_ge(ready, 1)
                nc.scalar.activation(A.qT[:, :], S.ps[:, 0, :], ACT.Copy)
                act.wait_ge(picked, 1)
                for j in range(3):
                    act.wait_ge(ready, 3 + j)
                    nc.scalar.activation(S.prc[:, j, :], S.ps[:, 3 + j, :], ACT.Copy, scale=S.hcol[:, 3 + j:4 + j]).then_inc(scaled, 1)
                act.wait_ge(ready, 6)
                nc.scalar.activation(A.v[:, :, :], S.ps[:, 2, :].rearrange("p (b n) -> p b n", b=NB), ACT.Copy)

            @block.vector
            def _(dve):
                link = Link(dve, chain)
                for j in range(3):
                    a = R_SW + 14 * j
                    nc.vector.tensor_copy(S.hcol[:, 3 * j:3 * j + 3].rearrange("p (n o) -> p n o", o=1),
                                          S.col[:, a:a + 12].rearrange("p (n h) -> p n h", h=HP)[:, :, bass.ds(hp, 1)])
                link(nc.vector.tensor_copy(S.hcol[:, 9:18].rearrange("p (n o) -> p n o", o=1),
                                           S.col[:, R_W0:R_END].rearrange("p (n h) -> p n h", h=HP)[:, :, bass.ds(hp, 1)]))
                link(nc.vector.tensor_scalar(S.hcol[:, 18:19], S.hcol[:, 14:15], -1.0, 1.0, ALU.mult, ALU.add))
                nc.vector.tensor_copy(S.wst[:, :, :], S.wall[:, :, bass.ds(hp * PAIR, PAIR)]).then_inc(picked, 1)
                dve.wait_ge(ready, 2)
                nc.vector.tensor_copy(A.kT[:, :], S.ps[:, 1, :])
                for j in range(3):
                    dve.wait_ge(scaled, j + 1)
                    conv_taps(nc, link, S.prc[:, j, :], S.ps[:, 3 + j, :], S.hcol[:, j:j + 1], S.hcol[:, 6 + j:7 + j], conved)
        clear_block(nc, [ready, scaled, chain, picked, conved])


def na_block(nc, g, S, hp, A):
    units = [(qb, hh) for qb in (2, 3, 0, 1) for hh in (0, 1)]
    with ExitStack() as ctx:
        sem = lambda n: ctx.enter_context(nc.semaphore("na_" + n))
        masked = sem("bias_masked")
        scored, read, maxed, exped = sem("scored"), sem("scores_read"), sem("maxed"), sem("exped")
        normed, turned, copied, summed, written, chain = (sem("normed"), sem("turned"), sem("pt_copied"), sem("av_summed"),
                                                          sem("o_written"), sem("chain"))
        sb = lambda n, s: ctx.enter_context(nc.sbuf_tensor("na_" + n, s, F32))
        bias = A.bias
        s_, p_, pt = sb("s", [P, 2, T]), sb("p", [P, 2, T]), sb("pt", [P, 2, NB, P])
        nmax, ssum, rinv = sb("nmax", [P, 8]), sb("ssum", [P, 8]), sb("rinv", [P, 8])

        def keys(u):
            return T if units[u][0] >= 2 else T_CTX

        with nc.Block() as block:
            @block.sync
            def _(sp):
                sp.sem_clear(S.slab_full)
                load_pair_slabs(sp, g, S, hp + 1)
                for rows, cleared in ((g.item_x, S.item_x_cleared), (g.item_y, S.item_y_cleared)):
                    flat = rows.rearrange("r d -> (r d)").rearrange("(h p a d) -> h p a d", h=HP, p=P, d=ZERO_W)
                    sp.dma_start(flat[bass.ds(hp, 1)].rearrange("o p a d -> p (o a) d"),
                                 S.zero[:, :].unsqueeze(1).to_broadcast([P, ROWS * D // (HP * P * ZERO_W), ZERO_W])).then_inc(cleared, 16)

            @block.gpsimd
            def _(pool):
                pool.wait_ge(A.bias_full, 16 * 8)
                b = bias[:, :, :, :].rearrange("p q h (r c) -> p (q h r) c", c=GRID_W)
                nc.gpsimd.tensor_tensor(b, b, S.cst[:, C_WIN:C_WIN + GRID_W].unsqueeze(1).to_broadcast([P, 16, GRID_W]),
                                        ALU.add).then_inc(masked, 1)

            @block.tensor
            def _(pe):
                n = len(units)
                for i in range(n + 2):
                    if i < n:
                        qb, hh = units[i]
                        if i >= 2:
                            pe.wait_ge(read, i - 1)
                        h0 = hh * HD
                        nc.tensor.matmul(S.ps[:, i % 2, 0:keys(i)], A.qT[h0:h0 + HD, qb * P:(qb + 1) * P],
                                         A.kT[h0:h0 + HD, 0:keys(i)], start=True, stop=True).then_inc(scored, 1)
                    if 0 <= i - 1 < n:
                        u = i - 1
                        pe.wait_ge(normed, u + 1)
                        if u >= 2:
                            pe.wait_ge(copied, u - 1)
                        for b in range(keys(u) // P):
                            last = nc.tensor.transpose(S.ps[:, 2 + u % 2, b * P:(b + 1) * P], p_[:, u % 2, b * P:(b + 1) * P],
                                                       S.cst[:, C_ID:C_ID + P])
                        last.then_inc(turned, 1)
                    if 0 <= i - 2 < n:
                        u = i - 2
                        qb, hh = units[u]
                        pe.wait_ge(copied, u + 1)
                        if u >= 2:
                            pe.wait_ge(written, u - 1)
                        h0 = hh * HD
                        nk = keys(u) // P
                        for b in range(nk):
                            last = nc.tensor.matmul(S.ps[h0:h0 + HD, 4 + u % 2, 0:P], A.v[:, b, h0:h0 + HD], pt[:, u % 2, b, :],
                                                    start=(b == 0), stop=(b == nk - 1))
                        last.then_inc(summed, 1)

            @block.vector
            def _(dve):
                link = Link(dve, chain)
                n = len(units)
                dve.wait_ge(masked, 1)
                for i in range(n + 1):
                    if i < n:
                        qb, hh = units[i]
                        dve.wait_ge(scored, i + 1)
                        if i >= 2:
                            dve.wait_ge(exped, i - 1)
                        if keys(i) == T:
                            nc.vector.tensor_scalar(s_[:, i % 2, 0:T_CTX], S.ps[:, i % 2, 0:T_CTX], NA_SCALE, None, ALU.mult)
                            nc.vector.scalar_tensor_tensor(out=s_[:, i % 2, T_CTX:T], in0=S.ps[:, i % 2, T_CTX:T],
                                                           scalar=NA_SCALE, in1=bias[:, qb - 2, hh, :],
                                                           op0=ALU.mult, op1=ALU.add).then_inc(read, 1)
                        else:
                            nc.vector.tensor_scalar(s_[:, i % 2, 0:T_CTX], S.ps[:, i % 2, 0:T_CTX], NA_SCALE, None,
                                                    ALU.mult).then_inc(read, 1)
                        dve.wait_ge(read, i + 1)
                        nc.vector.tensor_reduce(nmax[:, i:i + 1], s_[:, i % 2, 0:keys(i)], AX.X, ALU.max,
                                                negate=True).then_inc(maxed, 1)
                    if i >= 1:
                        u = i - 1
                        dve.wait_ge(exped, u + 1)
                        link(nc.vector.reciprocal(rinv[:, u:u + 1], ssum[:, u:u + 1]))
                        nc.vector.tensor_scalar(p_[:, u % 2, 0:keys(u)], p_[:, u % 2, 0:keys(u)], rinv[:, u:u + 1], None,
                                                ALU.mult).then_inc(normed, 1)

            @block.scalar
            def _(act):
                n = len(units)
                for i in range(n + 2):
                    if i < n:
                        act.wait_ge(maxed, i + 1)
                        if i >= 2:
                            act.wait_ge(turned, i - 1)
                        nc.scalar.activation(p_[:, i % 2, 0:keys(i)], s_[:, i % 2, 0:keys(i)], ACT.Exp,
                                             bias=nmax[:, i:i + 1], accum_out=ssum[:, i:i + 1]).then_inc(exped, 1)
                    if 0 <= i - 1 < n:
                        u = i - 1
                        act.wait_ge(turned, u + 1)
                        if u >= 2:
                            act.wait_ge(summed, u - 1)
                        nk = keys(u) // P
                        nc.scalar.activation(pt[:, u % 2, 0:nk, :], S.ps[:, 2 + u % 2, 0:nk * P].rearrange("p (b q) -> p b q", q=P),
                                             ACT.Copy).then_inc(copied, 1)
                    if 0 <= i - 2 < n:
                        u = i - 2
                        qb, hh = units[u]
                        act.wait_ge(summed, u + 1)
                        h0 = hh * HD
                        nc.scalar.activation(S.oT[h0:h0 + HD, bass.ds(hp, 1), qb * P:(qb + 1) * P].rearrange("p o t -> p (o t)"),
                                             S.ps[h0:h0 + HD, 4 + u % 2, 0:P], ACT.Copy).then_inc(written, 1)
        clear_block(nc, [A.bias_full, masked, scored, read, maxed, exped, normed, turned, copied, summed, written, chain])


def toeplitz_copies(nc, g, S):
    na, nb = 15, 31
    flat = g.na_rpb.rearrange("n h a b -> (n h a b)")
    with nc.Block() as block:
        @block.sync
        def _(sp):
            for h in range(2 * HP):
                at = flat[h * na * nb + 4 * nb + 15:h * na * nb + 4 * nb + 16]
                src = bass.AP(tensor=at.tensor, offset=at.offset, ap=[[nb, 7], [-1, GRID_W], [1, GRID_W]])
                sp.dma_start(g.toep[h].rearrange("c a b -> a c b"), src).then_inc(S.toep_written, 16)


NC_ = T_CTX // CH
E_IN, E_EX, E_INV, E_BAR = range(4)
BA, BR, BB, BK, BBB, BKB = range(6)


def rwkv_state(nc, S, sb):
    R = Tiles()
    R.last = [sb(f"rw_last{d}", [P, P]) for d in range(2)]
    free = S.h[:, :, :].rearrange("p b d -> p (b d)")
    n = 6 * NC_ * P
    R.bd = [free[:, 0:n].rearrange("p (w c t) -> p w c t", w=6, c=NC_), sb("rw_bd1", [P, 6, NC_, P])]
    R.y, R.bonus = free[:, n:n + T], free[:, n + T:n + 2 * T]
    R.vbd = sb("rw_vbd", [P, NC_, P])
    return R


def rwkv_pair(nc, g, S, R, hp):
    with ExitStack() as st:
        sb = lambda n, s: st.enter_context(nc.sbuf_tensor("rw_" + n, s, F32))
        R.gate = sb("gate", [P, T])
        R.wc = sb("wc", [P, 2, NC_])
        with nc.Fori(0, 2) as half:
            rwkv_half(nc, S, R, half * T_CTX)
        rwkv_finish(nc, S, R, hp)


def rwkv_half(nc, S, R, tok):
    n_tok = T_CTX
    with ExitStack() as st:
        sem = lambda m: st.enter_context(nc.semaphore("rw_" + m))
        sb = lambda m, s: st.enter_context(nc.sbuf_tensor("rp_" + m, s, F32))
        sem = lambda m: st.enter_context(nc.semaphore("rw_" + m))
        sig, av, keff, nka = sb("sig", [P, 2, n_tok]), sb("a", [P, 2, n_tok]), sb("keff", [P, 2, n_tok]), sb("nka", [P, 2, n_tok])
        cinc, y_, z_, w_ = sb("cinc", [P, 2, n_tok]), sb("cexc", [P, 2, n_tok]), sb("cbar", [P, 2, n_tok]), sb("crev", [P, n_tok])
        kraw, sq, kk, ex = sb("kraw", [P, n_tok]), sb("sq", [P, n_tok]), sb("kk", [P, n_tok]), sb("ex", [P, 2, 4, n_tok])
        xl = sb("xl", [P, 2, n_tok])
        rkv = sb("rkv", [P, 3, n_tok])
        staged, loraed, sigmoided, squared, normsum, rooted = (sem("staged"), sem("loraed"), sem("sigmoided"), sem("squared"),
                                                               sem("normsum"), sem("rooted"))
        argued, exped, chain, bonused, summed, keyed = sem("argued"), sem("exped"), sem("chain"), sem("bonused"), sem("summed"), sem("keyed")
        h = S.hcol
        built, values_built, bonus_set = [sem("built0"), sem("built1")], sem("values_built"), sem("bonus_set")
        r, k, v = rkv[:, 0, :], rkv[:, 1, :], rkv[:, 2, :]

        def build(eng, d):
            terms = ((BA, kk[:, :], E_EX), (BR, r, E_IN), (BB, nka[:, d, :], E_INV), (BK, keff[:, d, :], E_INV),
                     (BBB, nka[:, d, :], E_BAR), (BKB, keff[:, d, :], E_BAR))
            for which, x, e in terms:
                for hh in range(2):
                    p0 = hh * CH
                    last = eng.tensor_tensor(R.bd[d][p0:p0 + CH, which, :, p0:p0 + CH],
                                             x[p0:p0 + CH, :].rearrange("p (c t) -> p c t", t=CH),
                                             ex[p0:p0 + CH, d, e, :].rearrange("p (c t) -> p c t", t=CH), ALU.mult)
            last.then_inc(built[d], 1)
        names = ["tn", "An", "Bn", "Kn", "LT", "MbT", "AkT", "MkT", "Et", "Tm", "Z", "F", "G", "U0"]
        M = [{m: st.enter_context(nc.sbuf_tensor(f"rc_{m}{d}", [P, NC_, P], F32)) for m in names[1:] if m not in ("F", "G", "U0")} for d in range(2)]
        for d, m, t in ((0, "G", sig), (1, "G", av), (0, "U0", cinc), (1, "U0", z_), (0, "F", keff), (1, "F", nka)):
            M[d][m] = t[:, :, :].rearrange("p a (c n) -> p (a c) n", n=P)
        Vn = st.enter_context(nc.sbuf_tensor("rc_Vn", [P, NC_, P], F32))
        X = [st.enter_context(nc.sbuf_tensor(f"rc_X{d}", [P, NC_ + 1, P], F32)) for d in range(2)]
        tmp = st.enter_context(nc.sbuf_tensor("rc_tmp", [P, T_CTX], F32))
        turned, turn_cp, grams, masked, leveled = sem("turned"), sem("turn_copied"), sem("grams"), sem("masked"), sem("leveled")
        l0_turned, inv_ready, f_sum, f_copied, tz_sum = sem("l0_turned"), sem("inverse_ready"), sem("f_sum"), sem("f_copied"), sem("tz_sum")
        n1_sum, n1_cp, gu_sum, gu_cp, ph_sum, ph_ready = sem("n1_sum"), sem("n1_copied"), sem("gu_sum"), sem("gu_copied"), sem("ph_sum"), sem("ph_ready")
        x_sum, x_ready, y_sum = sem("x_sum"), sem("x_ready"), sem("y_sum")
        xinit = sem("x_init")
        ident = S.cst[:, C_ID:C_ID + P]
        order = [list(range(NC_)), list(range(NC_))[::-1]]

        def bank(d, b):
            return S.ps[:, 4 * d + b, :].rearrange("p (c n) -> p c n", n=P)

        def all_chunks(d, b, lhsT, rhs):
            for c in range(NC_):
                last = nc.tensor.matmul(bank(d, b)[:, c, :], lhsT[:, c, :], rhs[:, c, :], start=True, stop=True)
            return last

        with nc.Block() as block:
            @block.tensor
            def _(pe):
                pe.wait_ge(staged, 1)
                for j in range(4):
                    nc.tensor.matmul(S.ps[:, j, 0:n_tok], S.wst[:, j, :], xl[:, 0, :], start=True, stop=True).then_inc(loraed, 1)
                nc.tensor.matmul(S.ps[:, 4, 0:n_tok], S.wst[:, 4, :], xl[:, 1, :], start=True, stop=True).then_inc(loraed, 1)
                pe.wait_ge(squared, 1)
                nc.tensor.matmul(S.ps[:, 5, 0:n_tok], S.cst[:, C_ONES:C_ONES + P], sq[:, :], start=True, stop=True).then_inc(normsum, 1)
                pe.wait_ge(bonused, 1)
                nc.tensor.matmul(S.ps[:, 6, 0:n_tok], S.cst[:, C_ONES:C_ONES + P], kraw[:, :], start=True, stop=True).then_inc(summed, 1)
                for d in range(2):
                    pe.wait_ge(built[d], 1)
                    if d == 0:
                        pe.wait_ge(values_built, 2)
                        pe.wait_ge(sigmoided, 4)
                    else:
                        pe.wait_ge(rooted, 1)
                        pe.wait_ge(bonus_set, 1)
                    src = [R.bd[d][:, BA], R.bd[d][:, BBB], R.bd[d][:, BKB]] + ([R.vbd[:, :]] if d == 0 else [])
                    for b, s in enumerate(src):
                        for c in range(NC_):
                            last = nc.tensor.transpose(bank(d, b)[:, c, :], s[:, c, :], ident)
                    last.then_inc(turned, 1)
                for d in range(2):
                    pe.wait_ge(turn_cp, d + 1)
                    all_chunks(d, 0, R.bd[d][:, BB], R.bd[d][:, BA])
                    all_chunks(d, 1, R.bd[d][:, BB], R.bd[d][:, BR])
                    all_chunks(d, 2, R.bd[d][:, BK], R.bd[d][:, BA])
                    all_chunks(d, 3, R.bd[d][:, BK], R.bd[d][:, BR]).then_inc(grams, 1)
                for d in range(2):
                    pe.wait_ge(masked, d + 1)
                    pe.wait_ge(leveled, d + 1)
                    for c in range(NC_):
                        last = nc.tensor.transpose(bank(d, 0)[:, c, :], M[d]["Et"][:, c, :], ident)
                    last.then_inc(l0_turned, 1)
                for n in range(1, 6):
                    for d in range(2):
                        pe.wait_ge(inv_ready, 2 * (n - 1) + d + 1)
                        pe.wait_ge(leveled, 2 * n + d + 1)
                        all_chunks(d, 1, M[d]["Et"], M[d]["Tm"]).then_inc(f_sum, 1)
                    for d in range(2):
                        pe.wait_ge(f_copied, 2 * (n - 1) + d + 1)
                        if n < 5:
                            all_chunks(d, 2, M[d]["Z"], M[d]["F"])
                        all_chunks(d, 3, M[d]["F"], M[d]["Z"]).then_inc(tz_sum, 1)
                for d in range(2):
                    all_chunks(d, 0, M[d]["AkT"], Vn).then_inc(n1_sum, 1)
                for d in range(2):
                    pe.wait_ge(inv_ready, 10 + d + 1)
                    pe.wait_ge(n1_cp, d + 1)
                    all_chunks(d, 1, M[d]["Z"], M[d]["An"])
                    all_chunks(d, 2, M[d]["Z"], M[d]["F"]).then_inc(gu_sum, 1)
                for d in range(2):
                    pe.wait_ge(gu_cp, d + 1)
                    all_chunks(d, 3, M[d]["G"], M[d]["Bn"])
                    all_chunks(d, 0, M[d]["G"], M[d]["MbT"]).then_inc(ph_sum, 1)
                for i in range(NC_):
                    for d in range(2):
                        c = order[d][i]
                        if i >= 2:
                            pe.wait_ge(x_ready, 2 * (i - 2) + d + 1)
                        o = bank(d, 1 + i % 2)[:, 0, :]
                        nc.tensor.matmul(o, M[d]["Bn"][:, c, :], M[d]["U0"][:, c, :], start=True, stop=False)
                        nc.tensor.matmul(o, M[d]["Kn"][:, c, :], Vn[:, c, :], start=False, stop=False)
                        if i == 0:
                            pe.wait_ge(ph_ready, d + 1)
                            pe.wait_ge(xinit, d + 1)
                        else:
                            pe.wait_ge(x_ready, 2 * (i - 1) + d + 1)
                        nc.tensor.matmul(o, M[d]["LT"][:, c, :], X[d][:, i, :], start=False, stop=True).then_inc(x_sum, 1)
                for d in range(2):
                    for i in range(NC_):
                        c = order[d][i]
                        o = bank(d, 3)[:, c, :]
                        nc.tensor.matmul(o, X[d][:, i, :], M[d]["Tm"][:, c, :], start=True, stop=False)
                        nc.tensor.matmul(o, M[d]["U0"][:, c, :], M[d]["MbT"][:, c, :], start=False, stop=False)
                        last = nc.tensor.matmul(o, Vn[:, c, :], M[d]["MkT"][:, c, :], start=False, stop=True)
                    last.then_inc(y_sum, 1)

            @block.scalar
            def _(act):
                for j in range(4):
                    act.wait_ge(loraed, j + 1)
                    nc.scalar.activation((sig if j < 2 else av)[:, j % 2, :], S.ps[:, j, 0:n_tok], ACT.Sigmoid,
                                         bias=h[:, 9 + j:10 + j]).then_inc(sigmoided, 1)
                act.wait_ge(loraed, 5)
                nc.scalar.activation(R.gate[:, bass.ds(tok, n_tok)], S.ps[:, 4, 0:n_tok], ACT.Copy)
                act.wait_ge(normsum, 1)
                nc.scalar.activation(sq[:, :], S.ps[:, 5, 0:n_tok], ACT.Sqrt).then_inc(rooted, 1)
                act.wait_ge(argued, 1)
                args = [[(cinc[:, 0], -1), (y_[:, 0], -1), (cinc[:, 0], 1), (z_[:, 0], -1)],
                        [(w_[:, :], -1), (z_[:, 1], -1), (w_[:, :], 1), (y_[:, 1], -1)]]
                for d in range(2):
                    for e in range(4):
                        a, sign = args[d][e]
                        nc.scalar.activation(ex[:, d, e, :], a, ACT.Exp, scale=sign * DECAY).then_inc(exped, 1)
                    tot = cinc[:, d, :].rearrange("p (c t) -> p c t", t=CH)[:, :, CH - 1:CH]
                    nc.scalar.activation(R.wc[:, d, :].rearrange("p (c o) -> p c o", o=1), tot, ACT.Exp, scale=-DECAY)
                for d in range(2):
                    nc.scalar.activation(X[d][:, 0, :], R.last[d][:, :], ACT.Copy).then_inc(xinit, 1)
                for d in range(2):
                    act.wait_ge(turned, d + 1)
                    nc.scalar.activation(M[d]["An"][:, :, :], bank(d, 0), ACT.Copy)
                    nc.scalar.activation(M[d]["Bn"][:, :, :], bank(d, 1), ACT.Copy)
                    last = nc.scalar.activation(M[d]["Kn"][:, :, :], bank(d, 2), ACT.Copy)
                    if d == 0:
                        last = nc.scalar.activation(Vn[:, :, :], bank(d, 3), ACT.Copy)
                    last.then_inc(turn_cp, 1)
                for n in range(1, 6):
                    for d in range(2):
                        act.wait_ge(f_sum, 2 * (n - 1) + d + 1)
                        nc.scalar.activation(M[d]["F"][:, :, :], bank(d, 1), ACT.Copy).then_inc(f_copied, 1)
                for d in range(2):
                    act.wait_ge(n1_sum, d + 1)
                    act.wait_ge(tz_sum, 8 + d + 1)
                    nc.scalar.activation(M[d]["F"][:, :, :], bank(d, 0), ACT.Copy).then_inc(n1_cp, 1)
                for d in range(2):
                    act.wait_ge(gu_sum, d + 1)
                    nc.scalar.activation(M[d]["G"][:, :, :], bank(d, 1), ACT.Copy)
                    nc.scalar.activation(M[d]["U0"][:, :, :], bank(d, 2), ACT.Copy).then_inc(gu_cp, 1)
                for i in range(NC_):
                    for d in range(2):
                        act.wait_ge(x_sum, 2 * i + d + 1)
                        nc.scalar.activation(X[d][:, i + 1, :], bank(d, 1 + i % 2)[:, 0, :], ACT.Copy).then_inc(x_ready, 1)
                act.wait_ge(x_ready, 2 * NC_)
                for d in range(2):
                    nc.scalar.activation(R.last[d][:, :], X[d][:, NC_, :], ACT.Copy)

            @block.gpsimd
            def _(pool):
                nc.gpsimd.tensor_copy(xl[:, :, :], S.xlora[:, :, bass.ds(tok, n_tok)]).then_inc(staged, 1)
                nc.gpsimd.tensor_copy(rkv[:, :, :], S.prc[:, :, bass.ds(tok, n_tok)]).then_inc(staged, 1)
                pool.wait_ge(staged, 2)
                for hh in range(2):
                    p0 = hh * CH
                    nc.gpsimd.tensor_copy(R.vbd[p0:p0 + CH, :, p0:p0 + CH], v[p0:p0 + CH, :].rearrange("p (c t) -> p c t", t=CH)).then_inc(values_built, 1)
                pool.wait_ge(keyed, 1)
                pool.wait_ge(exped, 8)
                build(nc.gpsimd, 1)
                for n in range(6):
                    for d in range(2):
                        if n == 0:
                            pool.wait_ge(masked, d + 1)
                        elif n == 1:
                            pool.wait_ge(inv_ready, d + 1)
                        else:
                            pool.wait_ge(f_sum, 2 * (n - 2) + d + 1)
                        lvl = S.cst[:, C_LVL + n * P:C_LVL + (n + 1) * P].unsqueeze(1).to_broadcast([P, NC_, P])
                        nc.gpsimd.tensor_tensor(M[d]["Et"][:, :, :], M[d]["LT"][:, :, :], lvl, ALU.mult).then_inc(leveled, 1)

            @block.vector
            def _(dve):
                link = Link(dve, chain)
                dve.wait_ge(staged, 2)
                link(nc.vector.tensor_scalar(kraw[:, :], k, h[:, 13:14], None, ALU.mult))
                nc.vector.tensor_tensor(sq[:, :], kraw[:, :], kraw[:, :], ALU.mult).then_inc(squared, 1)
                dve.wait_ge(sigmoided, 2)
                for d in range(2):
                    link(nc.vector.tensor_tensor_scan(cinc[:, d, :], S.reset[:, 0:n_tok], sig[:, d, :], 0.0, ALU.mult, ALU.add))
                    nc.vector.tensor_tensor(y_[:, d, :], cinc[:, d, :], sig[:, d, :], ALU.subtract)
                    c4 = cinc[:, d, :].rearrange("p (c t) -> p c t", t=CH)
                    link(nc.vector.tensor_tensor(z_[:, d, :].rearrange("p (c t) -> p c t", t=CH),
                                                 c4[:, :, CH - 1:CH].to_broadcast([P, NC_, CH]), c4, ALU.subtract))
                nc.vector.tensor_tensor(w_[:, :], z_[:, 1, :], sig[:, 1, :], ALU.add).then_inc(argued, 1)
                dve.wait_ge(sigmoided, 4)
                for d in range(2):
                    link(nc.vector.tensor_scalar(keff[:, d, :], av[:, d, :], h[:, 14:15], h[:, 18:19], ALU.mult, ALU.add))
                    link(nc.vector.tensor_tensor(keff[:, d, :], keff[:, d, :], k, ALU.mult))
                dve.wait_ge(rooted, 1)
                link(nc.vector.tensor_scalar(sq[:, :], sq[:, :], 1e-12, None, ALU.max))
                link(nc.vector.reciprocal(sq[:, :], sq[:, :]))
                link(nc.vector.tensor_tensor(kk[:, :], kraw[:, :], sq[:, :], ALU.mult))
                for d in range(2):
                    last = nc.vector.scalar_tensor_tensor(out=nka[:, d, :], in0=kk[:, :], scalar=-1.0, in1=av[:, d, :],
                                                          op0=ALU.mult, op1=ALU.mult)
                last.then_inc(keyed, 1)
                dve.wait_ge(keyed, 1)
                link(nc.vector.tensor_tensor(kraw[:, :], keff[:, 0, :], keff[:, 1, :], ALU.add))
                nc.vector.scalar_tensor_tensor(out=kraw[:, :], in0=kraw[:, :], scalar=h[:, 15:16], in1=r,
                                               op0=ALU.mult, op1=ALU.mult).then_inc(bonused, 1)
                dve.wait_ge(exped, 4)
                build(nc.vector, 0)
                dve.wait_ge(summed, 1)
                nc.vector.tensor_tensor(R.bonus[:, bass.ds(tok, n_tok)], S.ps[:, 6, 0:n_tok], v, ALU.mult).then_inc(bonus_set, 1)
                idb = ident.unsqueeze(1).to_broadcast([P, NC_, P])
                for d in range(2):
                    dve.wait_ge(grams, d + 1)
                    for b, (m, inc) in enumerate((("LT", 0), ("MbT", 1), ("AkT", 0), ("MkT", 1))):
                        a = C_MASK + (2 * d + inc) * P
                        last = nc.vector.tensor_tensor(M[d][m][:, :, :], bank(d, b),
                                                       S.cst[:, a:a + P].unsqueeze(1).to_broadcast([P, NC_, P]), ALU.mult)
                    last.then_inc(masked, 1)
                for d in range(2):
                    dve.wait_ge(leveled, d + 1)
                    nc.vector.tensor_tensor(M[d]["Z"][:, :, :], M[d]["Et"][:, :, :], idb, ALU.add)
                    dve.wait_ge(l0_turned, d + 1)
                    nc.vector.tensor_tensor(M[d]["Tm"][:, :, :], bank(d, 0), idb, ALU.add).then_inc(inv_ready, 1)
                for n in range(1, 6):
                    for d in range(2):
                        dve.wait_ge(tz_sum, 2 * (n - 1) + d + 1)
                        dve.wait_ge(inv_ready, 2 * (n - 1) + d + 1)
                        if n < 5:
                            nc.vector.tensor_tensor(M[d]["Tm"][:, :, :], M[d]["Tm"][:, :, :], bank(d, 2), ALU.add)
                        nc.vector.tensor_tensor(M[d]["Z"][:, :, :], M[d]["Z"][:, :, :], bank(d, 3), ALU.add).then_inc(inv_ready, 1)
                for d in range(2):
                    dve.wait_ge(ph_sum, d + 1)
                    for c in range(NC_):
                        nc.vector.scalar_tensor_tensor(out=M[d]["LT"][:, c, :], in0=ident, scalar=R.wc[:, d, c:c + 1],
                                                       in1=bank(d, 3)[:, c, :], op0=ALU.mult, op1=ALU.add)
                    nc.vector.tensor_tensor(M[d]["Tm"][:, :, :], bank(d, 0), R.bd[d][:, BR], ALU.add).then_inc(ph_ready, 1)
                for d in range(2):
                    dve.wait_ge(y_sum, d + 1)
                    both = bank(d, 3).rearrange("p c (h t) -> p c t h", h=2)
                    dst = R.y[:, bass.ds(tok, T_CTX)].rearrange("p (c t) -> p c t", t=CH) if d == 0 else tmp[:, :].rearrange("p (c t) -> p c t", t=CH)
                    link(nc.vector.tensor_reduce(dst, both, AX.X, ALU.add))
                nc.vector.tensor_tensor(R.y[:, bass.ds(tok, T_CTX)], R.y[:, bass.ds(tok, T_CTX)], tmp[:, :], ALU.add)
        clear_block(nc, [staged, loraed, sigmoided, squared, normsum, rooted, argued, exped, chain, bonused, summed, keyed, *built, values_built, bonus_set,
                         turned, turn_cp, grams, masked, leveled, l0_turned, inv_ready, f_sum, f_copied, tz_sum, n1_sum, n1_cp, gu_sum, gu_cp, ph_sum, ph_ready, x_sum, x_ready, y_sum, xinit])


def rwkv_finish(nc, S, R, hp):
    with ExitStack() as st:
        sem = lambda m: st.enter_context(nc.semaphore("rf_" + m))
        sq = st.enter_context(nc.sbuf_tensor("rf_sq", [P, T], F32))
        meaned, centred, squared, vared, rooted, chain = sem("meaned"), sem("centred"), sem("squared"), sem("vared"), sem("rooted"), sem("chain")
        ones = S.cst[:, C_ONES:C_ONES + P]
        with nc.Block() as block:
            @block.gpsimd
            def _(pool):
                for d in range(2):
                    nc.gpsimd.memset(R.last[d][:, :], 0.0)

            @block.tensor
            def _(pe):
                nc.tensor.matmul(S.ps[:, 0, :], ones, R.y[:, :], start=True, stop=True).then_inc(meaned, 1)
                pe.wait_ge(squared, 1)
                nc.tensor.matmul(S.ps[:, 1, :], ones, sq[:, :], start=True, stop=True).then_inc(vared, 1)

            @block.scalar
            def _(act):
                act.wait_ge(centred, 1)
                nc.scalar.activation(sq[:, :], R.y[:, :], ACT.Square).then_inc(squared, 1)
                act.wait_ge(centred, 2)
                nc.scalar.activation(sq[:, :], sq[:, :], ACT.Sqrt).then_inc(rooted, 1)

            @block.vector
            def _(dve):
                link = Link(dve, chain)
                dve.wait_ge(meaned, 1)
                nc.vector.scalar_tensor_tensor(out=R.y[:, :], in0=S.ps[:, 0, :], scalar=-1.0 / CH, in1=R.y[:, :],
                                               op0=ALU.mult, op1=ALU.add).then_inc(centred, 1)
                dve.wait_ge(vared, 1)
                nc.vector.tensor_scalar(sq[:, :], S.ps[:, 1, :], 1.0 / CH, 64e-5, ALU.mult, ALU.add).then_inc(centred, 1)
                dve.wait_ge(rooted, 1)
                link(nc.vector.reciprocal(sq[:, :], sq[:, :]))
                link(nc.vector.tensor_tensor(R.y[:, :], R.y[:, :], sq[:, :], ALU.mult))
                link(nc.vector.tensor_scalar(R.y[:, :], R.y[:, :], S.hcol[:, 16:17], S.hcol[:, 17:18], ALU.mult, ALU.add))
                link(nc.vector.tensor_tensor(R.y[:, :], R.y[:, :], R.bonus[:, :], ALU.add))
                nc.vector.tensor_tensor(S.oT[:, bass.ds(hp + HP, 1), :].rearrange("p o t -> p (o t)"), R.y[:, :], R.gate[:, :], ALU.mult)
        clear_block(nc, [meaned, centred, squared, vared, rooted, chain])


LN_EPS = 1e-5


def load_projection(eng, wout, project, full):
    for hf in range(2):
        eng.dma_start(wout[:, hf], project.rearrange("(k p) n -> p k n", p=P)[:, :, hf * 512:(hf + 1) * 512]).then_inc(full[hf], 16)


def post_block(nc, g, S, l, n, blocks, project=None, ahead=None, load_h=False):
    blocks = list(blocks)
    with ExitStack() as st:
        sem = lambda m: st.enter_context(nc.semaphore(f"po{l}{n}_" + m))
        sb = lambda m, s: st.enter_context(nc.sbuf_tensor(f"po{l}{n}_" + m, s, F32))
        gate = sb("gate", [P, 2, D])
        lng, lnb, t_ = sb("ln_g", [P, D]), sb("ln_b", [P, D]), sb("t", [P, 2, D])
        stat, agg, rstd = sb("stat", [P, NB, 2, 6]), sb("agg", [P, NB, 2]), sb("rstd", [P, NB])
        hl, lnl = sem("h_loaded"), sem("ln_loaded")
        if ahead:
            wout, wl = ahead
        else:
            wout = sb("w_out", [P, 2, KD, 512]) if project is not None else None
            wl = [sem("w_loaded0"), sem("w_loaded1")]
        gsum, gcp, proj, chain, vared, rooted, used, normed = (sem("gate_sum"), sem("gate_copied"), sem("projected"), sem("chain"),
                                                               sem("vared"), sem("rooted"), sem("used"), sem("normed"))
        gidx = 2 if n == 0 else 5
        sides = [0, 1] if blocks[0] == 0 else [1]
        with phase(nc, [hl, lnl, *wl, gsum, gcp, proj, chain, vared, rooted, used, normed]) as block:
            @block.sync
            def _(sp):
                if project is not None and not ahead:
                    load_projection(sp, wout, project, wl)
                if load_h:
                    load_tokens(sp, g, S.h, hl)
                sp.dma_start(lng[:, :], g.ln_g[l, n:n + 1, :].to_broadcast([P, D])).then_inc(lnl, 16)
                sp.dma_start(lnb[:, :], g.ln_b[l, n:n + 1, :].to_broadcast([P, D])).then_inc(lnl, 16)

            @block.tensor
            def _(pe):
                for side in sides:
                    for k in range(KD):
                        col = S.mcol[:, l, 1 - side, gidx * KD + k:gidx * KD + k + 1]
                        last = nc.tensor.matmul(S.ps[:, 4 + 2 * side + k // 4, (k % 4) * P:(k % 4 + 1) * P],
                                                col.to_broadcast([P, P]), S.cst[:, C_ID:C_ID + P], start=True, stop=True)
                last.then_inc(gsum, 1)
                if project is not None:
                    for i, b in enumerate(blocks):
                        if i >= 2:
                            pe.wait_ge(used, i - 1)
                        for hf in range(2):
                            if i == 0:
                                pe.wait_ge(wl[hf], 16)
                            for k in range(KD):
                                last = nc.tensor.matmul(S.ps[:, 2 * (i % 2) + hf, :], S.oT[:, k, b * P:(b + 1) * P],
                                                        wout[:, hf, k, :], start=(k == 0), stop=(k == KD - 1))
                        last.then_inc(proj, 1)

            @block.scalar
            def _(act):
                act.wait_ge(gsum, 1)
                for side in sides:
                    nc.scalar.activation(gate[:, side, :].rearrange("p (a n) -> p a n", a=2),
                                         S.ps[:, 4 + 2 * side:6 + 2 * side, :], ACT.Copy).then_inc(gcp, 1)
                for i in range(len(blocks)):
                    act.wait_ge(vared, i + 1)
                    nc.scalar.activation(rstd[:, i:i + 1], agg[:, i, 1:2], ACT.Sqrt).then_inc(rooted, 1)

            @block.vector
            def _(dve):
                link = Link(dve, chain)
                dve.wait_ge(gcp, len(sides))
                if load_h:
                    dve.wait_ge(hl, 32)
                for i, b in enumerate(blocks):
                    t = t_[:, i % 2, :]
                    if project is not None:
                        dve.wait_ge(proj, i + 1)
                        y = S.ps[:, 2 * (i % 2):2 * (i % 2) + 2, :]
                    else:
                        y = S.acc[:, b, :].rearrange("p (a n) -> p a n", a=2)
                    nc.vector.tensor_tensor(t.rearrange("p (a n) -> p a n", a=2), y,
                                            gate[:, b // 2, :].rearrange("p (a n) -> p a n", a=2), ALU.mult).then_inc(used, 1)
                    dve.wait_ge(used, i + 1)
                    link(nc.vector.scalar_tensor_tensor(out=t, in0=S.h[:, b, :], scalar=ALPHA, in1=t, op0=ALU.mult, op1=ALU.add))
                    for a in range(2):
                        last = nc.vector.bn_stats(stat[:, i, a, :], t[:, a * 512:(a + 1) * 512])
                        link(last)
                    link(nc.vector.bn_aggr(agg[:, i, :], stat[:, i, :, :].rearrange("p a s -> p (a s)")))
                    nc.vector.tensor_scalar(agg[:, i, 1:2], agg[:, i, 1:2], LN_EPS, None, ALU.add).then_inc(vared, 1)
                    dve.wait_ge(rooted, i + 1)
                    link(nc.vector.reciprocal(rstd[:, i:i + 1], rstd[:, i:i + 1]))
                    nc.vector.tensor_scalar(S.h[:, b, :], t, agg[:, i, 0:1], rstd[:, i:i + 1], ALU.subtract, ALU.mult).then_inc(normed, 1)

            @block.gpsimd
            def _(pool):
                pool.wait_ge(lnl, 32)
                for i, b in enumerate(blocks):
                    pool.wait_ge(normed, i + 1)
                    nc.gpsimd.tensor_tensor(S.h[:, b, :], S.h[:, b, :], lng[:, :], ALU.mult).then_inc(hl, 1)
                    pool.wait_ge(hl, (32 if load_h else 0) + i + 1)
                    nc.gpsimd.tensor_tensor(S.h[:, b, :], S.h[:, b, :], lnb[:, :], ALU.add)


def router_block(nc, g, S, l, blocks, load_ahead):
    blocks = list(blocks)
    nb = len(blocks)
    with ExitStack() as st:
        sem = lambda m: st.enter_context(nc.semaphore(f"ro{l}_" + m))
        sb = lambda m, s: st.enter_context(nc.sbuf_tensor(f"ro{l}_" + m, s, F32))
        s_, sel, pair, cmp_, rank = (sb("s", [P, nb, 4, 4]), sb("sel", [P, nb, 4, 4]), sb("pair", [P, nb, 4]), sb("cmp", [P, nb, 4, 4]),
                                     sb("rank", [P, nb, 4, 4]))
        top, grank, gcmp, tot = sb("top", [P, nb, 4]), sb("grank", [P, nb, 4]), sb("gcmp", [P, nb, 4]), sb("tot", [P, nb])
        chosen, most = sb("chosen", [P, nb, N_EXP]), sb("most", [P, 3 + N_ITEM])
        cnt, tmp = sb("counts", [P, 3, N_EXP]), sb("tmp", [P, N_ITEM, N_EXP])
        row, rest, most2 = sb("row", [P, nb, N_EXP]), sb("rest", [P, nb, N_EXP]), sb("most2", [P, 2, nb])
        scored, sgm, chain, picked, counted = sem("scored"), sem("sigmoided"), sem("chain"), sem("picked"), sem("counted")
        block = st.enter_context(phase(nc, [scored, sgm, chain, picked, counted]))

        @block.sync
        def _(sp):
            load_ahead(sp)

        @block.tensor
        def _(pe):
            for i, b in enumerate(blocks):
                for k in range(KD):
                    last = nc.tensor.matmul(S.ps[:, 0, i * N_EXP:(i + 1) * N_EXP], S.uT[:, k, b * P:(b + 1) * P], S.router[:, k, :],
                                            start=(k == 0), stop=(k == KD - 1))
            last.then_inc(scored, 1)
            pe.wait_ge(picked, 1)
            for i in range(nb):
                for j in range(i + 1):
                    m = C_TRI if j == i else C_ALL
                    nc.tensor.matmul(S.ps[:, 1, i * N_EXP:(i + 1) * N_EXP], S.cst[:, m:m + P], chosen[:, j, :], start=(j == 0), stop=(j == i))
            for j in range(nb):
                last = nc.tensor.matmul(S.ps[:, 2, 0:N_EXP], S.cst[:, C_ALL:C_ALL + P], chosen[:, j, :], start=(j == 0), stop=(j == nb - 1))
            last.then_inc(counted, 1)

        @block.scalar
        def _(act):
            act.wait_ge(scored, 1)
            nc.scalar.activation(s_[:, :, :, :], S.ps[:, 0, 0:nb * N_EXP].rearrange("p (b g e) -> p b g e", g=4, e=4),
                                 ACT.Sigmoid).then_inc(sgm, 1)

        @block.vector
        def _(dve):
            link = Link(dve, chain)
            dve.wait_ge(sgm, 1)
            flat = lambda t: t[:, :, :, :].rearrange("p b g e -> p b (g e)")
            link(nc.vector.tensor_tensor(flat(sel), flat(s_), S.rbias[:, :].unsqueeze(1).to_broadcast([P, nb, N_EXP]), ALU.add))
            first = True
            for i in range(4):
                for j in range(i + 1, 4):
                    o = top if first else pair
                    link(nc.vector.tensor_tensor(o[:, :, :], sel[:, :, :, i], sel[:, :, :, j], ALU.add))
                    if not first:
                        link(nc.vector.tensor_tensor(top[:, :, :], top[:, :, :], pair[:, :, :], ALU.max))
                    first = False
            link(nc.vector.memset(grank[:, :, :], 0.0))
            link(nc.vector.memset(rank[:, :, :, :], 0.0))
            for j in range(4):
                for lo, hi, op in ((0, j, ALU.is_gt), (j + 1, 4, ALU.is_ge)):
                    if hi > lo:
                        w = hi - lo
                        link(nc.vector.tensor_tensor(gcmp[:, :, lo:hi], top[:, :, j:j + 1].to_broadcast([P, nb, w]), top[:, :, lo:hi], op))
                        link(nc.vector.tensor_tensor(grank[:, :, lo:hi], grank[:, :, lo:hi], gcmp[:, :, lo:hi], ALU.add))
                        link(nc.vector.tensor_tensor(cmp_[:, :, :, lo:hi], sel[:, :, :, j:j + 1].to_broadcast([P, nb, 4, w]),
                                                     sel[:, :, :, lo:hi], op))
                        link(nc.vector.tensor_tensor(rank[:, :, :, lo:hi], rank[:, :, :, lo:hi], cmp_[:, :, :, lo:hi], ALU.add))
            link(nc.vector.tensor_scalar(grank[:, :, :], grank[:, :, :], 0.5, None, ALU.is_lt))
            link(nc.vector.tensor_scalar(rank[:, :, :, :], rank[:, :, :, :], 1.5, None, ALU.is_lt))
            link(nc.vector.tensor_tensor(rank[:, :, :, :], rank[:, :, :, :], grank[:, :, :].unsqueeze(3).to_broadcast([P, nb, 4, 4]), ALU.mult))
            nc.vector.tensor_copy(chosen[:, :, :], flat(rank)).then_inc(picked, 1)
            dve.wait_ge(picked, 1)
            link(nc.vector.tensor_tensor(flat(rank), flat(rank), flat(s_), ALU.mult))
            link(nc.vector.tensor_reduce(tot[:, :], flat(rank), AX.X, ALU.add))
            link(nc.vector.reciprocal(tot[:, :], tot[:, :]))
            nc.vector.tensor_tensor(S.combine[:, blocks[0]:blocks[-1] + 1, :], flat(rank), tot[:, :].unsqueeze(2).to_broadcast([P, nb, N_EXP]), ALU.mult)
            dve.wait_ge(counted, 1)
            place = S.place[:, blocks[0]:blocks[-1] + 1, :]
            link(nc.vector.scalar_tensor_tensor(out=place, in0=S.ps[:, 1, 0:nb * N_EXP].rearrange("p (b e) -> p b e", b=nb), scalar=1.0,
                                                in1=chosen[:, :, :], op0=ALU.add, op1=ALU.mult))
            link(nc.vector.tensor_scalar(place, place, -1.0, None, ALU.add))
            n_, first_, last_ = cnt[:, 0, :], cnt[:, 1, :], cnt[:, 2, :]
            link(nc.vector.tensor_scalar(n_, S.ps[:, 2, 0:N_EXP], 0.5, None, ALU.is_gt))
            for r in range(1, nb):
                link(nc.vector.tensor_scalar(first_, S.ps[:, 2, 0:N_EXP], r * P + 0.5, None, ALU.is_gt))
                link(nc.vector.tensor_tensor(n_, n_, first_, ALU.add))
            link(nc.vector.tensor_scalar(n_[:, 0:1], n_[:, 0:1], 1.0, None, ALU.max))
            link(nc.vector.tensor_tensor_scan(last_, S.cst[:, C_ALL:C_ALL + N_EXP], n_, 0.0, ALU.mult, ALU.add))
            link(nc.vector.tensor_tensor(first_, last_, n_, ALU.subtract))
            link(nc.vector.tensor_scalar(first_, first_, float(P), None, ALU.mult))
            link(nc.vector.tensor_tensor(row[:, :, :], place, first_.unsqueeze(1).to_broadcast([P, nb, N_EXP]), ALU.add))
            link(nc.vector.tensor_scalar(rest[:, :, :], row[:, :, :], -1.0, float(ROWS), ALU.mult, ALU.add))
            link(nc.vector.tensor_tensor(rest[:, :, :], rest[:, :, :], chosen[:, :, :], ALU.mult))
            link(nc.vector.scalar_tensor_tensor(out=row[:, :, :], in0=row[:, :, :], scalar=1.0, in1=chosen[:, :, :], op0=ALU.add, op1=ALU.mult))
            for n, r in ((0, row), (1, rest)):
                best = most2[:, n, :]
                link(nc.vector.tensor_reduce(best, r[:, :, :], AX.X, ALU.max))
                link(nc.vector.tensor_tensor(r[:, :, :], r[:, :, :], best.unsqueeze(2).to_broadcast([P, nb, N_EXP]), ALU.is_equal))
                link(nc.vector.tensor_tensor(r[:, :, :], r[:, :, :], S.combine[:, blocks[0]:blocks[-1] + 1, :], ALU.mult))
                link(nc.vector.tensor_reduce(S.two_gates[:, n, blocks[0]:blocks[-1] + 1], r[:, :, :], AX.X, ALU.add))
            link(nc.vector.tensor_scalar(most2[:, 0, :], most2[:, 0, :], -1.0, None, ALU.add))
            link(nc.vector.tensor_scalar(most2[:, 1, :], most2[:, 1, :], -1.0, float(ROWS), ALU.mult, ALU.add))
            nc.vector.tensor_copy(S.two_rows[:, :, blocks[0]:blocks[-1] + 1], most2[:, :, :])
            link(nc.vector.tensor_tensor(tmp[:, :, :], S.cst[:, C_JIDX:C_JIDX + N_ITEM].unsqueeze(2).to_broadcast([P, N_ITEM, N_EXP]),
                                         last_.unsqueeze(1).to_broadcast([P, N_ITEM, N_EXP]), ALU.is_ge))
            link(nc.vector.tensor_reduce(most[:, 3:3 + N_ITEM], tmp[:, :, :], AX.X, ALU.add))
            link(nc.vector.tensor_scalar(most[:, 3:3 + N_ITEM], most[:, 3:3 + N_ITEM], float(N_EXP - 1), None, ALU.min))
            nc.vector.tensor_copy(S.item_expert[:, :], most[:, 3:3 + N_ITEM])
            link(nc.vector.memset(most[:, 1:2], 1.0))
            for r in range(1, MAX_STEPS):
                link(nc.vector.tensor_scalar(most[:, 2:3], cnt[:, 2, N_EXP - 1:N_EXP], 2 * r + TAIL[l] + 0.5, None, ALU.is_gt))
                link(nc.vector.tensor_tensor(most[:, 1:2], most[:, 1:2], most[:, 2:3], ALU.add))
            nc.vector.tensor_copy(S.pairs[:, :], most[:, 1:2])


def dispatch_block(nc, g, S, l, blocks, load_ahead):
    blocks = list(blocks)
    with ExitStack() as st:
        turned, copied, sent = [st.enter_context(nc.semaphore(f"tm{l}_{m}")) for m in ("turned", "copied", "sent")]
        uN = st.enter_context(nc.sbuf_tensor(f"tm{l}_tokens", [P, NB, D], F32))
        block = st.enter_context(phase(nc, [turned, copied, sent]))
        jobs = [(b, k4) for b in blocks for k4 in range(KD // 4)]

        @block.sync
        def _(sp):
            load_ahead(sp)

        @block.tensor
        def _(pe):
            for j, (b, k4) in enumerate(jobs):
                if j >= 4:
                    pe.wait_ge(copied, j - 3)
                for k in range(4):
                    last = nc.tensor.transpose(S.ps[:, j % 4, k * P:(k + 1) * P], S.uT[:, k4 * 4 + k, b * P:(b + 1) * P],
                                               S.cst[:, C_ID:C_ID + P])
                last.then_inc(turned, 1)

        @block.scalar
        def _(act):
            for j, (b, k4) in enumerate(jobs):
                act.wait_ge(turned, j + 1)
                nc.scalar.activation(uN[:, b, k4 * 512:(k4 + 1) * 512], S.ps[:, j % 4, :], ACT.Copy).then_inc(copied, 1)

        @block.gpsimd
        def _(pool):
            for i, b in enumerate(blocks):
                pool.wait_ge(copied, 2 * (i + 1))
                for n in range(2):
                    nc.gpsimd.indirect_dma_start(out=g.item_x[:, :], out_offset=bass.IndirectOffsetOnAxis(ap=S.two_rows[:, n, b:b + 1], axis=0),
                                                 in_=uN[:, b, :], in_offset=None).then_inc(sent, 16)
            pool.wait_ge(sent, 16 * 2 * len(blocks))


def combine_block(nc, g, S, l, blocks):
    blocks = list(blocks)
    with ExitStack() as st:
        got = [st.enter_context(nc.semaphore(f"cb{l}_block{b}_rows_in")) for b in blocks]
        first = st.enter_context(nc.semaphore(f"cb{l}_first_done"))
        yg = st.enter_context(nc.sbuf_tensor(f"cb{l}_y", [P, len(blocks), 2, D], F32))
        block = st.enter_context(phase(nc, [*got, first]))

        @block.gpsimd
        def _(pool):
            for i, b in enumerate(blocks):
                for n in range(2):
                    nc.gpsimd.indirect_dma_start(out=yg[:, i, n, :], out_offset=None, in_=g.item_y[:, :],
                                                 in_offset=bass.IndirectOffsetOnAxis(ap=S.two_rows[:, n, b:b + 1], axis=0)).then_inc(got[i], 16)

        @block.vector
        def _(dve):
            for i, b in enumerate(blocks):
                dve.wait_ge(got[i], 32)
                nc.vector.tensor_scalar(S.acc[:, b, :], yg[:, i, 0, :], S.two_gates[:, 0, b:b + 1], None, ALU.mult).then_inc(first, 1)
                dve.wait_ge(first, i + 1)
                nc.vector.scalar_tensor_tensor(out=S.acc[:, b, :], in0=yg[:, i, 1, :], scalar=S.two_gates[:, 1, b:b + 1], in1=S.acc[:, b, :],
                                               op0=ALU.mult, op1=ALU.add)


def moe(nc, g, S, l, blocks):
    FC = D_EXP // P
    with ExitStack() as st:
        sem = lambda m: st.enter_context(nc.semaphore(f"mo{l}_" + m))
        sb = lambda m, s: st.enter_context(nc.sbuf_tensor(f"mo{l}_" + m, s, F32))
        wg, wu, wd = sb("w_gate", [P, 2, KD, D_EXP]), sb("w_up", [P, 2, KD, D_EXP]), sb("w_down", [P, 2, FC, D])
        xN, xT, y = sb("xN", [P, 2, D]), sb("xT", [P, 2, KD, P]), sb("y", [P, 2, D])
        he, heT, sg = sb("he", [P, D_EXP]), sb("heT", [P, FC, P]), sb("silu", [P, D_EXP])
        gfull, dfull = [sem(f"gate_up_full{x}") for x in range(2)], [sem(f"down_full{x}") for x in range(2)]
        stored = [sem(f"y_stored{x}") for x in range(2)]
        xfull1 = sem("x_full1")
        names = ["x_full0", "xt_ready", "xt_copied", "gate_ready", "up_ready", "silu_done", "he_done", "het_ready", "het_copied",
                 "y_ready", "y_copied"]
        sems = [sem(m) for m in names]
        (xfull0, xt_ready, xt_copied, gate_ready, up_ready, silu_done, he_done, het_ready, het_copied, y_ready, y_copied) = sems
        xfull = [xfull0, xfull1]
        ident = S.cst[:, C_ID:C_ID + P]
        src = [w[l].rearrange("e (k p) n -> e p k n", p=P) for w in (g.exp_w_gate, g.exp_w_up, g.exp_w_down)]

        def load_gate_up(eng, x, e):
            for w, dst in ((0, wg), (1, wu)):
                eng.dma_start(dst[:, x], src[w][bass.ds(e, 1)].rearrange("o p k n -> p (o k) n")).then_inc(gfull[x], 16)

        def load_down(eng, x, e):
            eng.dma_start(wd[:, x], src[2][bass.ds(e, 1)].rearrange("o p k n -> p (o k) n")).then_inc(dfull[x], 16)

        def load_x(eng, x, item):
            eng.dma_start(xN[:, x, :], g.item_x[bass.ds(item * P, P), :]).then_inc(xfull[x], 16)

        def expert_of(eng, item):
            return eng.value_load(S.item_expert[0:1, bass.ds(item, 1)], min_val=0, max_val=N_EXP - 1)

        def turn_x(pe, n, buf):
            pe.wait_ge(xfull[buf], 16)
            for hf in range(2):
                for k in range(4):
                    last = nc.tensor.transpose(S.ps[:, 2 + 2 * n + hf, k * P:(k + 1) * P],
                                               xN[:, buf, (4 * hf + k) * P:(4 * hf + k + 1) * P], ident)
                last.then_inc(xt_ready, 1)

        def take_xt(act, n, buf):
            for hf in range(2):
                act.wait_ge(xt_ready, 2 * n + hf + 1)
                nc.scalar.activation(xT[:, buf, 4 * hf:4 * hf + 4, :], S.ps[:, 2 + 2 * n + hf, :].rearrange("p (k t) -> p k t", t=P),
                                     ACT.Copy).then_inc(xt_copied, 1)

        def load_weights(sp, x, e):
            load_gate_up(sp, x, e)
            load_down(sp, x, e)

        router_block(nc, g, S, l, blocks, lambda sp: load_weights(sp, 0, 0))
        dispatch_block(nc, g, S, l, blocks, lambda sp: load_weights(sp, 1, expert_of(sp, 1)))
        with phase(nc, sems) as block:
            @block.sync
            def _(sp):
                for x in range(2):
                    load_x(sp, x, x)

            @block.gpsimd
            def _(pool):
                nc.gpsimd.memset(y[:, :, :], 0.0).then_inc(y_ready, 1)

            @block.tensor
            def _(pe):
                turn_x(pe, 0, 0)

            @block.scalar
            def _(act):
                act.wait_ge(y_ready, 1)
                for x in range(2):
                    act.dma_start(g.item_y[(N_ITEM - 2 + x) * P:(N_ITEM - 1 + x) * P, :], y[:, x, :]).then_inc(stored[x], 16)
                take_xt(act, 0, 0)

        def step_block(first, steps, ahead):
            with phase(nc, sems) as block:
                @block.sync
                def _(sp):
                    if ahead:
                        load_x(sp, 0, first + 2)
                    for x in range(ahead):
                        e = expert_of(sp, first + (x + 2))
                        sp.wait_ge(up_ready, x + 1)
                        if steps == 2:
                            sp.sem_clear(gfull[x])
                        load_gate_up(sp, x, e)
                        if x == 0 and ahead == 2:
                            sp.wait_ge(xt_ready, 2)
                            sp.sem_clear(xfull[1])
                            load_x(sp, 1, first + 3)
                        sp.wait_ge(y_ready, 2 * (x + 1))
                        if steps == 2:
                            sp.sem_clear(dfull[x])
                        load_down(sp, x, e)

                @block.tensor
                def _(pe):
                    for s in range(steps):
                        x = s % 2
                        pe.wait_ge(gfull[x], 32 * (s // 2 + 1))
                        if s:
                            pe.wait_ge(xt_copied, 2 * s)
                            pe.wait_ge(he_done, s)
                        for bank, w, rdy in ((0, wg, gate_ready), (1, wu, up_ready)):
                            for k in range(KD):
                                last = nc.tensor.matmul(S.ps[:, bank, :], xT[:, x, k, :], w[:, x, k, :], start=(k == 0), stop=(k == KD - 1))
                            last.then_inc(rdy, 1)
                        if s + 1 < steps + ahead and s < 2:
                            turn_x(pe, s, 1 - x)
                        pe.wait_ge(he_done, s + 1)
                        if s:
                            pe.wait_ge(y_copied, 2 * s)
                        for f in range(FC):
                            last = nc.tensor.transpose(S.ps[:, 6, f * P:(f + 1) * P], he[:, f * P:(f + 1) * P], ident)
                        last.then_inc(het_ready, 1)
                        pe.wait_ge(het_copied, s + 1)
                        pe.wait_ge(dfull[x], 16 * (s // 2 + 1))
                        for hf in range(2):
                            for f in range(FC):
                                last = nc.tensor.matmul(S.ps[:, 7 - hf, :], heT[:, f, :], wd[:, x, f, hf * 512:(hf + 1) * 512],
                                                        start=(f == 0), stop=(f == FC - 1))
                            last.then_inc(y_ready, 1)

                @block.scalar
                def _(act):
                    for s in range(steps):
                        x = s % 2
                        act.wait_ge(gate_ready, s + 1)
                        if s:
                            act.wait_ge(he_done, s)
                        nc.scalar.activation(sg[:, :], S.ps[:, 0, :], ACT.Silu).then_inc(silu_done, 1)
                        act.wait_ge(het_ready, s + 1)
                        if s:
                            act.wait_ge(y_ready, 2 * s)
                        nc.scalar.activation(heT[:, :, :], S.ps[:, 6, :].rearrange("p (f t) -> p f t", t=P), ACT.Copy).then_inc(het_copied, 1)
                        if s + 1 < steps + ahead and s < 2:
                            take_xt(act, s, 1 - x)
                        act.wait_ge(stored[x], 16)
                        act.sem_clear(stored[x])
                        for hf in range(2):
                            act.wait_ge(y_ready, 2 * s + hf + 1)
                            nc.scalar.activation(y[:, x, hf * 512:(hf + 1) * 512], S.ps[:, 7 - hf, :], ACT.Copy).then_inc(y_copied, 1)
                        act.wait_ge(y_copied, 2 * s + 2)
                        act.dma_start(g.item_y[bass.ds((first + s) * P, P), :], y[:, x, :]).then_inc(stored[x], 16)

                @block.vector
                def _(dve):
                    for s in range(steps):
                        dve.wait_ge(silu_done, s + 1)
                        dve.wait_ge(up_ready, s + 1)
                        if s:
                            dve.wait_ge(het_ready, s)
                        nc.vector.tensor_tensor(he[:, :], sg[:, :], S.ps[:, 1, :], ALU.mult).then_inc(he_done, 1)

        n_steps = nc.values_load(S.pairs[0:1, 0:1], min_val=1, max_val=MAX_STEPS)
        with nc.Fori(0, n_steps) as it:
            step_block(it * 2, 2, 2)
        step_block(n_steps * 2, TAIL[l], TAIL[l] - 2)
        with nc.Block() as block:
            @block.sync
            def _(sp):
                for x in range(2):
                    sp.wait_ge(stored[x], 16)
        clear_block(nc, gfull + dfull + stored + [xfull1])


def odd_mixer(nc, g, S, l, load_ahead):
    n = T_LAT
    with ExitStack() as st:
        sem = lambda m: st.enter_context(nc.semaphore("da_" + m))
        sb = lambda m, s: st.enter_context(nc.sbuf_tensor("da_" + m, s, F32))
        slab, rope = sb("slab", [P, 3, KD, P]), sb("rope", [P, 2, n])
        lvec, lprod, lam, subln = sb("lambda_vectors", [P, 4, HD]), sb("lprod", [P, HD]), sb("lam", [P, 4]), sb("subln", [P, P])
        qraw, kraw, q, k, v = sb("qraw", [P, n]), sb("kraw", [P, T]), sb("q", [P, n]), sb("k", [P, T]), sb("v", [P, NB, P])
        rt = sb("rotated", [P, 2, n])
        p_, a_, aT, o_ = sb("p", [P, 2, 2, T]), sb("a", [P, 2, T]), sb("aT", [P, 2, NB, P]), sb("o", [P, 2, P])
        junk = sb("junk", [P, P])
        nmax, ssum, rsum, ss, rt_, inv = sb("nmax", [P, 4]), sb("ssum", [P, 4]), sb("rsum", [P, 4]), sb("ss", [P, 2]), sb("root", [P, 2]), sb("inv", [P, 2])
        full = sem("slab_full")
        src = g.odd_w_in[0].rearrange("(k p) n -> p k n", p=P)

        def load(sp, h):
            for j in range(3):
                sp.dma_start(slab[:, j], src[:, :, bass.ds(h * P + j * 2 * DA_H * HD, P)]).then_inc(full, 16)

        once, summed_l, exped_l, ch0 = sem("once"), sem("lambda_sums"), sem("lambda_exps"), sem("lchain")
        with nc.Block() as block:
            @block.sync
            def _(sp):
                load(sp, 0)
                sp.dma_start(rope[:, :, :], g.rope.rearrange("p (a t) -> p a t", a=2)).then_inc(once, 16)
                for i, x in enumerate((g.da_lq1, g.da_lk1, g.da_lq2, g.da_lk2)):
                    sp.dma_start(lvec[:, i, :], x[0:1, :].to_broadcast([P, HD])).then_inc(once, 16)
                sp.dma_start(subln[:, :], g.da_subln_g[0:1, :].to_broadcast([P, P])).then_inc(once, 16)
                load_ahead(sp)

            @block.vector
            def _(dve):
                link = Link(dve, ch0)
                dve.wait_ge(once, 16 * 6)
                for i in range(2):
                    link(nc.vector.tensor_tensor(lprod[:, :], lvec[:, 2 * i, :], lvec[:, 2 * i + 1, :], ALU.mult))
                    nc.vector.tensor_reduce(lam[:, i:i + 1], lprod[:, :], AX.X, ALU.add).then_inc(summed_l, 1)
                    dve.wait_ge(summed_l, i + 1)
                link(nc.vector.tensor_scalar(subln[:, :], subln[:, :], 2.0 * (1.0 - LAMBDA_INIT), None, ALU.mult))
                dve.wait_ge(exped_l, 1)
                link(nc.vector.tensor_tensor(lam[:, 2:3], lam[:, 0:1], lam[:, 1:2], ALU.subtract))
                link(nc.vector.tensor_scalar(lam[:, 3:4], lam[:, 2:3], LAMBDA_INIT, None, ALU.add))

            @block.scalar
            def _(act):
                act.wait_ge(summed_l, 2)
                nc.scalar.activation(lam[:, 0:2], lam[:, 0:2], ACT.Exp).then_inc(exped_l, 1)

        clear_block(nc, [once, summed_l, exped_l, ch0])
        names = ["ready", "raw", "turned", "scored", "maxed", "exped", "diffed", "a_turned", "a_copied", "summed",
                 "squared", "scaled", "rooted", "normed", "o_turned", "chain"]
        (ready, raw, turned, scored, maxed, exped, diffed, a_turned, a_copied, summed, squared, scaled, rooted,
         normed, o_turned, chain) = [sem(m) for m in names]
        ident = S.cst[:, C_ID:C_ID + P]

        def body(h, attend=True, project=True, prefetch=True):
            with nc.Block() as block:
                if project:
                    @block.sync
                    def _(sp):
                        sp.wait_ge(ready, 3)
                        sp.sem_clear(full)
                        if prefetch:
                            load(sp, h + 2)

                @block.tensor
                def _(pe):
                    if attend:
                        for u in range(2):
                            for m in range(2):
                                nc.tensor.matmul(S.ps[:, 2 * u + m, :], q[m * HD:(m + 1) * HD, u * P:(u + 1) * P], k[m * HD:(m + 1) * HD, :],
                                                 start=True, stop=True).then_inc(scored, 1)
                    if project:
                        pe.wait_ge(full, 16 * 3)
                        for kk in range(KD):
                            last = nc.tensor.matmul(S.ps[:, 4, 0:n], slab[:, 0, kk, :], S.uT[:, kk, T_CTX:T], start=(kk == 0), stop=(kk == KD - 1))
                        last.then_inc(ready, 1)
                        for kk in range(KD):
                            last = nc.tensor.matmul(S.ps[:, 5, :], slab[:, 1, kk, :], S.uT[:, kk, :], start=(kk == 0), stop=(kk == KD - 1))
                        last.then_inc(ready, 1)
                    if attend:
                        for u in range(2):
                            pe.wait_ge(diffed, u + 1)
                            for b in range(NB):
                                last = nc.tensor.transpose(S.ps[:, 2 * u, b * P:(b + 1) * P], a_[:, u, b * P:(b + 1) * P], ident)
                            last.then_inc(a_turned, 1)
                    if project:
                        for b in range(NB):
                            for kk in range(KD):
                                last = nc.tensor.matmul(S.ps[:, 6, b * P:(b + 1) * P], S.uT[:, kk, b * P:(b + 1) * P], slab[:, 2, kk, :],
                                                        start=(kk == 0), stop=(kk == KD - 1))
                        last.then_inc(ready, 1)
                        rot = S.cst[:, C_ROT:C_ROT + P]
                        pe.wait_ge(raw, 1)
                        nc.tensor.matmul(S.ps[:, 4, n:2 * n], rot, qraw[:, :], start=True, stop=True).then_inc(turned, 1)
                        pe.wait_ge(raw, 2)
                        nc.tensor.matmul(S.ps[:, 7, 0:n], rot, kraw[:, T_CTX:T], start=True, stop=True).then_inc(turned, 1)
                    if attend:
                        for u in range(2):
                            pe.wait_ge(a_copied, u + 1)
                            for b in range(NB):
                                last = nc.tensor.matmul(S.ps[:, 2 * u + 1, 0:P], aT[:, u, b, :], v[:, b, :], start=(b == 0), stop=(b == NB - 1))
                            last.then_inc(summed, 1)
                        for u in range(2):
                            pe.wait_ge(normed, u + 1)
                            nc.tensor.transpose(S.ps[:, 2 * u, 0:P], o_[:, u, :], ident).then_inc(o_turned, 1)

                @block.scalar
                def _(act):
                    if attend:
                        for j in range(4):
                            act.wait_ge(maxed, j + 1)
                            nc.scalar.activation(p_[:, j // 2, j % 2, :], S.ps[:, j, :], ACT.Exp, bias=nmax[:, j:j + 1], scale=NA_SCALE,
                                                 accum_out=ssum[:, j:j + 1]).then_inc(exped, 1)
                    if project:
                        act.wait_ge(ready, 1)
                        nc.scalar.activation(qraw[:, :], S.ps[:, 4, 0:n], ACT.Copy).then_inc(raw, 1)
                        act.wait_ge(ready, 2)
                        nc.scalar.activation(kraw[:, :], S.ps[:, 5, :], ACT.Copy).then_inc(raw, 1)
                    if attend:
                        for u in range(2):
                            act.wait_ge(a_turned, u + 1)
                            nc.scalar.activation(aT[:, u, :, :], S.ps[:, 2 * u, :].rearrange("p (b q) -> p b q", b=NB), ACT.Copy).then_inc(a_copied, 1)
                        for u in range(2):
                            act.wait_ge(summed, u + 1)
                            if u:
                                act.wait_ge(squared, 1)
                            nc.scalar.activation(junk[:, :], S.ps[:, 2 * u + 1, 0:P], ACT.Square, accum_out=ss[:, u:u + 1]).then_inc(squared, 1)
                            act.wait_ge(scaled, u + 1)
                            nc.scalar.activation(rt_[:, u:u + 1], ss[:, u:u + 1], ACT.Sqrt).then_inc(rooted, 1)
                    if project:
                        act.wait_ge(ready, 3)
                        if attend:
                            act.wait_ge(summed, 2)
                        nc.scalar.activation(v[:, :, :], S.ps[:, 6, :].rearrange("p (b e) -> p b e", b=NB), ACT.Copy)
                    if attend:
                        for u in range(2):
                            act.wait_ge(o_turned, u + 1)
                            nc.scalar.activation(S.oT[:, bass.ds(h, 1), T_CTX + u * P:T_CTX + (u + 1) * P].rearrange("p o t -> p (o t)"),
                                                 S.ps[:, 2 * u, 0:P], ACT.Copy)

                @block.vector
                def _(dve):
                    link = Link(dve, chain)
                    if attend:
                        for j in range(4):
                            dve.wait_ge(scored, j + 1)
                            link(nc.vector.tensor_reduce(nmax[:, j:j + 1], S.ps[:, j, :], AX.X, ALU.max, negate=True))
                            nc.vector.tensor_scalar(nmax[:, j:j + 1], nmax[:, j:j + 1], NA_SCALE, None, ALU.mult).then_inc(maxed, 1)
                        for u in range(2):
                            dve.wait_ge(exped, 2 * u + 2)
                            link(nc.vector.reciprocal(rsum[:, 2 * u:2 * u + 2], ssum[:, 2 * u:2 * u + 2]))
                            link(nc.vector.tensor_scalar(rsum[:, 2 * u + 1:2 * u + 2], rsum[:, 2 * u + 1:2 * u + 2], lam[:, 3:4], None, ALU.mult))
                            link(nc.vector.tensor_scalar(p_[:, u, 1, :], p_[:, u, 1, :], rsum[:, 2 * u + 1:2 * u + 2], None, ALU.mult))
                            nc.vector.scalar_tensor_tensor(out=a_[:, u, :], in0=p_[:, u, 0, :], scalar=rsum[:, 2 * u:2 * u + 1], in1=p_[:, u, 1, :],
                                                           op0=ALU.mult, op1=ALU.subtract).then_inc(diffed, 1)
                    if project:
                        for i, (r, rb, c0, out) in enumerate(((qraw[:, :], 4, n, q[:, :]), (kraw[:, T_CTX:T], 7, 0, k[:, T_CTX:T]))):
                            dve.wait_ge(turned, i + 1)
                            if i:
                                nc.vector.tensor_copy(k[:, 0:T_CTX], kraw[:, 0:T_CTX])
                            nc.vector.tensor_tensor(rt[:, i, :], S.ps[:, rb, c0:c0 + n], rope[:, 1, :], ALU.mult)
                            link(nc.vector.tensor_tensor(out, r, rope[:, 0, :], ALU.mult))
                            nc.vector.tensor_tensor(out, out, rt[:, i, :], ALU.add)
                    if attend:
                        for u in range(2):
                            dve.wait_ge(squared, u + 1)
                            nc.vector.tensor_scalar(ss[:, u:u + 1], ss[:, u:u + 1], 1.0 / P, 1e-5, ALU.mult, ALU.add).then_inc(scaled, 1)
                            dve.wait_ge(rooted, u + 1)
                            r_, i_ = rt_[:, u:u + 1], inv[:, u:u + 1]
                            link(nc.vector.reciprocal(i_, r_))
                            link(nc.vector.scalar_tensor_tensor(out=r_, in0=i_, scalar=ss[:, u:u + 1], in1=r_, op0=ALU.mult, op1=ALU.add))
                            link(nc.vector.reciprocal(i_, r_))
                            nc.vector.scalar_tensor_tensor(out=o_[:, u, :], in0=S.ps[:, 2 * u + 1, 0:P], scalar=i_, in1=subln[:, :],
                                                           op0=ALU.mult, op1=ALU.mult).then_inc(normed, 1)
            clear_block(nc, [ready, raw, turned, scored, maxed, exped, diffed, a_turned, a_copied, summed, squared,
                             scaled, rooted, normed, o_turned, chain])

        body(-1, attend=False)
        with nc.Fori(0, DA_H - 2) as h:
            body(h)
        body(DA_H - 2, prefetch=False)
        body(DA_H - 1, project=False)


def even_mixer(nc, g, S, sb, ctx):
    S.wall_full = ctx.enter_context(nc.semaphore("lora_weights_full"))
    S.xlora, S.wall, S.wst = sb("xlora", [P, 2, T]), sb("lora_w", [P, 5, W_NA]), sb("lora_w_pair", [P, 5, P])
    S.reset, S.hcol, S.prc = sb("scan_reset", [P, T]), sb("pair_columns", [P, 19]), sb("rkv", [P, 3, T])
    S.zero = sb("zero", [P, ZERO_W])
    S.item_x_cleared, S.item_y_cleared = [ctx.enter_context(nc.semaphore(m)) for m in ("item_tokens_cleared", "item_outputs_cleared")]
    R = rwkv_state(nc, S, sb)
    lora_block(nc, g, S, R)
    with nc.Block() as block:
        @block.sync
        def _(sp):
            sp.wait_ge(S.wall_full, 16 * 5)

        @block.gpsimd
        def _(pool):
            nc.gpsimd.memset(S.zero[:, :], 0.0)
    with nc.Fori(0, HP) as hp:
        with ExitStack() as st:
            sb2 = lambda n, s: st.enter_context(nc.sbuf_tensor(n, s, F32))
            A = Tiles()
            A.qT, A.kT, A.v = sb2("qT", [P, T]), sb2("kT", [P, T]), sb2("v", [P, NB, P])
            A.bias = sb2("na_bias", [P, 2, 2, T_LAT])
            A.bias_full = st.enter_context(nc.semaphore("na_bias_full"))
            project_block(nc, g, S, hp, A)
            na_block(nc, g, S, hp, A)
        rwkv_pair(nc, g, S, R, hp)
    with nc.Block() as block:
        @block.sync
        def _(sp):
            sp.wait_ge(S.slab_full, 16 * 6)
            sp.wait_ge(S.item_x_cleared, 16 * HP)
            sp.wait_ge(S.item_y_cleared, 16 * HP)





class Inputs:

    def __init__(self, x, c, ctx, c_ctx, ada_w, ada_b, ln_g, ln_b, even_w_in, even_w_out, shift_w, na_rpb,
                 rw_w0, rw_w_up, rw_a0, rw_a_up, rw_g_up, rw_k_k, rw_k_a, rw_r_k, rw_gn_g, rw_gn_b,
                 odd_w_in, odd_w_out, da_lq1, da_lk1, da_lq2, da_lk2, da_subln_g, router_w, router_b,
                 exp_w_gate, exp_w_up, exp_w_down, const, rope):
        self.x, self.c, self.ctx, self.c_ctx = x, c, ctx, c_ctx
        self.ada_w, self.ada_b, self.ln_g, self.ln_b = ada_w, ada_b, ln_g, ln_b
        self.even_w_in, self.even_w_out, self.shift_w, self.na_rpb = even_w_in, even_w_out, shift_w, na_rpb
        self.rw_w0, self.rw_w_up, self.rw_a0, self.rw_a_up, self.rw_g_up = rw_w0, rw_w_up, rw_a0, rw_a_up, rw_g_up
        self.rw_k_k, self.rw_k_a, self.rw_r_k, self.rw_gn_g, self.rw_gn_b = rw_k_k, rw_k_a, rw_r_k, rw_gn_g, rw_gn_b
        self.odd_w_in, self.odd_w_out, self.da_subln_g = odd_w_in, odd_w_out, da_subln_g
        self.da_lq1, self.da_lk1, self.da_lq2, self.da_lk2 = da_lq1, da_lk1, da_lq2, da_lk2
        self.router_w, self.router_b = router_w, router_b
        self.exp_w_gate, self.exp_w_up, self.exp_w_down = exp_w_gate, exp_w_up, exp_w_down
        self.const, self.rope = const, rope


def program(nc, g, outs):
    with ExitStack() as ctx:
        def sb(name, shape):
            return ctx.enter_context(nc.sbuf_tensor(name, shape, F32))
        S = Tiles()
        S.cst = sb("constants", [P, C_END])
        S.col = sb("vector_columns", [P, R_END])
        S.adab = sb("ada_b_columns", [P, 96])
        S.csil = sb("silu_c", [P, 16])
        S.mcol = sb("modulation_columns", [P, DEPTH, 2, 48])
        S.router = sb("router", [P, KD, N_EXP])
        S.rbias = sb("router_bias", [P, N_EXP])
        S.ps = ctx.enter_context(nc.psum_tensor("psum", [P, 8, 512], F32))
        S.uT = sb("uT", [P, KD, T])
        g.toep = nc.dram_tensor("na_bias_toeplitz", (2 * HP, GRID_W, 7, GRID_W), F32).ap()
        g.item_x = nc.dram_tensor("item_tokens", (ROWS, D), F32).ap()
        g.item_y = nc.dram_tensor("item_outputs", (ROWS, D), F32).ap()
        S.toep_written = ctx.enter_context(nc.semaphore("toeplitz_written"))
        toeplitz_copies(nc, g, S)
        stages(nc, g, S, outs)


_INS = ["x", "c", "ctx", "c_ctx", "ada_w", "ada_b", "ln_g", "ln_b", "even_w_in", "even_w_out", "shift_w", "na_rpb",
        "rw_w0", "rw_w_up", "rw_a0", "rw_a_up", "rw_g_up", "rw_k_k", "rw_k_a", "rw_r_k", "rw_gn_g", "rw_gn_b",
        "odd_w_in", "odd_w_out", "da_lq1", "da_lk1", "da_lq2", "da_lk2", "da_subln_g", "router_w", "router_b",
        "exp_w_gate", "exp_w_up", "exp_w_down"]


def kernel(**inputs):
    import numpy as np
    import concourse.bacc as bacc
    from concourse.bass_utils import run_bass_kernel_spmd as run

    nc = bacc.Bacc("TRN2", target_bir_lowering=False, num_devices=1)
    arrays = {"in_" + name: np.ascontiguousarray(inputs[name]) for name in _INS}
    arrays["in_const"], arrays["in_rope"] = shape_constants(np)
    aps = [nc.dram_tensor(name, a.shape, F32, kind="ExternalInput").ap() for name, a in arrays.items()]
    outs = [nc.dram_tensor(f"out_{i}", s, F32, kind="ExternalOutput").ap() for i, s in enumerate(OUTS)]
    program(nc, Inputs(*aps), outs)
    r = run(nc, [arrays], core_ids=[0])
    got = tuple(r.results[0][f"out_{i}"] for i in range(len(OUTS)))
    return got[0] if len(got) == 1 else got


OUTS = [(1, T_LAT, D)]


def stages(nc, g, S, outs):
    with ExitStack() as ctx:
        sb = lambda n, s: ctx.enter_context(nc.sbuf_tensor(n, s, F32))
        S.combine, S.place = sb("combine", [P, NB, N_EXP]), sb("place", [P, NB, N_EXP])
        S.two_gates = sb("two_gates", [P, 2, NB])
        S.two_rows = ctx.enter_context(nc.sbuf_tensor("two_rows", [P, 2, NB], mybir.dt.uint32))
        S.item_expert = ctx.enter_context(nc.sbuf_tensor("item_expert", [P, N_ITEM], mybir.dt.int32))
        S.pairs = ctx.enter_context(nc.sbuf_tensor("item_pairs", [P, 1], mybir.dt.int32))
        S.h = sb("h", [P, NB, D])
        S.tokens_in, S.lora_in = ctx.enter_context(nc.semaphore("tokens_in")), ctx.enter_context(nc.semaphore("lora_slab_in"))
        with nc.sbuf_tensor("oT0", [P, 2 * HP, T], F32) as S.oT:
            S.lora_slab = S.oT[:, 0:2 * HP // 2, :].rearrange("p h t -> p (h t)").rearrange("p (k n) -> p k n", k=KD)
            with ExitStack() as mx:
                setup_block(nc, g, S)
                ada_blocks(nc, g, S)
                S.wslab = mx.enter_context(nc.sbuf_tensor("pair_slabs", [P, 6, KD, P], F32))
                S.slab_full = ctx.enter_context(nc.semaphore("pair_slabs_full"))
                modulate_block(nc, g, S, 0, 0, first=True)
                even_mixer(nc, g, S, lambda n, s: mx.enter_context(nc.sbuf_tensor(n, s, F32)), ctx)
            post_block(nc, g, S, 0, 0, range(NB), project=g.even_w_out[0], load_h=True)
        experts(nc, g, S, 0, range(NB))
        latent = range(T_CTX // P, NB)
        modulate_block(nc, g, S, 1, 0)
        with nc.sbuf_tensor("oT1", [P, 2 * HP, T], F32) as S.oT:
            with nc.sbuf_tensor("odd_w_out", [P, 2, KD, 512], F32) as wout, nc.semaphore("odd_w_out_full0") as full0, \
                    nc.semaphore("odd_w_out_full1") as full1:
                odd_mixer(nc, g, S, 1, lambda sp: load_projection(sp, wout, g.odd_w_out[0], [full0, full1]))
                post_block(nc, g, S, 1, 0, latent, project=g.odd_w_out[0], ahead=(wout, [full0, full1]))
        experts(nc, g, S, 1, latent)
        written = ctx.enter_context(nc.semaphore("output_written"))
        with nc.Block() as block:
            @block.sync
            def _(sp):
                sp.dma_start(outs[0][0].rearrange("(b p) d -> p b d", p=P), S.h[:, T_CTX // P:NB, :]).then_inc(written, 16)
                sp.wait_ge(written, 16)


def experts(nc, g, S, l, blocks):
    modulate_block(nc, g, S, l, 3, blocks=blocks)
    moe(nc, g, S, l, blocks)
    with nc.sbuf_tensor(f"acc{l}", [P, NB, D], F32) as S.acc:
        combine_block(nc, g, S, l, blocks)
        post_block(nc, g, S, l, 1, blocks)
```
